# Optimizing a Trainium2 kernel written in Bass

```python
import math
import jax
import jax.numpy as jnp
from jax import lax
import numpy as np

D_MODEL = 1024
BATCH = 1
SEQ = 512
DEPTH = 2
DEC_BATCH = 8
DEC_SEQ = 4
PAST_LEN = 1024
PAGE_SIZE = 128

N_EVEN = (DEPTH + 1) // 2
N_ODD = DEPTH // 2
FFN_HIDDEN = 2816
MIX_HALF = D_MODEL // 2
GLA_HEADS = 4
GLA_DK = 64
GLA_DV = MIX_HALF // GLA_HEADS
GLA_RANK = 16
GLA_TAU = 16.0
RET_HEADS = 4
RET_DK = 64
RET_DV = MIX_HALF // RET_HEADS
RET_THETA = 10000.0
LA_CHUNK = 64
S5_WIDTH = MIX_HALF
S5_GROUP = 16
S5_GROUPS = S5_WIDTH // S5_GROUP
S5_STATE = 64
S5_STEP_MIN = 0.001
S5_STEP_MAX = 0.1
SWA_HD = 64
SWA_HEADS = MIX_HALF // SWA_HD
SWA_KV_HEADS = 2
SWA_WINDOW = 128
ROPE_THETA = 500000.0
N_MEM = 256
MEM_HEADS = 4
MEM_HD = D_MODEL // MEM_HEADS
NORM_EPS = 1e-6
EVEN_SIZES = (GLA_HEADS * GLA_DK, GLA_HEADS * GLA_DK, GLA_HEADS * GLA_DV, GLA_HEADS * GLA_DV, GLA_RANK,
              RET_HEADS * RET_DK, RET_HEADS * RET_DK, RET_HEADS * RET_DV, RET_HEADS * RET_DV)
ODD_SIZES = (S5_WIDTH, SWA_HEADS * SWA_HD, SWA_KV_HEADS * SWA_HD, SWA_KV_HEADS * SWA_HD)
EVEN_IN = sum(EVEN_SIZES)
ODD_IN = sum(ODD_SIZES)

kernel_name = 'hybrid_gla_retnet_s5_swa_macaron_step'

def rms_norm(x, gain=None):
    xf = x.astype(jnp.float32)
    y = xf * lax.rsqrt(jnp.mean(xf * xf, axis=-1, keepdims=True) + NORM_EPS)
    if gain is not None:
        y = y * gain.astype(jnp.float32)
    return y.astype(x.dtype)

def split_cols(t, sizes):
    return jnp.split(t, np.cumsum(sizes)[:-1].tolist(), axis=-1)

def swiglu(h, w_gate, w_up, w_down):
    return (jax.nn.silu(h @ w_gate) * (h @ w_up)) @ w_down

def partial_rotary(x, pos):
    rd = x.shape[-1] // 4
    half = rd // 2
    inv = 1.0 / (ROPE_THETA ** (jnp.arange(half, dtype=jnp.float32) * 2.0 / rd))
    ang = pos[:, None] * inv[None, :]
    cos, sin = jnp.cos(ang)[:, None, :], jnp.sin(ang)[:, None, :]
    xf = x.astype(jnp.float32)
    x1, x2, rest = xf[..., :half], xf[..., half:rd], xf[..., rd:]
    return jnp.concatenate([x1 * cos - x2 * sin, x2 * cos + x1 * sin, rest], axis=-1).astype(x.dtype)

def retention_rotate(x, pos):
    dk = x.shape[-1]
    inv = 1.0 / (RET_THETA ** jnp.linspace(0.0, 1.0, dk // 2, dtype=jnp.float32))
    ang = pos[:, None] * inv[None, :]
    cos, sin = jnp.cos(ang)[:, None, :], jnp.sin(ang)[:, None, :]
    xf = x.astype(jnp.float32)
    xe, xo = xf[..., 0::2], xf[..., 1::2]
    return jnp.stack([xe * cos - xo * sin, xo * cos + xe * sin], axis=-1).reshape(x.shape).astype(x.dtype)

def chunked_gated_linear_attention(q, k, v, log_a, s0):
    f32 = jnp.float32
    bsz, seq, n_heads, _ = q.shape
    dv = v.shape[-1]
    chunk = math.gcd(seq, LA_CHUNK)
    n_chunks = seq // chunk

    def blocks(t):
        return t.astype(f32).reshape(bsz, n_chunks, chunk, n_heads, t.shape[-1]).transpose(1, 0, 3, 2, 4)

    q, k, v, log_a = blocks(q), blocks(k), blocks(v), blocks(log_a)
    cum = jnp.cumsum(log_a, axis=3)
    cum_last = cum[:, :, :, -1:, :]
    q_dec = q * jnp.exp(cum)
    k_inv = k * jnp.exp(-cum)
    k_dec = k * jnp.exp(cum_last - cum)
    causal = jnp.tril(jnp.ones((chunk, chunk), dtype=bool))
    scores = jnp.where(causal, jnp.einsum('nbhtd,nbhsd->nbhts', q_dec, k_inv), 0.0)
    o_intra = jnp.einsum('nbhts,nbhsv->nbhtv', scores, v)

    def step(state, inp):
        q_c, k_c, v_c, last_c = inp
        o_c = jnp.einsum('bhtd,bhdv->bhtv', q_c, state)
        state = state * jnp.exp(last_c[:, :, 0, :, None]) + jnp.einsum('bhtd,bhtv->bhdv', k_c, v_c)
        return state, o_c

    s_final, o_inter = lax.scan(step, s0.astype(f32), (q_dec, k_dec, v, cum_last))
    out = (o_intra + o_inter).transpose(1, 0, 3, 2, 4).reshape(bsz, seq, n_heads, dv)
    return out, s_final

def gla_retention_mixer(h, pos, gla_s0, ret_s0, w, i):
    f32 = jnp.float32
    bsz, seq, _ = h.shape
    gq, gk, gv, gg, ga, rq, rk, rv, rg = split_cols(h @ w['even_w_in'][i], EVEN_SIZES)

    def heads(t, n):
        return t.reshape(bsz, seq, n, -1)

    log_a = jax.nn.log_sigmoid((ga @ w['gla_w_gate'][i] + w['gla_b_gate'][i]).astype(f32)) / GLA_TAU
    o_g, s_g = chunked_gated_linear_attention(heads(gq, GLA_HEADS) * GLA_DK ** -0.5, heads(gk, GLA_HEADS),
                                              heads(gv, GLA_HEADS), heads(log_a, GLA_HEADS), gla_s0)
    o_g = rms_norm(o_g, w['gla_out_norm'][i]) * jax.nn.silu(heads(gg, GLA_HEADS).astype(f32))
    log_decay = jnp.log(1.0 - 2.0 ** (-5.0 - jnp.arange(RET_HEADS, dtype=f32)))
    q_r = retention_rotate(heads(rq, RET_HEADS), pos)
    k_r = retention_rotate(heads(rk, RET_HEADS), pos) * RET_DK ** -0.5
    log_g = jnp.broadcast_to(log_decay[:, None], (bsz, seq, RET_HEADS, RET_DK))
    o_r, s_r = chunked_gated_linear_attention(q_r, k_r, heads(rv, RET_HEADS), log_g, ret_s0)
    o_r = rms_norm(o_r) * jax.nn.silu(heads(rg, RET_HEADS).astype(f32))
    mixed = jnp.concatenate([o_g.reshape(bsz, seq, -1), o_r.reshape(bsz, seq, -1)], axis=-1)
    return mixed.astype(h.dtype) @ w['even_w_out'][i], s_g, s_r

def complex_affine_combine(e1, e2):
    a1r, a1i, b1r, b1i = e1
    a2r, a2i, b2r, b2i = e2
    return (a2r * a1r - a2i * a1i, a2r * a1i + a2i * a1r,
            a2r * b1r - a2i * b1i + b2r, a2r * b1i + a2i * b1r + b2i)

def s5_scan(u, s_re0, s_im0, w, i):
    f32 = jnp.float32
    bsz, seq, _ = u.shape
    a_re, a_im = w['s5_a_re'][i].astype(f32), w['s5_a_im'][i].astype(f32)
    step = jnp.exp(w['s5_log_step'][i].astype(f32))[:, None]
    mag = jnp.exp(a_re * step)
    ab_re, ab_im = mag * jnp.cos(a_im * step), mag * jnp.sin(a_im * step)
    den = a_re * a_re + a_im * a_im
    coef_re = ((ab_re - 1.0) * a_re + ab_im * a_im) / den
    coef_im = (ab_im * a_re - (ab_re - 1.0) * a_im) / den
    b_re, b_im = w['s5_b_re'][i].astype(f32), w['s5_b_im'][i].astype(f32)
    bb_re = coef_re[..., None] * b_re - coef_im[..., None] * b_im
    bb_im = coef_re[..., None] * b_im + coef_im[..., None] * b_re
    uf = u.astype(f32).reshape(bsz, seq, S5_GROUPS, S5_GROUP)
    bu_re = jnp.einsum('blgi,gni->blgn', uf, bb_re)
    bu_im = jnp.einsum('blgi,gni->blgn', uf, bb_im)
    x_re0, x_im0 = s_re0.astype(f32), s_im0.astype(f32)
    bu_re = bu_re.at[:, 0].add(ab_re * x_re0 - ab_im * x_im0)
    bu_im = bu_im.at[:, 0].add(ab_re * x_im0 + ab_im * x_re0)
    a_re_t = jnp.broadcast_to(ab_re, bu_re.shape)
    a_im_t = jnp.broadcast_to(ab_im, bu_im.shape)
    _, _, h_re, h_im = lax.associative_scan(complex_affine_combine, (a_re_t, a_im_t, bu_re, bu_im), axis=1)
    y = (jnp.einsum('blgn,gin->blgi', h_re, w['s5_c_re'][i].astype(f32))
         - jnp.einsum('blgn,gin->blgi', h_im, w['s5_c_im'][i].astype(f32)))
    y = y.reshape(bsz, seq, S5_WIDTH) + w['s5_d'][i].astype(f32) * uf.reshape(bsz, seq, S5_WIDTH)
    z = jax.nn.gelu(y)
    out = z * jax.nn.sigmoid(z @ w['s5_w_glu'][i].astype(f32) + w['s5_b_glu'][i].astype(f32))
    return out, h_re[:, -1], h_im[:, -1]

def sliding_window_sink_attention(q, k, v, prev_k, prev_v, sinks, pos0):
    f32 = jnp.float32
    bsz, seq, n_q, hd = q.shape
    n_kv = k.shape[2]
    grp = n_q // n_kv
    past = prev_k.shape[1]
    win = SWA_WINDOW
    pad = jnp.zeros((bsz, win - past, n_kv, hd), k.dtype)
    k_ext = jnp.concatenate([pad, prev_k.astype(k.dtype), k], axis=1)
    v_ext = jnp.concatenate([pad, prev_v.astype(v.dtype), v], axis=1)
    qb = math.gcd(seq, win)
    nb = seq // qb
    idx = np.arange(nb)[:, None] * qb + np.arange(qb + win)[None, :]
    kb = jnp.take(k_ext, idx, axis=1)
    vb = jnp.take(v_ext, idx, axis=1)
    qr = q.reshape(bsz, nb, qb, n_kv, grp, hd)
    s = jnp.einsum('bnqkgd,bnskd->bnkgqs', qr, kb).astype(f32) * hd ** -0.5
    q_pos = pos0 + np.arange(seq).reshape(nb, qb)
    k_pos = pos0 - win + idx
    kp, qp = k_pos[:, None, :], q_pos[:, :, None]
    mask = (kp <= qp) & (kp > qp - win) & (kp >= pos0 - past)
    s = jnp.where(mask[None, :, None, None], s, -jnp.inf)
    sink = sinks.astype(f32).reshape(n_kv, grp)[None, None, :, :, None, None]
    m = jnp.maximum(jnp.max(s, axis=-1, keepdims=True), sink)
    e = jnp.exp(s - m)
    p = e / (jnp.sum(e, axis=-1, keepdims=True) + jnp.exp(sink - m))
    o = jnp.einsum('bnkgqs,bnskd->bnqkgd', p.astype(v.dtype), vb).reshape(bsz, seq, n_q * hd)
    keep = min(win, past + seq)
    return o, k_ext[:, -keep:], v_ext[:, -keep:]

def s5_swa_mixer(h, pos, pos0, s_re0, s_im0, prev_k, prev_v, w, i):
    bsz, seq, _ = h.shape
    u, q, k, v = split_cols(h @ w['odd_w_in'][i], ODD_SIZES)
    c_out, s_re, s_im = s5_scan(u, s_re0, s_im0, w, i)
    q = partial_rotary(rms_norm(q.reshape(bsz, seq, SWA_HEADS, SWA_HD), w['swa_q_norm'][i]), pos)
    k = partial_rotary(rms_norm(k.reshape(bsz, seq, SWA_KV_HEADS, SWA_HD), w['swa_k_norm'][i]), pos)
    v = v.reshape(bsz, seq, SWA_KV_HEADS, SWA_HD)
    d_out, buf_k, buf_v = sliding_window_sink_attention(q, k, v, prev_k, prev_v, w['swa_sinks'][i], pos0)
    mixed = jnp.concatenate([c_out.astype(h.dtype), d_out.astype(h.dtype)], axis=-1)
    return mixed @ w['odd_w_out'][i], s_re, s_im, buf_k, buf_v

def memory_kv(mem, w, layer):
    bsz, n_mem, _ = mem.shape
    mn = rms_norm(mem, w['mem_m_norm'][layer])
    k = rms_norm((mn @ w['mem_w_k'][layer]).reshape(bsz, n_mem, MEM_HEADS, MEM_HD), w['mem_k_norm'][layer])
    v = (mn @ w['mem_w_v'][layer]).reshape(bsz, n_mem, MEM_HEADS, MEM_HD)
    return k, v

def memory_attend(h, mem_k, mem_v, w, layer):
    bsz, seq, _ = h.shape
    q = rms_norm((h @ w['mem_w_q'][layer]).reshape(bsz, seq, MEM_HEADS, MEM_HD), w['mem_q_norm'][layer])
    s = jnp.einsum('blhd,bmhd->bhlm', q, mem_k.astype(q.dtype)).astype(jnp.float32) * MEM_HD ** -0.5
    p = jax.nn.softmax(s, axis=-1).astype(mem_v.dtype)
    o = jnp.einsum('bhlm,bmhd->blhd', p, mem_v).reshape(bsz, seq, D_MODEL)
    return o.astype(h.dtype) @ w['mem_w_o'][layer]

def run_trunk(x, pos0, gla_s, ret_s, s5_re, s5_im, swa_k, swa_v, mem_k, mem_v, w):
    pos = pos0 + jnp.arange(x.shape[1], dtype=jnp.float32)
    new_gla, new_ret, new_s5_re, new_s5_im, new_swa_k, new_swa_v = [], [], [], [], [], []
    for layer in range(DEPTH):
        x = x + 0.5 * swiglu(rms_norm(x, w['ffn1_norm'][layer]), w['ffn1_w_gate'][layer],
                             w['ffn1_w_up'][layer], w['ffn1_w_down'][layer])
        h = rms_norm(x, w['mix_norm'][layer])
        i = layer // 2
        if layer % 2 == 0:
            mix, g_s, r_s = gla_retention_mixer(h, pos, gla_s[i], ret_s[i], w, i)
            new_gla.append(g_s)
            new_ret.append(r_s)
        else:
            mix, sr, si, kb, vb = s5_swa_mixer(h, pos, pos0, s5_re[i], s5_im[i], swa_k[i], swa_v[i], w, i)
            new_s5_re.append(sr)
            new_s5_im.append(si)
            new_swa_k.append(kb)
            new_swa_v.append(vb)
        x = x + mix
        x = x + memory_attend(rms_norm(x, w['mem_x_norm'][layer]), mem_k[layer], mem_v[layer], w, layer)
        x = x + 0.5 * swiglu(rms_norm(x, w['ffn2_norm'][layer]), w['ffn2_w_gate'][layer],
                             w['ffn2_w_up'][layer], w['ffn2_w_down'][layer])
    return (x, jnp.stack(new_gla), jnp.stack(new_ret), jnp.stack(new_s5_re), jnp.stack(new_s5_im),
            jnp.stack(new_swa_k), jnp.stack(new_swa_v))

def setup_inputs(seed: int = 0) -> dict:
    key = jax.random.key(seed)
    keys = iter(jax.random.split(key, 64))
    f32 = jnp.float32

    def normal(shape, scale=1.0):
        return scale * jax.random.normal(next(keys), shape, f32)

    def gain(shape):
        return 1.0 + 0.05 * jax.random.normal(next(keys), shape, f32)

    win = min(SWA_WINDOW, PAST_LEN)
    log_lo, log_hi = math.log(S5_STEP_MIN), math.log(S5_STEP_MAX)
    n_idx = jnp.arange(S5_STATE, dtype=f32)
    mix_w = 2 * MIX_HALF
    return {
        'x_prompt': normal((BATCH, SEQ, D_MODEL)),
        'x_sample': normal((DEC_BATCH, DEC_SEQ, D_MODEL)),
        'mem_prompt': normal((BATCH, N_MEM, D_MODEL)),
        'state_gla': normal((N_EVEN, DEC_BATCH, GLA_HEADS, GLA_DK, GLA_DV), 0.5),
        'state_ret': normal((N_EVEN, DEC_BATCH, RET_HEADS, RET_DK, RET_DV), 0.5),
        'state_s5_re': normal((N_ODD, DEC_BATCH, S5_GROUPS, S5_STATE), 0.1),
        'state_s5_im': normal((N_ODD, DEC_BATCH, S5_GROUPS, S5_STATE), 0.1),
        'cache_swa_k': normal((N_ODD, DEC_BATCH, win, SWA_KV_HEADS, SWA_HD)),
        'cache_swa_v': normal((N_ODD, DEC_BATCH, win, SWA_KV_HEADS, SWA_HD)),
        'cache_mem_k': normal((DEPTH, DEC_BATCH, N_MEM, MEM_HEADS, MEM_HD)),
        'cache_mem_v': normal((DEPTH, DEC_BATCH, N_MEM, MEM_HEADS, MEM_HD)),
        'ffn1_norm': gain((DEPTH, D_MODEL)),
        'ffn1_w_gate': normal((DEPTH, D_MODEL, FFN_HIDDEN), D_MODEL ** -0.5),
        'ffn1_w_up': normal((DEPTH, D_MODEL, FFN_HIDDEN), D_MODEL ** -0.5),
        'ffn1_w_down': normal((DEPTH, FFN_HIDDEN, D_MODEL), FFN_HIDDEN ** -0.5),
        'ffn2_norm': gain((DEPTH, D_MODEL)),
        'ffn2_w_gate': normal((DEPTH, D_MODEL, FFN_HIDDEN), D_MODEL ** -0.5),
        'ffn2_w_up': normal((DEPTH, D_MODEL, FFN_HIDDEN), D_MODEL ** -0.5),
        'ffn2_w_down': normal((DEPTH, FFN_HIDDEN, D_MODEL), FFN_HIDDEN ** -0.5),
        'mix_norm': gain((DEPTH, D_MODEL)),
        'even_w_in': normal((N_EVEN, D_MODEL, EVEN_IN), D_MODEL ** -0.5),
        'gla_w_gate': normal((N_EVEN, GLA_RANK, GLA_HEADS * GLA_DK), GLA_RANK ** -0.5),
        'gla_b_gate': normal((N_EVEN, GLA_HEADS * GLA_DK), 0.01),
        'gla_out_norm': gain((N_EVEN, GLA_DV)),
        'even_w_out': normal((N_EVEN, mix_w, D_MODEL), mix_w ** -0.5),
        'odd_w_in': normal((N_ODD, D_MODEL, ODD_IN), D_MODEL ** -0.5),
        's5_a_re': -0.5 + normal((N_ODD, S5_GROUPS, S5_STATE), 0.01),
        's5_a_im': math.pi * n_idx + normal((N_ODD, S5_GROUPS, S5_STATE), 0.01),
        's5_log_step': log_lo + (log_hi - log_lo) * jax.random.uniform(next(keys), (N_ODD, S5_GROUPS), f32),
        's5_b_re': normal((N_ODD, S5_GROUPS, S5_STATE, S5_GROUP), (2.0 * S5_GROUP) ** -0.5),
        's5_b_im': normal((N_ODD, S5_GROUPS, S5_STATE, S5_GROUP), (2.0 * S5_GROUP) ** -0.5),
        's5_c_re': normal((N_ODD, S5_GROUPS, S5_GROUP, S5_STATE), (2.0 * S5_STATE) ** -0.5),
        's5_c_im': normal((N_ODD, S5_GROUPS, S5_GROUP, S5_STATE), (2.0 * S5_STATE) ** -0.5),
        's5_d': normal((N_ODD, S5_WIDTH)),
        's5_w_glu': normal((N_ODD, S5_WIDTH, S5_WIDTH), S5_WIDTH ** -0.5),
        's5_b_glu': normal((N_ODD, S5_WIDTH), 0.01),
        'swa_q_norm': gain((N_ODD, SWA_HD)),
        'swa_k_norm': gain((N_ODD, SWA_HD)),
        'swa_sinks': normal((N_ODD, SWA_HEADS), 0.5),
        'odd_w_out': normal((N_ODD, mix_w, D_MODEL), mix_w ** -0.5),
        'mem_x_norm': gain((DEPTH, D_MODEL)),
        'mem_m_norm': gain((DEPTH, D_MODEL)),
        'mem_w_q': normal((DEPTH, D_MODEL, D_MODEL), D_MODEL ** -0.5),
        'mem_w_k': normal((DEPTH, D_MODEL, D_MODEL), D_MODEL ** -0.5),
        'mem_w_v': normal((DEPTH, D_MODEL, D_MODEL), D_MODEL ** -0.5),
        'mem_w_o': normal((DEPTH, D_MODEL, D_MODEL), D_MODEL ** -0.5),
        'mem_q_norm': gain((DEPTH, MEM_HD)),
        'mem_k_norm': gain((DEPTH, MEM_HD)),
    }

def reference(x_prompt, x_sample, mem_prompt, state_gla, state_ret, state_s5_re, state_s5_im,
              cache_swa_k, cache_swa_v, cache_mem_k, cache_mem_v,
              ffn1_norm, ffn1_w_gate, ffn1_w_up, ffn1_w_down, ffn2_norm, ffn2_w_gate, ffn2_w_up, ffn2_w_down,
              mix_norm, even_w_in, gla_w_gate, gla_b_gate, gla_out_norm, even_w_out,
              odd_w_in, s5_a_re, s5_a_im, s5_log_step, s5_b_re, s5_b_im, s5_c_re, s5_c_im, s5_d, s5_w_glu,
              s5_b_glu, swa_q_norm, swa_k_norm, swa_sinks, odd_w_out,
              mem_x_norm, mem_m_norm, mem_w_q, mem_w_k, mem_w_v, mem_w_o, mem_q_norm, mem_k_norm):
    w = dict(ffn1_norm=ffn1_norm, ffn1_w_gate=ffn1_w_gate, ffn1_w_up=ffn1_w_up, ffn1_w_down=ffn1_w_down,
             ffn2_norm=ffn2_norm, ffn2_w_gate=ffn2_w_gate, ffn2_w_up=ffn2_w_up, ffn2_w_down=ffn2_w_down,
             mix_norm=mix_norm, even_w_in=even_w_in, gla_w_gate=gla_w_gate, gla_b_gate=gla_b_gate,
             gla_out_norm=gla_out_norm, even_w_out=even_w_out, odd_w_in=odd_w_in,
             s5_a_re=s5_a_re, s5_a_im=s5_a_im, s5_log_step=s5_log_step, s5_b_re=s5_b_re, s5_b_im=s5_b_im,
             s5_c_re=s5_c_re, s5_c_im=s5_c_im, s5_d=s5_d, s5_w_glu=s5_w_glu, s5_b_glu=s5_b_glu,
             swa_q_norm=swa_q_norm, swa_k_norm=swa_k_norm, swa_sinks=swa_sinks, odd_w_out=odd_w_out,
             mem_x_norm=mem_x_norm, mem_m_norm=mem_m_norm, mem_w_q=mem_w_q, mem_w_k=mem_w_k,
             mem_w_v=mem_w_v, mem_w_o=mem_w_o, mem_q_norm=mem_q_norm, mem_k_norm=mem_k_norm)
    dt = x_prompt.dtype
    mem_kv = [memory_kv(mem_prompt, w, layer) for layer in range(DEPTH)]
    p_mem_k = jnp.stack([kv[0] for kv in mem_kv])
    p_mem_v = jnp.stack([kv[1] for kv in mem_kv])
    z_gla = jnp.zeros((N_EVEN, BATCH, GLA_HEADS, GLA_DK, GLA_DV), dt)
    z_ret = jnp.zeros((N_EVEN, BATCH, RET_HEADS, RET_DK, RET_DV), dt)
    z_s5 = jnp.zeros((N_ODD, BATCH, S5_GROUPS, S5_STATE), dt)
    z_buf = jnp.zeros((N_ODD, BATCH, 0, SWA_KV_HEADS, SWA_HD), dt)
    y_prompt, p_gla, p_ret, p_s5_re, p_s5_im, p_swa_k, p_swa_v = run_trunk(
        x_prompt, 0, z_gla, z_ret, z_s5, z_s5, z_buf, z_buf, p_mem_k, p_mem_v, w)
    y_sample, s_gla, s_ret, s_s5_re, s_s5_im, s_swa_k, s_swa_v = run_trunk(
        x_sample, PAST_LEN, state_gla, state_ret, state_s5_re, state_s5_im, cache_swa_k, cache_swa_v,
        cache_mem_k, cache_mem_v, w)
    return (y_prompt, y_sample, p_gla, p_ret, p_s5_re, p_s5_im, p_swa_k, p_swa_v, p_mem_k, p_mem_v,
            s_gla, s_ret, s_s5_re, s_s5_im, s_swa_k, s_swa_v)


_drawn_inputs = setup_inputs


def setup_inputs(seed=0):
    import zlib

    import numpy as np

    out = dict(_drawn_inputs(seed))
    spreads = {}
    factors = {'gla_b_gate': 8.0,
     'gla_out_norm': 2.693,
     's5_a_re': 16.434,
     's5_c_re': 4.315,
     's5_c_im': 4.363,
     's5_b_glu': 64.0,
     'swa_q_norm': 8.0,
     'swa_sinks': 49.907,
     'mem_x_norm': 8.0,
     'mem_q_norm': 8.0}
    for name, (base, spread) in spreads.items():
        noise = np.random.default_rng([zlib.crc32(name.encode()), seed]).standard_normal(out[name].shape)
        drawn = base * np.exp(spread * noise) if base else spread * noise
        out[name] = jnp.asarray(drawn.astype(out[name].dtype))
    for name, factor in factors.items():
        out[name] = (out[name] * factor).astype(out[name].dtype)
    return out
```

```python
from contextlib import ExitStack

import concourse.bass as bass
from concourse import mybir

F32 = mybir.dt.float32
F32R = mybir.dt.float32r
I32 = mybir.dt.int32
ACT = mybir.ActivationFunctionType
ALU = mybir.AluOpType
AX_X = mybir.AxisListType.X

P = 128
D_MODEL = 1024
KT = D_MODEL // P
SEQ, DEC_BATCH, DEC_SEQ = 512, 8, 4
TS = DEC_BATCH * DEC_SEQ
TOK = SEQ + TS
PAST_LEN = 1024
FFN_HIDDEN = 2816
HT = FFN_HIDDEN // P // 2
N_MEM, MEM_HEADS, MEM_HD = 256, 4, 256
EPS = 1e-6
CHUNK = 64
S5_TILES = 16
WIN = 128
NEG = -1e30
TWO_PI = 6.283185307179586
MAGIC = 12582912.0
MAGIC13 = 1536.0
PI_SAFE = 3.1415925

GQ, GK, GV, GG, RQ, RK, RV, RG, GA = 0, 2, 4, 8, 12, 14, 16, 20, 24
EVEN_TILES = 26
SU, SQ, SK, SV = 0, 4, 8, 9
ODD_TILES = 10

IDENT, ONES, ONES64, SWAP2, SWAP8 = range(5)
VEC = {}
_at = 0
for _name, _n in (("ffn1_norm", 16), ("ffn2_norm", 16), ("mix_norm", 16), ("mem_x_norm", 16), ("mem_m_norm", 16),
                  ("mem_q_norm", 4), ("mem_k_norm", 4), ("gla_out_norm", 1), ("one", 1), ("gla_b_gate", 2),
                  ("swa_q_norm", 1), ("swa_k_norm", 1), ("s5_d", 4), ("s5_b_glu", 4), ("sinks", 8),
                  ("sink_rows", 2), ("s5_a_re", 16), ("s5_a_im", 16), ("s5_log_step", 16), ("ret_last", 32)):
    VEC[_name] = _at
    _at += _n
NVEC = _at


class Core:

    def sem(self, name):
        self.section_sems.append(self.nc.alloc_semaphore(name))
        return self.section_sems[-1]

    def end_section(self):
        self.nc.clear_and_free_semaphores(self.section_sems)
        self.section_sems = []
        self.nc.all_engine_barrier(sem_only=True)


def halves(n):
    return (2, n // 2) if n > 512 else (1, n)


def in_groups(ap, n):
    g, w = halves(n)
    return ap.rearrange("p (a c) -> p a c", c=w)


def first_chunks(core, sp, weights, kt):
    for s in range(2):
        sp.dma_start(core.raw[s][:, 0:kt * P], weights[s][0]).then_inc(core.landed[s], 16)


def high_part(nc, core, s, kt):
    return nc.scalar.activation(core.high[s][:, 0:kt * P], core.raw[s][:, 0:kt * P], ACT.Copy)


def low_part(nc, core, s, kt):
    return nc.vector.tensor_tensor(core.low[s][:, 0:kt * P], core.raw[s][:, 0:kt * P],
                                   core.high[s][:, 0:kt * P].bitcast(F32), ALU.subtract)


def projection(nc, core, name, weights, pairs, kt, src, cols, finish, dst, scale=1.0, after=None, norm=None, scaled=False):
    groups, width = halves(cols)
    base = list(core.loads)
    core.loads = [b + 16 * pairs for b in base]
    last_pair = pairs - 1

    def sem(what):
        return core.sem(f"{name}_{what}")

    with ExitStack() as ctx:
        def sb(what, shape, dt=F32):
            return ctx.enter_context(nc.sbuf_tensor(f"{name}_{what}", shape, dt))

        high_ready = sem("high_ready")
        low_ready = sem("low_ready")
        tile_done = sem("tile_done")
        psum_free = [sem("psum_free0"), sem("psum_free1")]
        rstd = core.rstd[:, 0:cols]
        if finish == "gate":
            gate_scaled = sem("gate_scaled")
            up_scaled = sem("up_scaled")
            gate_ready = sem("gate_ready")
            product_ready = sem("product_ready")
            hid_high = sem("hid_high")
            hid_ready = sem("hid_ready")
            sg, up, prod = sb("sg", [P, cols]), sb("up", [P, cols]), sb("prod", [P, cols])
        if norm:
            x_tiles, gain = norm
            x_high, x_ready = sem("x_high"), sem("x_ready")
            sq_act, sq_pool = sem("sq_act"), sem("sq_pool")
            added = sem("added")
            summed, log_ready, rstd_ready = sem("summed"), sem("log_ready"), sem("rstd_ready")
            sq = [sb("sq0", [P, 2, cols]), sb("sq1", [P, 2, cols])]
            total = sb("total", [P, cols])
            half_k = kt // 2
        acc = [core.ps[:, 2 * s:2 * s + groups, 0:width] for s in range(2)]
        sums = core.ps[:, 4:4 + groups, 0:width]

        with nc.Block(name) as block:
            @block.sync
            def _(sp):
                def load(s, source, size):
                    sp.dma_start(core.raw[s][:, 0:size * P], source).then_inc(core.landed[s], 16)

                load(0, weights[0][1], kt)
                if pairs > 2:
                    with sp.Fori(0, pairs - 2) as i:
                        sp.wait_ge(low_ready, i * 2 + 1)
                        load(1, weights[1][i + 1], kt)
                        sp.wait_ge(low_ready, i * 2 + 2)
                        load(0, weights[0][i + 2], kt)
                sp.wait_ge(low_ready, 2 * last_pair - 1)
                load(1, weights[1][last_pair], kt)
                if after is not None:
                    for s in range(2):
                        sp.wait_ge(low_ready, 2 * last_pair + s)
                        load(s, after[0][s][0], after[1])

            @block.gpsimd
            def _(pool):
                if norm:
                    for k in range(4):
                        if k >= 2:
                            pool.wait_ge(added, 2 * k - 3)
                        x = x_tiles[4 + k]
                        nc.gpsimd.tensor_tensor(sq[1][:, k % 2], x, x, ALU.mult).then_inc(sq_pool, 1)

            @block.scalar
            def _(act):
                def split_high(s, landed_at, done_at, size=kt):
                    act.wait_ge(core.landed[s], landed_at)
                    if done_at is not None:
                        act.wait_ge(tile_done, done_at)
                    high_part(nc, core, s, size).then_inc(high_ready, 1)

                def gate(i):
                    act.wait_ge(gate_scaled, i + 1)
                    nc.scalar.activation(sg[:], sg[:], ACT.Silu).then_inc(gate_ready, 1)

                if norm:
                    for k in range(kt):
                        nc.scalar.activation(src[0][:, k], x_tiles[k], ACT.Copy, scale=core.vec(gain + k)).then_inc(x_high, 1)
                        if k == 3:
                            split_high(1, base[1] + 16, None)
                    for k in range(4):
                        if k >= 2:
                            act.wait_ge(added, 2 * k - 3)
                        nc.scalar.activation(sq[0][:, k % 2], x_tiles[k], ACT.Square).then_inc(sq_act, 1)
                    act.wait_ge(summed, 1)
                    nc.scalar.activation(in_groups(rstd, cols), sums, ACT.Ln, bias=core.eps[:], scale=1.0 / D_MODEL
                                         ).then_inc(log_ready, 1)
                    act.wait_ge(log_ready, 1)
                    nc.scalar.activation(rstd, rstd, ACT.Exp, scale=-0.5).then_inc(rstd_ready, 1)
                else:
                    split_high(1, base[1] + 16, None)
                with act.Fori(0, last_pair) as i:
                    split_high(0, i * 16 + (base[0] + 16), i * 2 + 1)
                    if finish == "gate":
                        gate(i)
                    split_high(1, i * 16 + (base[1] + 32), i * 2 + 2)
                if after is not None:
                    split_high(0, base[0] + 16 * pairs, 2 * last_pair + 1, after[1])
                if finish == "gate":
                    gate(last_pair)

            @block.vector
            def _(dve):
                def split_low(s, high_at, size=kt):
                    dve.wait_ge(high_ready, high_at)
                    low_part(nc, core, s, size).then_inc(low_ready, 1)

                def finish_tile(s, i):
                    dve.wait_ge(tile_done, i * 2 + (s + 1))
                    if finish == "gate":
                        to = (sg, up)[s]
                        nc.vector.tensor_tensor(in_groups(to[:], cols), acc[s], in_groups(rstd, cols), ALU.mult
                                                ).then_inc((gate_scaled, up_scaled)[s], 1)
                        if s == 0:
                            return
                        dve.wait_ge(up_scaled, i + 1)
                        dve.wait_ge(gate_ready, i + 1)
                        nc.vector.tensor_tensor(prod[:], sg[:], up[:], ALU.mult).then_inc(product_ready, 1)
                        dve.wait_ge(product_ready, i + 1)
                        high = dst[0][:, bass.ds(i, 1), :].rearrange("p o c -> p (o c)")
                        low = dst[1][:, bass.ds(i, 1), :].rearrange("p o c -> p (o c)")
                        nc.vector.tensor_scalar(high, prod[:], 1.0, None, ALU.mult).then_inc(hid_high, 1)
                        dve.wait_ge(hid_high, i + 1)
                        nc.vector.tensor_tensor(low, prod[:], high.bitcast(F32), ALU.subtract).then_inc(hid_ready, 1)
                        return
                    out = dst[:, bass.ds(i * 2 + s, 1), :].rearrange("p o (a c) -> p (o a) c", c=width)
                    if finish == "add":
                        ins = nc.vector.scalar_tensor_tensor(out, acc[s], scale, out, ALU.mult, ALU.add)
                    elif scaled:
                        ins = nc.vector.tensor_tensor(out, acc[s], in_groups(rstd, cols), ALU.mult)
                    else:
                        ins = nc.vector.tensor_scalar(out, acc[s], scale, None, ALU.mult)
                    ins.then_inc(psum_free[s], 1)

                if norm:
                    for k in range(kt):
                        dve.wait_ge(x_high, k + 1)
                        nc.vector.scalar_tensor_tensor(src[1][:, k], x_tiles[k], core.vec(gain + k),
                                                       src[0][:, k].bitcast(F32), ALU.mult, ALU.subtract).then_inc(x_ready, 1)
                        if k == 4:
                            split_low(1, 1)
                    for n in range(1, 8):
                        e, k = n % 2, n // 2
                        if n == 1:
                            dve.wait_ge(sq_act, 1)
                        dve.wait_ge((sq_act, sq_pool)[e], k + 1)
                        if n > 1:
                            dve.wait_ge(added, n - 1)
                        first = sq[0][:, 0] if n == 1 else total[:]
                        nc.vector.tensor_tensor(total[:], first, sq[e][:, k % 2], ALU.add).then_inc(added, 1)
                    dve.wait_ge(rstd_ready, 1)
                else:
                    split_low(1, 1)
                with dve.Fori(0, last_pair) as i:
                    for s in range(2):
                        split_low(s, i * 2 + (s + 2))
                        finish_tile(s, i)
                if after is not None:
                    split_low(0, 2 * pairs, after[1])
                for s in range(2):
                    finish_tile(s, last_pair)

            @block.tensor
            def _(pe):
                def tile(s, i, first=False):
                    if not (first and s == 0):
                        pe.wait_ge(low_ready, i * 2 + s)
                    if not first:
                        if finish == "gate":
                            pe.wait_ge((gate_scaled, up_scaled)[s], i)
                        else:
                            pe.wait_ge(psum_free[s], i)
                    for k in range(kt):
                        if norm and first and s == 0:
                            pe.wait_ge(x_ready, k + 1)
                        if norm and first and s == 1 and k == half_k:
                            pe.wait_ge(added, 7)
                            for a in range(groups):
                                ins = nc.tensor.matmul(sums[:, a, :], core.mats[:, ONES],
                                                       total[:, a * width:(a + 1) * width], start=True, stop=True)
                            ins.then_inc(summed, 1)
                        w_high = core.high[s][:, k * P:(k + 1) * P]
                        w_low = core.low[s][:, k * P:(k + 1) * P]
                        passes = ((w_high, src[0]), (w_high, src[1]), (w_low, src[0]))
                        for n, (w, x) in enumerate(passes):
                            for a in range(groups):
                                last = nc.tensor.matmul(acc[s][:, a, :], w, x[:, k, a * width:(a + 1) * width],
                                                        start=(k == 0 and n == 0), stop=(k == kt - 1 and n == 2))
                    last.then_inc(tile_done, 1)

                for s in range(2):
                    tile(s, 0, True)
                with pe.Fori(1, pairs) as i:
                    for s in range(2):
                        tile(s, i)


def rms_norm(nc, core, name, groups, ones, count, cols):
    g_n, width = halves(cols)
    tiles = [(g, t) for g, group in enumerate(groups) for t in range(len(group["x"]))]
    last_of = [sum(len(x["x"]) for x in groups[:g + 1]) for g in range(len(groups))]
    times = "times" in groups[0]
    split = "split" in groups[0]
    with ExitStack() as ctx:
        def sem(what):
            return core.sem(f"{name}_{what}")

        squared, summed, log_ready, rstd_ready = sem("squared"), sem("summed"), sem("log_ready"), sem("rstd_ready")
        normed, timed, high_ready, done = sem("normed"), sem("timed"), sem("high_ready"), sem("done")
        sq = ctx.enter_context(nc.sbuf_tensor(f"{name}_sq", [P, 2, cols], F32))
        rstd = ctx.enter_context(nc.sbuf_tensor(f"{name}_rstd", [P, 2, cols], F32))
        val = ctx.enter_context(nc.sbuf_tensor(f"{name}_val", [P, 2, cols], F32)) if split else None

        def total(g):
            b = 2 * (g % 2)
            return core.ps[:, b:b + g_n, 0:width]

        def value(n, group, t):
            return val[:, n % 2] if split else group["out"][t]

        with nc.Block(name) as block:
            @block.scalar
            def _(act):
                def squares(g):
                    for n, (gg, t) in enumerate(tiles):
                        if gg != g:
                            continue
                        if n >= 2:
                            act.wait_ge(summed, n - 1)
                        nc.scalar.activation(sq[:, n % 2], groups[g]["x"][t], ACT.Square).then_inc(squared, 1)

                def scales(g):
                    act.wait_ge(summed, last_of[g])
                    if g >= 2:
                        act.wait_ge(done, last_of[g - 2])
                    nc.scalar.activation(in_groups(rstd[:, g % 2], cols), total(g), ACT.Ln, bias=core.eps[:],
                                         scale=1.0 / count).then_inc(log_ready, 1)
                    act.wait_ge(log_ready, g + 1)
                    nc.scalar.activation(rstd[:, g % 2], rstd[:, g % 2], ACT.Exp, scale=-0.5).then_inc(rstd_ready, 1)

                def highs(g):
                    for n, (gg, t) in enumerate(tiles):
                        if gg == g:
                            act.wait_ge(timed if times else normed, n + 1)
                            nc.scalar.activation(groups[g]["split"][t][0], value(n, groups[g], t),
                                                 ACT.Copy).then_inc(high_ready, 1)

                for g in range(len(groups) + 1):
                    if g < len(groups):
                        squares(g)
                        scales(g)
                    if g >= 1 and split:
                        highs(g - 1)

            @block.tensor
            def _(pe):
                for n, (g, t) in enumerate(tiles):
                    pe.wait_ge(squared, n + 1)
                    if t == 0 and g >= 2:
                        pe.wait_ge(log_ready, g - 1)
                    for a in range(g_n):
                        last = nc.tensor.matmul(total(g)[:, a, :], ones, sq[:, n % 2, a * width:(a + 1) * width],
                                                start=(t == 0), stop=(t == len(groups[g]["x"]) - 1))
                    last.then_inc(summed, 1)

            @block.vector
            def _(dve):
                def low(n):
                    g, t = tiles[n]
                    dve.wait_ge(high_ready, n + 1)
                    high, low_out = groups[g]["split"][t]
                    nc.vector.tensor_tensor(low_out, value(n, groups[g], t), high.bitcast(F32),
                                            ALU.subtract).then_inc(done, 1)

                for n, (g, t) in enumerate(tiles):
                    group = groups[g]
                    if split and n >= 2:
                        low(n - 2)
                        dve.wait_ge(done, n - 1)
                    if t == 0:
                        dve.wait_ge(rstd_ready, g + 1)
                    ins = nc.vector.scalar_tensor_tensor(value(n, group, t), group["x"][t], group["gain"][t],
                                                         rstd[:, g % 2], ALU.mult, ALU.mult)
                    ins.then_inc(normed if split else done, 1)
                    if times:
                        dve.wait_ge(normed, n + 1)
                        nc.vector.tensor_tensor(value(n, group, t), value(n, group, t), group["times"][t],
                                                ALU.mult).then_inc(timed, 1)
                if split:
                    for n in range(max(0, len(tiles) - 2), len(tiles)):
                        low(n)


def of_x(core, gain):
    return [core.x[:, k] for k in range(KT)], gain


def load_constants(nc, core, a):
    landed, high_ready = core.sem("constants_landed"), core.sem("first_high")
    with nc.Block("constants") as block:
        @block.sync
        def _(sp):
            loads = [(core.x[:], a["x"]), (core.mats[:], a["mats"]), (core.vectors[:], a["vectors"]),
                     (core.mask_chunk[:], a["mask_chunk"]), (core.mask_dec[:], a["mask_dec"]),
                     (core.resets[:], a["resets"])]
            for dst, src in loads:
                sp.dma_start(dst, src).then_inc(landed, 16)
            first_chunks(core, sp, *core.first)
            sp.wait_ge(landed, 16 * len(loads))

        @block.scalar
        def _(act):
            act.wait_ge(core.landed[0], 16)
            high_part(nc, core, 0, core.first[1]).then_inc(high_ready, 1)

        @block.vector
        def _(dve):
            nc.vector.memset(core.eps[:], EPS)
            dve.wait_ge(high_ready, 1)
            low_part(nc, core, 0, core.first[1])
    core.loads = [16, 0]


def ffn(nc, core, which, layer, after):
    name = f"ffn{which}_{layer}"
    with ExitStack() as ctx:
        hid = [ctx.enter_context(nc.sbuf_tensor(f"{name}_hid{s}", [P, HT, TOK], F32R)) for s in range(2)]
        for half in range(2):
            gate_up, down = core.ffn_weights(which, layer, half)
            nxt = (core.ffn_weights(which, layer, 1)[0], KT) if half == 0 else after
            norm = of_x(core, VEC[f"ffn{which}_norm"] + KT * layer) if half == 0 else None
            projection(nc, core, f"{name}_up{half}", gate_up, HT, KT, core.h, TOK, "gate", hid, after=(down, HT),
                       norm=norm, scaled=True)
            projection(nc, core, f"{name}_down{half}", down, KT // 2, HT, hid, TOK, "add", core.x, scale=0.5,
                       after=nxt)


def even_mixer(nc, core, a, out, after_in, after_out):
    qt, kt_, vt, gt = (GQ, GQ + 1, RQ, RQ + 1), (GK, GK + 1, RK, RK + 1), (GV, RV), (GG, RG)
    NB = SEQ // P
    with ExitStack() as ctx:
        pr = ctx.enter_context(nc.sbuf_tensor("even_proj", [P, EVEN_TILES, TOK], F32))
        projection(nc, core, "even_in", core.pairs_of(a["even_w_in"]), EVEN_TILES // 2, KT, core.h, TOK, "copy", pr,
                   after=after_in, norm=of_x(core, VEC["mix_norm"]), scaled=True)
        held = ctx.enter_context(ExitStack())

        def sb(what, shape, dt=F32):
            return held.enter_context(nc.sbuf_tensor(f"even_{what}", shape, dt))

        ki = sb("k_inv", [P, 4, TOK])
        last = sb("decay_last", [P, 4, 16])
        q_tiles = [pr[:, t] for t in qt]
        k_tiles = [pr[:, t] for t in kt_]

        with ExitStack() as c2:
            def sb2(what, shape, dt=F32):
                return c2.enter_context(nc.sbuf_tensor(f"even_{what}", shape, dt))

            def sem(what):
                return core.sem(f"evend_{what}")

            decay = sb2("decay", [P, 3, 4, TOK])
            rot = sb2("rot", [P, 2, TOK])
            wg = sb2("wg", [16, 256])
            za, zb, cum = sb2("za", [P, TOK]), sb2("zb", [P, TOK]), sb2("cum", [P, TOK])
            tables, gate_done, swapped = sem("tables"), sem("gate_done"), sem("swapped")
            dve_steps, act_steps, cos_done = sem("dve_steps"), sem("act_steps"), sem("cos_done")
            rotated = sem("rotated")
            with nc.Block("even_decay") as block:
                @block.sync
                def _(sp):
                    sp.dma_start(decay[:, :, 2:4], a["ret_decay"]).then_inc(tables, 16)
                    sp.dma_start(rot[:], a["ret_rot"]).then_inc(tables, 16)
                    sp.dma_start(wg[:], a["gla_w_gate"]).then_inc(tables, 16)

                @block.tensor
                def _(pe):
                    pe.wait_ge(tables, 48)
                    for j in range(2):
                        for g in range(2):
                            ins = nc.tensor.matmul(core.ps[:, 2 * j + g, 0:272], wg[:, j * P:(j + 1) * P],
                                                   pr[0:16, GA, g * 272:(g + 1) * 272], start=True, stop=True)
                        ins.then_inc(gate_done, 1)
                    for n, t in enumerate((RQ, RQ + 1, RK, RK + 1)):
                        b = 4 + 2 * (n % 2)
                        if n >= 2:
                            pe.wait_ge(rotated, n - 1)
                        for g in range(2):
                            ins = nc.tensor.matmul(core.ps[:, b + g, 0:272], core.mats[:, SWAP2],
                                                   pr[:, t, g * 272:(g + 1) * 272], start=True, stop=True)
                        ins.then_inc(swapped, 1)

                @block.scalar
                def _(act):
                    n = 0

                    def step(ins):
                        nonlocal n
                        n += 1
                        ins.then_inc(act_steps, 1)
                        act.wait_ge(act_steps, n)
                    for j in range(2):
                        act.wait_ge(dve_steps, 5 * j + 1)
                        step(nc.scalar.activation(zb[:], za[:], ACT.Abs))
                        step(nc.scalar.activation(zb[:], zb[:], ACT.Exp, scale=-1.0))
                        step(nc.scalar.activation(zb[:], zb[:], ACT.Ln, bias=1.0))
                        act.wait_ge(dve_steps, 5 * j + 5)
                        step(nc.scalar.activation(decay[:, 0, j], cum[:], ACT.Exp, scale=1.0 / 16))
                        step(nc.scalar.activation(decay[:, 1, j], cum[:], ACT.Exp, scale=-1.0 / 16))
                        step(nc.scalar.activation(decay[:, 2, j], zb[:], ACT.Exp, scale=1.0 / 16))
                        step(nc.scalar.activation(last[:, j, 0:8], cum[:, CHUNK - 1:SEQ:CHUNK], ACT.Exp, scale=1.0 / 16))
                        step(nc.scalar.activation(last[:, j, 8:16], cum[:, SEQ + 3:TOK:4], ACT.Exp, scale=1.0 / 16))

                @block.gpsimd
                def _(pool):
                    pool.wait_ge(tables, 48)
                    for n, t in enumerate((RQ, RQ + 1, RK, RK + 1)):
                        pool.wait_ge(swapped, n + 1)
                        nc.gpsimd.tensor_tensor(pr[:, t], pr[:, t], rot[:, 0], ALU.mult).then_inc(cos_done, 1)

                @block.vector
                def _(dve):
                    n = 0

                    def step(ins):
                        nonlocal n
                        n += 1
                        ins.then_inc(dve_steps, 1)
                        dve.wait_ge(dve_steps, n)
                    for j in range(2):
                        dve.wait_ge(gate_done, j + 1)
                        if j:
                            dve.wait_ge(act_steps, 8 * j)
                        step(nc.vector.tensor_scalar(in_groups(za[:], TOK), core.ps[:, 2 * j:2 * j + 2, 0:272],
                                                     core.vec(VEC["gla_b_gate"] + j), None, ALU.add))
                        dve.wait_ge(act_steps, 8 * j + 3)
                        step(nc.vector.scalar_tensor_tensor(za[:], za[:], 0.0, zb[:], ALU.min, ALU.subtract))
                        step(nc.vector.tensor_tensor_scan(cum[:], core.reset[:], za[:], 0.0, ALU.mult, ALU.add))
                        for lo, hi, w in ((0, SEQ, CHUNK), (SEQ, TOK, DEC_SEQ)):
                            c3 = cum[:, lo:hi].rearrange("p (c t) -> p c t", t=w)
                            end = c3[:, :, w - 1:w].to_broadcast([P, (hi - lo) // w, w])
                            z3 = zb[:, lo:hi].rearrange("p (c t) -> p c t", t=w)
                            step(nc.vector.tensor_tensor(z3, end, c3, ALU.subtract))
                    dve.wait_ge(tables, 48)
                    m = 0
                    for n2, t in enumerate((RQ, RQ + 1, RK, RK + 1)):
                        b = 4 + 2 * (n2 % 2)
                        dve.wait_ge(swapped, n2 + 1)
                        step(nc.vector.tensor_tensor(in_groups(za[:], TOK), core.ps[:, b:b + 2, 0:272],
                                                     in_groups(rot[:, 1], TOK), ALU.mult))
                        dve.wait_ge(cos_done, n2 + 1)
                        nc.vector.tensor_tensor(pr[:, t], pr[:, t], za[:], ALU.add).then_inc(rotated, 1)
                        dve.wait_ge(rotated, n2 + 1)
                    step(nc.vector.tensor_copy(last[:, 2:4, :].rearrange("p a b -> p (a b)"),
                                               core.vectors[:, VEC["ret_last"]:VEC["ret_last"] + 32]))
                    dve.wait_ge(act_steps, 16)
                    for j in range(4):
                        qs, ks = (0.125, 1.0) if j < 2 else (1.0, 0.125)
                        step(nc.vector.scalar_tensor_tensor(q_tiles[j], q_tiles[j], qs, decay[:, 0, j], ALU.mult, ALU.mult))
                        step(nc.vector.scalar_tensor_tensor(ki[:, j], k_tiles[j], ks, decay[:, 1, j], ALU.mult, ALU.mult))
                        step(nc.vector.scalar_tensor_tensor(k_tiles[j], k_tiles[j], ks, decay[:, 2, j], ALU.mult, ALU.mult))

        v_tok = sb("v_tok", [P, NB + 1, 8, P])
        kd_tok = sb("kd_tok", [P, NB + 1, 4, P])
        v_tiles = [pr[:, vt[h // 4] + h % 4] for h in range(8)]
        transposes(nc, core, "even_t", [(v_tiles[0:4], v_tok, 0), (v_tiles[4:8], v_tok, 4), (k_tiles, kd_tok, 0)])

        s_in = sb("s_in", [P, DEC_BATCH, 4, P])
        st = [pr[:, t:t + 2].rearrange("p a c -> p (a c)")[:, 0:3 * 2 * P].rearrange("p (s j c) -> p s j c", s=3, j=2)
              for t in (GK, RK)]
        sc = pr[:, GA, 0:4 * P].rearrange("p (u h c) -> p u h c", u=2, h=2)
        o_tiles = [pr[:, t:t + 4] for t in vt]
        units = [(tt, j) for tt in range(NB) for j in range(4)]
        with ExitStack() as c2:
            def sem(what):
                return core.sem(f"evenr_{what}")

            scored, masked, updated, stated = sem("scored"), sem("masked"), sem("updated"), sem("stated")
            out_done, out_copied, state_in = sem("out_done"), sem("out_copied"), sem("state_in")
            chained, stored, zeroed = sem("chained"), sem("stored"), sem("zeroed")
            with nc.Block("even_recur") as block:
                @block.sync
                def _(sp):
                    for j in range(2):
                        sp.dma_start(s_in[:, :, j, :], a["state_gla"][j]).then_inc(state_in, 16)
                        sp.dma_start(s_in[:, :, 2 + j, :], a["state_ret"][j]).then_inc(state_in, 16)
                    sp.wait_ge(stated, len(units))
                    sp.dma_start(out["p_gla"], st[0][:, 2]).then_inc(stored, 16)
                    sp.dma_start(out["p_ret"], st[1][:, 2]).then_inc(stored, 16)
                    sp.wait_ge(state_in, 64)
                    sp.wait_ge(stored, 32)

                @block.tensor
                def _(pe):
                    def first(u):
                        tt, j = units[u]
                        c = slice(tt * P, (tt + 1) * P)
                        if u >= 2:
                            pe.wait_ge(masked, u - 1)
                        for hh in range(2):
                            r = slice(64 * hh, 64 * hh + 64)
                            ins = nc.tensor.matmul(core.ps[:, 2 * (u % 2) + hh, 0:P], ki[r, j, c],
                                                   q_tiles[j][r, c], start=True, stop=True)
                        ins.then_inc(scored, 1)

                    def updates(u):
                        tt, j = units[u]
                        if u >= 1:
                            pe.wait_ge(stated, u)
                        for half in range(2):
                            s = slice(64 * half, 64 * half + 64)
                            for hh in range(2):
                                ins = nc.tensor.matmul(core.ps[64 * hh:64 * hh + 64, 4 + half, 0:P],
                                                       kd_tok[s, tt, j, 64 * hh:64 * hh + 64],
                                                       v_tok[s, tt, 2 * j + hh, :], start=True, stop=True)
                        ins.then_inc(updated, 1)

                    def second(u):
                        tt, j = units[u]
                        pe.wait_ge(masked, u + 1)
                        pe.wait_ge(chained, u + 1)
                        if u >= 1:
                            pe.wait_ge(out_copied, u)
                        for hh in range(2):
                            r = slice(64 * hh, 64 * hh + 64)
                            o = core.ps[:, 6 + hh, 0:P]
                            nc.tensor.matmul(o, v_tok[:, tt, 2 * j + hh, :], sc[:, u % 2, hh, :], start=True, stop=False)
                            for half in range(2):
                                ch = 2 * tt + half
                                if ch == 0:
                                    continue
                                ins = nc.tensor.matmul(o[:, 64 * half:64 * half + 64], st[j // 2][r, ch % 3, j % 2, :],
                                                       q_tiles[j][r, ch * CHUNK:(ch + 1) * CHUNK],
                                                       start=False, stop=(half == 1))
                        ins.then_inc(out_done, 1)

                    for u in range(len(units) + 1):
                        if u < len(units):
                            first(u)
                        if u >= 1:
                            second(u - 1)
                        if u < len(units):
                            updates(u)

                @block.scalar
                def _(act):
                    for u, (tt, j) in enumerate(units):
                        act.wait_ge(out_done, u + 1)
                        dst = o_tiles[j // 2][:, 2 * (j % 2):2 * (j % 2) + 2, tt * P:(tt + 1) * P]
                        nc.scalar.activation(dst, core.ps[:, 6:8, 0:P], ACT.Copy).then_inc(out_copied, 1)

                @block.vector
                def _(dve):
                    nc.vector.memset(sc, 0.0).then_inc(zeroed, 1)
                    dve.wait_ge(zeroed, 1)
                    for u, (tt, j) in enumerate(units):
                        dve.wait_ge(scored, u + 1)
                        if u >= 2:
                            dve.wait_ge(out_done, u - 1)
                        nc.vector.copy_predicated(sc[:, u % 2], core.mask_chunk[:].rearrange("p (h c) -> p h c", h=2),
                                                  core.ps[:, 2 * (u % 2):2 * (u % 2) + 2, 0:P]).then_inc(masked, 1)
                        dve.wait_ge(updated, u + 1)
                        for half in range(2):
                            ch = 2 * tt + half
                            new = st[j // 2][:, (ch + 1) % 3, j % 2, :]
                            add = core.ps[:, 4 + half, 0:P]
                            if ch >= 2:
                                dve.wait_ge(out_done, u - 4 + 1)
                            if half:
                                dve.wait_ge(chained, u + 1)
                            elif ch >= 2:
                                dve.wait_ge(stated, u - 3)
                            if ch == 0:
                                ins = nc.vector.tensor_copy(new, add)
                            else:
                                ins = nc.vector.scalar_tensor_tensor(new, st[j // 2][:, ch % 3, j % 2, :], last[:, j, ch:ch + 1], add,
                                                                     ALU.mult, ALU.add)
                            ins.then_inc(stated if half else chained, 1)

        kd_b = pr[0:TS, GK:GK + 2].rearrange("p a c -> p (a c)")[:, 0:8 * P].rearrange("p (u c) -> p u c", u=2)
        sc_s = pr[0:TS, GA + 1, 0:8 * TS].rearrange("p (h c) -> p h c", h=8)
        with ExitStack() as c2:
            def sem(what):
                return core.sem(f"evens_{what}")

            zeroed, scored, masked, out_done = sem("zeroed"), sem("scored"), sem("masked"), sem("out_done")
            picked, updated, stated, copied, stored = (sem("picked"), sem("updated"), sem("stated"), sem("copied"),
                                                       sem("stored"))
            with nc.Block("even_sample") as block:
                @block.tensor
                def _(pe):
                    for h in range(8):
                        r, j = slice(64 * (h % 2), 64 * (h % 2) + 64), h // 2
                        ins = nc.tensor.matmul(core.ps[0:TS, h % 2, j * TS:(j + 1) * TS], ki[r, j, SEQ:TOK],
                                               q_tiles[j][r, SEQ:TOK], start=True, stop=True)
                    ins.then_inc(scored, 1)
                    pe.wait_ge(masked, 2)
                    for h in range(8):
                        r, j = slice(64 * (h % 2), 64 * (h % 2) + 64), h // 2
                        o = core.ps[:, 2 + h % 2, j * TS:(j + 1) * TS]
                        nc.tensor.matmul(o, v_tok[0:TS, NB, h, :], sc_s[:, h, :], start=True, stop=False)
                        for b in range(DEC_BATCH):
                            c = slice(DEC_SEQ * b, DEC_SEQ * (b + 1))
                            ins = nc.tensor.matmul(o[:, c], s_in[r, b, j, :],
                                                   q_tiles[j][r, SEQ + DEC_SEQ * b:SEQ + DEC_SEQ * (b + 1)],
                                                   start=False, stop=(b == DEC_BATCH - 1))
                    ins.then_inc(out_done, 1)
                    for b in range(DEC_BATCH):
                        pe.wait_ge(picked, b + 1)
                        if b >= 2:
                            pe.wait_ge(stated, 4 * (b - 1))
                        for h in range(8):
                            ins = nc.tensor.matmul(core.ps[64 * (h % 2):64 * (h % 2) + 64, 4 + b % 2,
                                                           (h // 2) * P:(h // 2 + 1) * P],
                                                   kd_b[:, b % 2, h * 64:(h + 1) * 64], v_tok[0:TS, NB, h, :],
                                                   start=True, stop=True)
                        ins.then_inc(updated, 1)

                @block.scalar
                def _(act):
                    act.wait_ge(out_done, 1)
                    for g in range(2):
                        for hh in range(2):
                            nc.scalar.activation(o_tiles[g][:, hh:4:2, SEQ:TOK],
                                                 core.ps[:, 2 + hh, 2 * g * TS:2 * (g + 1) * TS].rearrange(
                                                     "p (j c) -> p j c", j=2), ACT.Copy).then_inc(copied, 1)

                @block.vector
                def _(dve):
                    nc.vector.memset(sc_s, 0.0).then_inc(zeroed, 1)
                    dve.wait_ge(zeroed, 1)
                    dve.wait_ge(scored, 1)
                    for hh in range(2):
                        nc.vector.copy_predicated(sc_s[:, hh:8:2], core.mask_dec[:].rearrange("p (j c) -> p j c", j=4),
                                                  core.ps[0:TS, hh, 0:4 * TS].rearrange("p (j c) -> p j c", j=4)
                                                  ).then_inc(masked, 1)
                    for b in range(DEC_BATCH + 1):
                        if b < DEC_BATCH:
                            if b >= 2:
                                dve.wait_ge(updated, b - 1)
                            nc.vector.tensor_scalar(kd_b[:, b % 2, :], kd_tok[0:TS, NB].rearrange("p a b -> p (a b)"),
                                                    core.mats[0:TS, 5, b:b + 1], None, ALU.mult).then_inc(picked, 1)
                        if b >= 1:
                            dve.wait_ge(updated, b)
                            dve.wait_ge(out_done, 1)
                            for j in range(4):
                                s = s_in[:, b - 1, j, :]
                                nc.vector.scalar_tensor_tensor(s, s, last[:, j, 8 + b - 1:8 + b],
                                                               core.ps[:, 4 + (b - 1) % 2, j * P:(j + 1) * P],
                                                               ALU.mult, ALU.add).then_inc(stated, 1)

                @block.sync
                def _(sp):
                    sp.wait_ge(stated, 4 * DEC_BATCH)
                    for j in range(2):
                        sp.dma_start(out["s_gla"][j], s_in[:, :, j, :]).then_inc(stored, 16)
                        sp.dma_start(out["s_ret"][j], s_in[:, :, 2 + j, :]).then_inc(stored, 16)
                    sp.wait_ge(stored, 64)

        held.close()
        with nc.Block("even_gates") as block:
            @block.scalar
            def _(act):
                for g in gt:
                    for t in range(4):
                        nc.scalar.activation(pr[:, g + t], pr[:, g + t], ACT.Silu)
        rms_norm(nc, core, "even_on", [dict(
            x=[o_tiles[h // 4][:, h % 4]], gain=[core.vec(VEC["gla_out_norm"] if h < 4 else VEC["one"])],
            split=[(core.h[0][:, h], core.h[1][:, h])], times=[pr[:, gt[h // 4] + h % 4]]) for h in range(8)],
            core.mats[:, ONES], P, TOK)
    projection(nc, core, "even_out", core.pairs_of(a["even_w_out"]), KT // 2, KT, core.h, TOK, "add", core.x,
               after=after_out)


def transposes(nc, core, name, jobs, blocks=None):
    blocks = blocks or [(b * P, P) for b in range(SEQ // P)] + [(SEQ, TS)]
    work = [(lo, w, n, job) for n, (lo, w) in enumerate(blocks) for job in jobs]
    with ExitStack() as ctx:
        turned = core.sem(f"{name}_turned")
        copied = [core.sem(f"{name}_copied{e}") for e in range(2)]
        with nc.Block(name) as block:
            @block.tensor
            def _(pe):
                for u, (lo, w, n, (tiles, dst, at)) in enumerate(work):
                    if u >= 4:
                        pe.wait_ge(copied[u % 2], (u - 4) // 2 + 1)
                    for t, tile in enumerate(tiles):
                        ins = nc.tensor.transpose(core.ps[0:w, u % 4, t * P:(t + 1) * P], tile[:, lo:lo + w],
                                                  core.mats[:, IDENT])
                    ins.then_inc(turned, 1)

            def copies(eng, which, copy):
                for u, (lo, w, n, (tiles, dst, at)) in enumerate(work):
                    if u % 2 == which:
                        eng.wait_ge(turned, u + 1)
                        src = core.ps[0:w, u % 4, 0:len(tiles) * P].rearrange("p (h c) -> p h c", c=P)
                        copy(dst[0:w, n, at:at + len(tiles), :], src).then_inc(copied[which], 1)

            @block.scalar
            def _(act):
                copies(act, 0, lambda o, i: nc.scalar.activation(o, i, ACT.Copy))

            @block.vector
            def _(dve):
                copies(dve, 1, lambda o, i: nc.vector.tensor_copy(o, i))


def memory_attention(nc, core, a, out, layer, after_out):
    name = f"mem{layer}"
    scale = MEM_HD ** -0.5
    w = {n: core.pairs_of(a[f"mem_w_{n}"][layer]) for n in "kvqo"}
    with ExitStack() as ctx:
        def sb(what, shape, dt=F32):
            return ctx.enter_context(nc.sbuf_tensor(f"{name}_{what}", shape, dt))

        kT = sb("kT", [P, KT, N_MEM])
        v_tok = sb("v", [P, 2, KT, P])
        with ExitStack() as c2:
            def sb2(what, shape, dt=F32):
                return c2.enter_context(nc.sbuf_tensor(f"{name}_{what}", shape, dt))

            mem = sb2("mem", [P, KT, N_MEM])
            mh = [sb2("mh0", [P, KT, N_MEM], F32R), sb2("mh1", [P, KT, N_MEM], F32R)]
            with nc.semaphore(f"{name}_loaded") as loaded, nc.Block(f"{name}_load") as block:
                @block.sync
                def _(sp):
                    sp.dma_start(mem[:], a["mem"]).then_inc(loaded, 16)
                    sp.wait_ge(loaded, 16)
            projection(nc, core, name + "k", w["k"], KT // 2, KT, mh, N_MEM, "copy", kT, after=(w["v"], KT),
                       norm=([mem[:, k] for k in range(KT)], VEC["mem_m_norm"] + KT * layer), scaled=True)
            projection(nc, core, name + "v", w["v"], KT // 2, KT, mh, N_MEM, "copy", mem, after=(w["q"], KT),
                       scaled=True)
            rms_norm(nc, core, name + "kn", [dict(
                x=[kT[:, 2 * h + t] for t in range(2)], gain=[core.vec(VEC["mem_k_norm"] + 2 * layer + t) for t in range(2)],
                out=[kT[:, 2 * h + t] for t in range(2)]) for h in range(MEM_HEADS)], core.mats[:, ONES], MEM_HD, N_MEM)
            transposes(nc, core, name + "vt", [([mem[:, k] for k in range(4)], v_tok, 0),
                                               ([mem[:, k] for k in range(4, 8)], v_tok, 4)], [(0, P), (P, P)])
        q = sb("q", [P, KT, TOK])
        projection(nc, core, name + "q", w["q"], KT // 2, KT, core.h, TOK, "copy", q, after=(w["o"], KT),
                   norm=of_x(core, VEC["mem_x_norm"] + KT * layer), scaled=True)
        rms_norm(nc, core, name + "qn", [dict(
            x=[q[:, 2 * h + t] for t in range(2)], gain=[core.vec(VEC["mem_q_norm"] + 2 * layer + t) for t in range(2)],
            out=[q[:, 2 * h + t] for t in range(2)]) for h in range(MEM_HEADS)], core.mats[:, ONES], MEM_HD, TOK)

        units = [(h, b) for h in range(MEM_HEADS) for b in range(SEQ // P)]
        NU = len(units)
        kb = sb("kb", [P, 2, KT, N_MEM])
        vb = sb("vb", [P, 2, 2, KT, P])
        prob = sb("prob", [P, 2, N_MEM])
        pT = sb("pT", [P, 2, 2, SEQ])
        small = sb("small", [P, 4, NU + 1])
        sT = sb("sT", [P, 2, P])
        pTs = sb("pTs", [P, 2, P])
        o_sb = sb("o", [P, 2, SEQ])
        o_s = sb("o_s", [P, KT, TS])
        with ExitStack() as c2:
            def sem(what):
                return core.sem(f"{name}_{what}")

            scored, maxed, negated, exped, inverted, scaled = [sem(n) for n in
                                                             ("scored", "maxed", "negated", "exped", "inverted", "scaled")]
            turned, turn_copied, out_done, out_copied, high_ready, low_ready = [sem(n) for n in
                ("turned", "turn_copied", "out_done", "out_copied", "high_ready", "low_ready")]
            k_in = [sem("k_in0"), sem("k_in1")]
            v_in = [sem("v_in0"), sem("v_in1")]
            k_used, v_used, s_copied, s_turned, stored = (sem("k_used"), sem("v_used"), sem("s_copied"), sem("s_turned"),
                                                          sem("stored"))
            with nc.Block(f"{name}_attend") as block:
                @block.sync
                def _(sp):
                    sp.dma_start(out["p_mem_k"][layer], kT[:]).then_inc(stored, 16)
                    sp.dma_start(out["p_mem_v"][layer], v_tok[:]).then_inc(stored, 16)
                    for b in range(DEC_BATCH):
                        if b >= 2:
                            sp.wait_ge(k_used, b - 1)
                        sp.dma_start(kb[:, b % 2], a["cache_mem_k"][layer, b]).then_inc(k_in[b % 2], 16)
                    for b in range(DEC_BATCH):
                        if b >= 2:
                            sp.wait_ge(v_used, b - 1)
                        sp.dma_start(vb[:, b % 2], a["cache_mem_v"][layer, b]).then_inc(v_in[b % 2], 16)
                    sp.wait_ge(stored, 32)

                @block.tensor
                def _(pe):
                    def scores(u):
                        h, b = units[u]
                        if u >= 2:
                            pe.wait_ge(exped, u - 1)
                        for t in range(2):
                            ins = nc.tensor.matmul(core.ps[:, u % 2, 0:N_MEM], q[:, 2 * h + t, b * P:(b + 1) * P],
                                                   kT[:, 2 * h + t, :], start=(t == 0), stop=(t == 1))
                        ins.then_inc(scored, 1)

                    def turn(u):
                        pe.wait_ge(scaled, u + 1)
                        if u >= 2:
                            pe.wait_ge(turn_copied, u - 1)
                        for t in range(2):
                            ins = nc.tensor.transpose(core.ps[:, 2 + u % 2, t * P:(t + 1) * P],
                                                      prob[:, u % 2, t * P:(t + 1) * P], core.mats[:, IDENT])
                        ins.then_inc(turned, 1)

                    def values(h):
                        pe.wait_ge(turn_copied, 4 * (h + 1))
                        if h >= 1:
                            pe.wait_ge(out_copied, 2 * h)
                        for d in range(2):
                            for t in range(2):
                                ins = nc.tensor.matmul(core.ps[:, 4 + d, :], v_tok[:, t, 2 * h + d, :], pT[:, h % 2, t, :],
                                                       start=(t == 0), stop=(t == 1))
                            ins.then_inc(out_done, 1)

                    def sample_scores(b):
                        pe.wait_ge(k_in[b % 2], 16 * (b // 2 + 1))
                        for m in range(2):
                            for h in range(MEM_HEADS):
                                c = m * P + h * TS + b * DEC_SEQ
                                for t in range(2):
                                    ins = nc.tensor.matmul(core.ps[:, 6, c:c + DEC_SEQ],
                                                           kb[:, b % 2, 2 * h + t, m * P:(m + 1) * P],
                                                           q[:, 2 * h + t, SEQ + b * DEC_SEQ:SEQ + (b + 1) * DEC_SEQ],
                                                           start=(t == 0), stop=(t == 1))
                        ins.then_inc(k_used, 1)

                    for u in range(NU + 1):
                        if u < NU:
                            scores(u)
                            if u % 2 == 1:
                                sample_scores(u // 2)
                        if u >= 1:
                            turn(u - 1)
                            if u % 4 == 0:
                                values(u // 4 - 1)
                    pe.wait_ge(s_copied, 1)
                    pe.wait_ge(exped, NU - 1)
                    for m in range(2):
                        ins = nc.tensor.transpose(core.ps[:, 0, m * P:(m + 1) * P], sT[:, m, :], core.mats[:, IDENT])
                    ins.then_inc(scored, 1)
                    turn(NU)
                    pe.wait_ge(turn_copied, NU + 1)
                    for b in range(DEC_BATCH):
                        pe.wait_ge(v_in[b % 2], 16 * (b // 2 + 1))
                        for f in range(KT):
                            c = f * TS + b * DEC_SEQ
                            r = (f // 2) * TS + b * DEC_SEQ
                            for t in range(2):
                                ins = nc.tensor.matmul(core.ps[:, 7, c:c + DEC_SEQ], vb[:, b % 2, t, f, :],
                                                       pTs[:, t, r:r + DEC_SEQ], start=(t == 0), stop=(t == 1))
                        ins.then_inc(v_used, 1)

                @block.vector
                def _(dve):
                    def row_max(u):
                        dve.wait_ge(scored, u + 1)
                        nc.vector.tensor_reduce(small[:, 0, u:u + 1], core.ps[:, u % 2, 0:N_MEM], AX_X, ALU.max
                                                ).then_inc(maxed, 1)
                        dve.wait_ge(maxed, u + 1)
                        nc.vector.tensor_scalar(small[:, 1, u:u + 1], small[:, 0, u:u + 1], -scale, None, ALU.mult
                                                ).then_inc(negated, 1)

                    def divide(u):
                        dve.wait_ge(exped, u + 1)
                        nc.vector.reciprocal(small[:, 3, u:u + 1], small[:, 2, u:u + 1]).then_inc(inverted, 1)
                        dve.wait_ge(inverted, u + 1)
                        nc.vector.tensor_scalar(prob[:, u % 2], prob[:, u % 2], small[:, 3, u:u + 1], None, ALU.mult
                                                ).then_inc(scaled, 1)

                    def low(h):
                        for d in range(2):
                            n = 2 * h + d
                            dve.wait_ge(high_ready, n + 1)
                            nc.vector.tensor_tensor(core.h[1][:, n, 0:SEQ], o_sb[:, d], core.h[0][:, n, 0:SEQ].bitcast(F32),
                                                    ALU.subtract).then_inc(low_ready, 1)

                    for u in range(NU):
                        row_max(u)
                        if u >= 1:
                            divide(u - 1)
                        if u % 4 == 3 and u > 4:
                            low(u // 4 - 1)
                    divide(NU - 1)
                    low(MEM_HEADS - 1)
                    dve.wait_ge(k_used, DEC_BATCH)
                    nc.vector.tensor_copy(sT[:], core.ps[:, 6, 0:2 * P].rearrange("p (m c) -> p m c", m=2)
                                          ).then_inc(s_copied, 1)
                    row_max(NU)
                    divide(NU)
                    dve.wait_ge(v_used, DEC_BATCH)
                    nc.vector.tensor_copy(o_s[:], core.ps[:, 7, 0:KT * TS].rearrange("p (f c) -> p f c", f=KT)
                                          ).then_inc(s_copied, 1)
                    dve.wait_ge(high_ready, 2 * MEM_HEADS + 1)
                    nc.vector.tensor_tensor(core.h[1][:, :, SEQ:TOK], o_s[:], core.h[0][:, :, SEQ:TOK].bitcast(F32),
                                            ALU.subtract).then_inc(low_ready, 1)

                @block.scalar
                def _(act):
                    def exps(u):
                        act.wait_ge(negated, u + 1)
                        if u >= 2:
                            act.wait_ge(turned, u - 1)
                        nc.scalar.activation(prob[:, u % 2], core.ps[:, u % 2, 0:N_MEM], ACT.Exp,
                                             bias=small[:, 1, u:u + 1], scale=scale, accum_out=small[:, 2, u:u + 1]
                                             ).then_inc(exped, 1)

                    def turned_copy(u):
                        act.wait_ge(turned, u + 1)
                        if u == NU:
                            dst = pTs[:]
                        else:
                            h, b = units[u]
                            if b == 0 and h >= 2:
                                act.wait_ge(out_done, 2 * (h - 1))
                            dst = pT[:, h % 2, :, b * P:(b + 1) * P]
                        nc.scalar.activation(dst, core.ps[:, 2 + u % 2, 0:2 * P].rearrange("p (t c) -> p t c", t=2),
                                             ACT.Copy).then_inc(turn_copied, 1)

                    def high(h):
                        for d in range(2):
                            n = 2 * h + d
                            act.wait_ge(out_done, n + 1)
                            if h >= 1:
                                act.wait_ge(low_ready, 2 * (h - 1) + d + 1)
                            nc.scalar.activation(o_sb[:, d], core.ps[:, 4 + d, :], ACT.Copy).then_inc(out_copied, 1)
                            act.wait_ge(out_copied, n + 1)
                            nc.scalar.activation(core.h[0][:, n, 0:SEQ], o_sb[:, d], ACT.Copy).then_inc(high_ready, 1)

                    for u in range(NU + 1):
                        if u < NU:
                            exps(u)
                        if u >= 1:
                            turned_copy(u - 1)
                            if u % 4 == 0:
                                high(u // 4 - 1)
                    exps(NU)
                    turned_copy(NU)
                    act.wait_ge(s_copied, 2)
                    nc.scalar.activation(core.h[0][:, :, SEQ:TOK], o_s[:], ACT.Copy).then_inc(high_ready, 1)
    projection(nc, core, name + "o", w["o"], KT // 2, KT, core.h, TOK, "add", core.x, after=after_out)


def s5(nc, core, pr, a, out):
    T, NB = S5_TILES, 8
    with ExitStack() as ctx:
        def sb(what, shape, dt=F32):
            return ctx.enter_context(nc.sbuf_tensor(f"s5_{what}", shape, dt))

        def sem(what):
            return core.sem(f"s5_{what}")

        prm = sb("prm", [P, 12, T])
        STEP, MAG, TH, PHI, PHIC, RND, SIN, COS, ABR, ABI, CR, CI = range(12)
        tmp = sb("tmp", [P, 4, T])
        fine = sb("fine", [P, 4, T, CHUNK])
        coarse = sb("coarse", [P, 4, T, NB])
        phi2 = sb("phi2", [P, 2, T])
        steps = sb("steps", [P, CHUNK + NB])
        b_in = sb("b_in", [P, 2, T, 32])
        bb = sb("bb", [P, 2, T, 32])
        bt = sb("bt", [P, 2, 4, P])
        cT = sb("cT", [P, 2, T, P])
        s0 = sb("s0", [P, 2, T, DEC_BATCH])
        inj = sb("inj", [P, 2, T, DEC_BATCH])
        fin = sb("fin", [P, 2, T, DEC_BATCH + 1])
        rot = sb("rot", [P, 2, 2, TOK])
        mags = sb("mags", [P, TOK])
        t0, t1, t2, t3 = sb("t0", [P, TOK]), sb("t1", [P, TOK]), sb("t2", [P, TOK]), sb("t3", [P, TOK])
        g = sb("g", [P, 2, TOK])
        hs = sb("hs", [P, 2, 2, TOK])
        z = core.z
        loaded, act_steps, dve_steps, b_turned, bt_ready = [sem(n) for n in
            ("loaded", "act_steps", "dve_steps", "b_turned", "bt_ready")]
        driven, drive_read, rot_ready, state_ready, tile_used = [sem(n) for n in
            ("driven", "drive_read", "rot_ready", "state_ready", "tile_used")]
        y_ready, summed, high_ready, z_ready, stored, fin_ready, pool_steps = [sem(n) for n in
            ("y_ready", "summed", "high_ready", "z_ready", "stored", "fin_ready", "pool_steps")]
        g2_ready, mags_ready, chain = sem("g2_ready"), sem("mags_ready"), sem("chain")
        v = nc.vector
        ANGLES = 8 + 5 + 3 + 2 * (7 + 5)

        with nc.Block("s5_prepare") as block:
            @block.sync
            def _(sp):
                for dst, src in ((steps[:], a["s5_steps"]), (b_in[:], a["s5_b"]), (cT[:], a["s5_c"]), (s0[:], a["state_s5"])):
                    sp.dma_start(dst, src).then_inc(loaded, 16)

            @block.scalar
            def _(act):
                n = 0

                def step(ins):
                    nonlocal n
                    n += 1
                    ins.then_inc(act_steps, 1)
                    act.wait_ge(act_steps, n)
                step(nc.scalar.activation(prm[:, STEP], core.vecs("s5_log_step"), ACT.Exp))
                act.wait_ge(dve_steps, 1)
                step(nc.scalar.activation(prm[:, MAG], prm[:, MAG], ACT.Exp))
                act.wait_ge(dve_steps, ANGLES)
                step(nc.scalar.activation(prm[:, SIN:COS + 1], prm[:, SIN:COS + 1], ACT.Sin))
                step(nc.scalar.activation(fine[:, 0:2], fine[:, 0:2], ACT.Sin))
                step(nc.scalar.activation(coarse[:, 0:2], coarse[:, 0:2], ACT.Sin))

            @block.tensor
            def _(pe):
                pe.wait_ge(bt_ready, 1)
                for ri in range(2):
                    for j4 in range(4):
                        ins = nc.tensor.transpose(core.ps[:, ri, j4 * P:(j4 + 1) * P],
                                                  bb[:, ri, 4 * j4:4 * j4 + 4, :].rearrange("p a b -> p (a b)"),
                                                  core.mats[:, IDENT])
                ins.then_inc(b_turned, 1)

            def to_angle(step, x, ring):
                step(v.tensor_scalar(ring, x, MAGIC, None, ALU.add))
                step(v.tensor_scalar(ring, ring, MAGIC, None, ALU.subtract))
                step(v.tensor_tensor(x, x, ring, ALU.subtract))
                step(v.tensor_scalar(x, x, TWO_PI, PI_SAFE, ALU.mult, ALU.min))
                step(v.tensor_scalar(x, x, -PI_SAFE, None, ALU.max))

            def prepare(step, dve, waits=True):
                if waits:
                    dve.wait_ge(act_steps, 1)
                step(v.tensor_tensor(prm[:, MAG], core.vecs("s5_a_re"), prm[:, STEP], ALU.mult))
                step(v.tensor_tensor(prm[:, TH], core.vecs("s5_a_im"), prm[:, STEP], ALU.mult))
                step(v.tensor_scalar(prm[:, PHI], prm[:, TH], 1.0 / TWO_PI, None, ALU.mult))
                step(v.tensor_scalar(prm[:, RND], prm[:, PHI], MAGIC, None, ALU.add))
                step(v.tensor_scalar(prm[:, RND], prm[:, RND], MAGIC, None, ALU.subtract))
                step(v.tensor_tensor(prm[:, PHI], prm[:, PHI], prm[:, RND], ALU.subtract))
                step(v.tensor_copy(prm[:, SIN], prm[:, PHI]))
                step(v.tensor_scalar(prm[:, COS], prm[:, PHI], 0.25, None, ALU.add))
                to_angle(step, prm[:, SIN:COS + 1], tmp[:, 0:2])
                step(v.tensor_scalar(tmp[:, 0], prm[:, PHI], MAGIC13, None, ALU.add))
                step(v.tensor_scalar(phi2[:, 0], tmp[:, 0], MAGIC13, None, ALU.subtract))
                step(v.tensor_tensor(phi2[:, 1], prm[:, PHI], phi2[:, 0], ALU.subtract))
                if waits:
                    dve.wait_ge(loaded, 64)
                for tab, lo, w in ((fine, 0, CHUNK), (coarse, CHUNK, NB)):
                    num = steps[:, lo:lo + w].rearrange("p (o c) -> p o c", o=1).to_broadcast([P, T, w])
                    hi = phi2[:, 0].rearrange("p (t o) -> p t o", o=1).to_broadcast([P, T, w])
                    lo_ = phi2[:, 1].rearrange("p (t o) -> p t o", o=1).to_broadcast([P, T, w])
                    step(v.tensor_tensor(tab[:, 0], num, hi, ALU.mult))
                    step(v.tensor_scalar(tab[:, 2], tab[:, 0], MAGIC, None, ALU.add))
                    step(v.tensor_scalar(tab[:, 2], tab[:, 2], MAGIC, None, ALU.subtract))
                    step(v.tensor_tensor(tab[:, 0], tab[:, 0], tab[:, 2], ALU.subtract))
                    step(v.tensor_tensor(tab[:, 2], num, lo_, ALU.mult))
                    step(v.tensor_tensor(tab[:, 1], tab[:, 0], tab[:, 2], ALU.add))
                    step(v.tensor_scalar(tab[:, 0], tab[:, 1], 0.25, None, ALU.add))
                    to_angle(step, tab[:, 0:2], tab[:, 2:4])

            @block.vector
            def _(dve):
                n = 0

                def step(ins):
                    nonlocal n
                    n += 1
                    ins.then_inc(dve_steps, 1)
                    dve.wait_ge(dve_steps, n)

                prepare(step, dve)
                assert n == ANGLES
                dve.wait_ge(act_steps, 5)
                are, aim = core.vecs("s5_a_re"), core.vecs("s5_a_im")
                m = tmp
                step(v.tensor_tensor(prm[:, ABR], prm[:, MAG], prm[:, COS], ALU.mult))
                step(v.tensor_tensor(prm[:, ABI], prm[:, MAG], prm[:, SIN], ALU.mult))
                step(v.tensor_tensor(m[:, 0], are, are, ALU.mult))
                step(v.tensor_tensor(m[:, 1], aim, aim, ALU.mult))
                step(v.tensor_tensor(m[:, 0], m[:, 0], m[:, 1], ALU.add))
                step(v.reciprocal(m[:, 0], m[:, 0]))
                step(v.tensor_scalar(m[:, 1], prm[:, ABR], 1.0, None, ALU.subtract))
                step(v.tensor_tensor(m[:, 2], m[:, 1], are, ALU.mult))
                step(v.tensor_tensor(m[:, 3], prm[:, ABI], aim, ALU.mult))
                step(v.tensor_tensor(m[:, 2], m[:, 2], m[:, 3], ALU.add))
                step(v.tensor_tensor(prm[:, CR], m[:, 2], m[:, 0], ALU.mult))
                step(v.tensor_tensor(m[:, 2], prm[:, ABI], are, ALU.mult))
                step(v.tensor_tensor(m[:, 3], m[:, 1], aim, ALU.mult))
                step(v.tensor_tensor(m[:, 2], m[:, 2], m[:, 3], ALU.subtract))
                step(v.tensor_tensor(prm[:, CI], m[:, 2], m[:, 0], ALU.mult))

                def cmul(o_re, o_im, x_re, x_im, y_re, y_im, s):
                    step(v.tensor_tensor(o_re, x_re, y_re, ALU.mult))
                    step(v.tensor_tensor(s, x_im, y_im, ALU.mult))
                    step(v.tensor_tensor(o_re, o_re, s, ALU.subtract))
                    step(v.tensor_tensor(o_im, x_re, y_im, ALU.mult))
                    step(v.tensor_tensor(s, x_im, y_re, ALU.mult))
                    step(v.tensor_tensor(o_im, o_im, s, ALU.add))

                def over(i, w):
                    return prm[:, i].rearrange("p (t o) -> p t o", o=1).to_broadcast([P, T, w])

                cmul(bb[:, 0], bb[:, 1], over(CR, 32), over(CI, 32), b_in[:, 0], b_in[:, 1],
                     t0[:, 0:T * 32].rearrange("p (t c) -> p t c", t=T))
                step(v.tensor_scalar(cT[:, 1], cT[:, 1], -1.0, None, ALU.mult))
                cmul(inj[:, 0], inj[:, 1], over(ABR, DEC_BATCH), over(ABI, DEC_BATCH), s0[:, 0], s0[:, 1],
                     t0[:, 0:T * DEC_BATCH].rearrange("p (t c) -> p t c", t=T))
                dve.sem_inc(bt_ready, 1)
                dve.wait_ge(b_turned, 1)
                v.tensor_copy(bt[:].rearrange("p r j c -> p r (j c)"), core.ps[:, 0:2, :]).then_inc(bt_ready, 1)

        with nc.Block("s5_scan") as block:
            @block.tensor
            def _(pe):
                def drive(j):
                    r = slice(32 * (j % 4), 32 * (j % 4) + 32)
                    if j >= 1:
                        pe.wait_ge(drive_read, j)
                    for ri in range(2):
                        for gr in range(2):
                            ins = nc.tensor.matmul(core.ps[:, 2 * ri + gr, 0:272], bt[r, ri, j // 4, :],
                                                   pr[r, SU + j // 4, gr * 272:(gr + 1) * 272], start=True, stop=True)
                    ins.then_inc(driven, 1)

                def outputs(j):
                    pe.wait_ge(state_ready, 2 * (j + 1))
                    if j % 4 == 0 and j >= 8:
                        pe.wait_ge(y_ready, j // 4 - 1)
                    b = 4 + 2 * ((j // 4) % 2)
                    for ri in range(2):
                        for gr in range(2):
                            ins = nc.tensor.matmul(core.ps[:, b + gr, 0:272], cT[:, ri, j, :],
                                                   hs[:, j % 2, ri, gr * 272:(gr + 1) * 272],
                                                   start=(j % 4 == 0 and ri == 0), stop=(j % 4 == 3 and ri == 1))
                    ins.then_inc(tile_used, 1)

                for j in range(T + 1):
                    if j < T:
                        drive(j)
                    if j >= 1:
                        outputs(j - 1)

            def finish_y(dve, t):
                b = 4 + 2 * (t % 2)
                dve.wait_ge(tile_used, 4 * (t + 1))
                v.scalar_tensor_tensor(in_groups(z[:, t], TOK), in_groups(pr[:, SU + t], TOK), core.vec(VEC["s5_d"] + t),
                                       core.ps[:, b:b + 2, 0:272], ALU.mult, ALU.add).then_inc(y_ready, 1)

            @block.gpsimd
            def _(pool):
                n = 0

                def step(ins):
                    nonlocal n
                    n += 1
                    ins.then_inc(pool_steps, 1)
                    pool.wait_ge(pool_steps, n)
                for j in range(T):
                    if j >= 2:
                        pool.wait_ge(state_ready, 2 * (j - 1))
                    dst = [rot[:, j % 2, ri, 0:SEQ].rearrange("p (c t) -> p c t", t=CHUNK) for ri in range(2)]
                    co = [coarse[:, ri, j].rearrange("p (c o) -> p c o", o=1).to_broadcast([P, NB, CHUNK]) for ri in range(2)]
                    fi = [fine[:, ri, j].rearrange("p (o t) -> p o t", o=1).to_broadcast([P, NB, CHUNK]) for ri in range(2)]
                    sc = t3[:, 0:SEQ].rearrange("p (c t) -> p c t", t=CHUNK)
                    step(nc.gpsimd.tensor_tensor(dst[0], co[0], fi[0], ALU.mult))
                    step(nc.gpsimd.tensor_tensor(sc, co[1], fi[1], ALU.mult))
                    step(nc.gpsimd.tensor_tensor(dst[0], dst[0], sc, ALU.subtract))
                    step(nc.gpsimd.tensor_tensor(dst[1], co[1], fi[0], ALU.mult))
                    step(nc.gpsimd.tensor_tensor(sc, co[0], fi[1], ALU.mult))
                    step(nc.gpsimd.tensor_tensor(dst[1], dst[1], sc, ALU.add))
                    for ri in range(2):
                        src = fine[:, ri, j, 0:DEC_SEQ].rearrange("p (o t) -> p o t", o=1).to_broadcast([P, DEC_BATCH, DEC_SEQ])
                        ins = nc.gpsimd.tensor_copy(rot[:, j % 2, ri, SEQ:TOK].rearrange("p (b t) -> p b t", t=DEC_SEQ), src)
                        if ri == 0:
                            step(ins)
                    ins.then_inc(rot_ready, 1)

            @block.vector
            def _(dve):
                n = 0

                def step(ins):
                    nonlocal n
                    n += 1
                    ins.then_inc(chain, 1)
                    dve.wait_ge(chain, n)

                def wide(ap):
                    return in_groups(ap, TOK)
                for j in range(T):
                    dve.wait_ge(driven, j + 1)
                    dve.wait_ge(rot_ready, j + 1)
                    co, si = rot[:, j % 2, 0], rot[:, j % 2, 1]
                    re, im = core.ps[:, 0:2, 0:272], core.ps[:, 2:4, 0:272]
                    v.tensor_scalar(mags[:], core.reset_s5[:], prm[:, MAG, j:j + 1], None, ALU.mult)
                    v.tensor_tensor(wide(t0[:]), re, wide(co), ALU.mult)
                    v.tensor_tensor(wide(t1[:]), im, wide(si), ALU.mult)
                    v.tensor_tensor(wide(t2[:]), im, wide(co), ALU.mult)
                    step(v.tensor_tensor(wide(g[:, 1]), re, wide(si), ALU.mult))
                    v.tensor_tensor(t0[:], t0[:], t1[:], ALU.add)
                    step(v.tensor_tensor(t2[:], t2[:], g[:, 1], ALU.subtract))
                    first = slice(SEQ, TOK, DEC_SEQ)
                    v.tensor_tensor(t0[:, first], t0[:, first], inj[:, 0, j], ALU.add)
                    ins = v.tensor_tensor(t2[:, first], t2[:, first], inj[:, 1, j], ALU.add)
                    ins.then_inc(drive_read, 1)
                    dve.wait_ge(drive_read, j + 1)
                    v.tensor_tensor_scan(g[:, 0], mags[:], t0[:], 0.0, ALU.mult, ALU.add)
                    step(v.tensor_tensor_scan(g[:, 1], mags[:], t2[:], 0.0, ALU.mult, ALU.add))
                    if j >= 2:
                        dve.wait_ge(tile_used, j - 1)
                    hr, hi = hs[:, j % 2, 0], hs[:, j % 2, 1]
                    v.tensor_tensor(hr, g[:, 0], co, ALU.mult)
                    v.tensor_tensor(t0[:], g[:, 1], si, ALU.mult)
                    v.tensor_tensor(hi, g[:, 0], si, ALU.mult)
                    step(v.tensor_tensor(t1[:], g[:, 1], co, ALU.mult))
                    v.tensor_tensor(hr, hr, t0[:], ALU.subtract).then_inc(state_ready, 1)
                    v.tensor_tensor(hi, hi, t1[:], ALU.add).then_inc(state_ready, 1)
                    dve.wait_ge(state_ready, 2 * (j + 1))
                    for ri in range(2):
                        v.tensor_copy(fin[:, ri, j, 0:1], hs[:, j % 2, ri, SEQ - 1:SEQ])
                        step(v.tensor_copy(fin[:, ri, j, 1:9], hs[:, j % 2, ri, SEQ + 3:TOK:DEC_SEQ]))
                    if j % 4 == 3 and j > 4:
                        finish_y(dve, j // 4 - 1)
                finish_y(dve, 3)

            @block.scalar
            def _(act):
                for t in range(4):
                    act.wait_ge(y_ready, t + 1)
                    nc.scalar.activation(z[:, t], z[:, t], ACT.Gelu_apprx_tanh).then_inc(z_ready, 1)
                    act.wait_ge(z_ready, t + 1)
                    nc.scalar.activation(core.h[0][:, 4 + t], z[:, t], ACT.Copy).then_inc(high_ready, 1)

            @block.sync
            def _(sp):
                sp.wait_ge(y_ready, 4)
                sp.dma_start(out["s5"], fin[:]).then_inc(stored, 16)
                sp.wait_ge(stored, 16)

        with nc.Block("s5_low") as block:
            @block.vector
            def _(dve):
                nc.vector.tensor_tensor(core.h[1][:, 4:8], z[:], core.h[0][:, 4:8].bitcast(F32), ALU.subtract)


def s5_gate(nc, core, glu):
    with ExitStack() as ctx:
        def sem(what):
            return core.sem(f"glu_{what}")

        sig_ready, prod_ready, high_ready = sem("sig_ready"), sem("prod_ready"), sem("high_ready")
        with nc.Block("s5_gate") as block:
            @block.scalar
            def _(act):
                for t in range(4):
                    nc.scalar.activation(glu[:, t], glu[:, t], ACT.Sigmoid, bias=core.vec(VEC["s5_b_glu"] + t)
                                         ).then_inc(sig_ready, 1)
                for t in range(4):
                    act.wait_ge(prod_ready, t + 1)
                    nc.scalar.activation(core.h[0][:, t], core.z[:, t], ACT.Copy).then_inc(high_ready, 1)

            @block.vector
            def _(dve):
                for t in range(4):
                    dve.wait_ge(sig_ready, t + 1)
                    nc.vector.tensor_tensor(core.z[:, t], core.z[:, t], glu[:, t], ALU.mult).then_inc(prod_ready, 1)
                for t in range(4):
                    dve.wait_ge(high_ready, t + 1)
                    nc.vector.tensor_tensor(core.h[1][:, t], core.z[:, t], core.h[0][:, t].bitcast(F32), ALU.subtract)


def window_attention(nc, core, pr, a, out):
    scale = 64 ** -0.5
    NB = SEQ // P
    with ExitStack() as ctx:
        def sb(what, shape, dt=F32):
            return ctx.enter_context(nc.sbuf_tensor(f"swa_{what}", shape, dt))

        heads = [pr[:, SQ + i] for i in range(4)] + [pr[:, SK]]
        rms_norm(nc, core, "swa_qk", [dict(x=[x], out=[x], gain=[core.vec(VEC["swa_q_norm" if i < 4 else "swa_k_norm"])])
                                      for i, x in enumerate(heads)], core.mats[:, ONES64], 64, TOK)
        rot = sb("rot", [P, 2, TOK])
        tmp = sb("tmp", [P, TOK])
        kc = sb("kc", [P, DEC_BATCH, P])
        vc = sb("vc", [P, DEC_BATCH, P])
        v_tok = sb("v_tok", [P, NB + 1, 1, P])
        mask = sb("mask", [P, 2 * P])
        mask_s = sb("mask_s", [P, P + TS])
        transposes(nc, core, "swa_vt", [([pr[:, SV]], v_tok, 0)])
        with ExitStack() as c2:
            def sem(what):
                return core.sem(f"swar_{what}")
            loaded, swapped, cosed, sined, rotated = [sem(n) for n in ("loaded", "swapped", "cosed", "sined", "rotated")]
            with nc.Block("swa_rotate") as block:
                @block.sync
                def _(sp):
                    loads = ((rot[:], a["swa_rot"]), (kc[:], a["cache_swa_k"]), (vc[:], a["cache_swa_v"]),
                             (mask[:], a["swa_mask"]), (mask_s[:], a["swa_mask_s"]))
                    for dst, src in loads:
                        sp.dma_start(dst, src).then_inc(loaded, 16)
                    sp.wait_ge(loaded, 16 * len(loads))

                @block.tensor
                def _(pe):
                    for n, x in enumerate(heads):
                        b = 2 * (n % 2)
                        if n >= 2:
                            pe.wait_ge(sined, n - 1)
                        for g in range(2):
                            ins = nc.tensor.matmul(core.ps[:, b + g, 0:272], core.mats[:, SWAP8],
                                                   x[:, g * 272:(g + 1) * 272], start=True, stop=True)
                        ins.then_inc(swapped, 1)

                @block.vector
                def _(dve):
                    dve.wait_ge(loaded, 80)
                    for n, x in enumerate(heads):
                        b = 2 * (n % 2)
                        dve.wait_ge(swapped, n + 1)
                        if n:
                            dve.wait_ge(rotated, n)
                        nc.vector.tensor_tensor(in_groups(tmp[:], TOK), core.ps[:, b:b + 2, 0:272],
                                                in_groups(rot[:, 1], TOK), ALU.mult).then_inc(sined, 1)
                        nc.vector.tensor_tensor(x, x, rot[:, 0], ALU.mult).then_inc(cosed, 1)
                        dve.wait_ge(sined, n + 1)
                        dve.wait_ge(cosed, n + 1)
                        nc.vector.tensor_tensor(x, x, tmp[:], ALU.add).then_inc(rotated, 1)

        units = [(b, i, kv) for b in range(NB) for i in range(4) for kv in range(2)]
        NU = len(units)
        logit = sb("logit", [P, 2, 2 * P])
        prob = sb("prob", [P, 2, 2 * P])
        pT = sb("pT", [P, 2, 2, P])
        small = sb("small", [P, 7, NU + 2])
        qs = sb("qs", [P, 4 * TS])
        sT = sb("sT", [P, 2, P])
        o_sb = sb("o_sb", [P, 4, TOK])
        sinks = core.vecs("sinks")
        kT = pr[:, SK]
        with ExitStack() as c2:
            def sem(what):
                return core.sem(f"swa_{what}")

            names = ("scored", "masked", "maxed", "sunk", "negated", "exped", "sink_exped", "totalled", "inverted", "scaled",
                     "turned", "turn_copied", "out_done", "out_copied", "q_ready", "cached", "sT_ready", "stored", "high_ready")
            S = {n: sem(n) for n in names}

            def keys(u):
                b = units[u][0] if u < NU else None
                return 2 * P if u < NU and b else (P if u < NU else P + TS)

            with nc.Block("swa_attend") as block:
                @block.sync
                def _(sp):
                    with nc.allow_non_contiguous_dma(reason="four new rows a batch"):
                        sp.dma_start(out["s_swa_k"][:, :, 0:WIN - DEC_SEQ], kc[:, :, DEC_SEQ:WIN]).then_inc(S["stored"], 16)
                        sp.dma_start(out["s_swa_k"][:, :, WIN - DEC_SEQ:WIN],
                                     kT[:, SEQ:TOK].rearrange("p (b t) -> p b t", t=DEC_SEQ)).then_inc(S["stored"], 16)
                        sp.dma_start(out["s_swa_v"][0:WIN - DEC_SEQ], vc[DEC_SEQ:WIN]).then_inc(S["stored"], 16)
                        for b in range(DEC_BATCH):
                            sp.dma_start(out["s_swa_v"][WIN - DEC_SEQ:WIN, b],
                                         v_tok[DEC_SEQ * b:DEC_SEQ * (b + 1), NB, 0, :]).then_inc(S["stored"], 16)
                        sp.dma_start(out["p_swa_k"], kT[:, SEQ - WIN:SEQ]).then_inc(S["stored"], 16)
                        sp.dma_start(out["p_swa_v"], v_tok[:, NB - 1, 0, :]).then_inc(S["stored"], 16)
                    sp.wait_ge(S["stored"], 16 * (5 + DEC_BATCH))

                @block.tensor
                def _(pe):
                    def scores(u):
                        b, i, kv = units[u]
                        r = slice(64 * kv, 64 * kv + 64)
                        lo = max(0, b - 1) * P
                        if u >= 2:
                            pe.wait_ge(S["masked"], u - 1)
                        nc.tensor.matmul(core.ps[:, u % 2, 0:keys(u)], pr[r, SQ + i, b * P:(b + 1) * P],
                                         kT[r, lo:(b + 1) * P], start=True, stop=True).then_inc(S["scored"], 1)

                    def turn(u):
                        pe.wait_ge(S["scaled"], u + 1)
                        if u >= 2:
                            pe.wait_ge(S["turn_copied"], u - 1)
                        n = keys(u)
                        for t in range((n + P - 1) // P):
                            w = min(P, n - t * P)
                            ins = nc.tensor.transpose(core.ps[0:w, 2 + u % 2, t * P:(t + 1) * P],
                                                      prob[:, u % 2, t * P:t * P + w], core.mats[:, IDENT])
                        ins.then_inc(S["turned"], 1)

                    def values(u):
                        b, i, kv = units[u]
                        r = slice(64 * kv, 64 * kv + 64)
                        pe.wait_ge(S["turn_copied"], u + 1)
                        if u >= 4:
                            pe.wait_ge(S["out_copied"], u // 2 - 1)
                        nt = keys(u) // P
                        for t in range(nt):
                            ins = nc.tensor.matmul(core.ps[r, 4 + (u // 2) % 2, 0:P],
                                                   v_tok[:, b - nt + 1 + t, 0, r], pT[:, u % 2, t, :],
                                                   start=(t == 0), stop=(t == nt - 1))
                        ins.then_inc(S["out_done"], 1)

                    def sample_scores(kv):
                        r = slice(64 * kv, 64 * kv + 64)
                        u = NU + kv
                        pe.wait_ge(S["q_ready"], 4)
                        for b in range(DEC_BATCH):
                            ins = nc.tensor.matmul(core.ps[:, 6 + kv, b * 16:(b + 1) * 16], kc[r, b, :],
                                                   qs[r, b * 16:(b + 1) * 16], start=True, stop=True)
                        ins.then_inc(S["cached"], 1)
                        pe.wait_ge(S["sT_ready"], kv + 1)
                        pe.wait_ge(S["masked"], u - 1)
                        nc.tensor.transpose(core.ps[:, u % 2, 0:P], sT[:, kv, :], core.mats[:, IDENT])
                        nc.tensor.matmul(core.ps[:, u % 2, P:P + TS], qs[r, :], kT[r, SEQ:TOK],
                                         start=True, stop=True).then_inc(S["scored"], 1)

                    def sample_values(kv):
                        r = slice(64 * kv, 64 * kv + 64)
                        u = NU + kv
                        pe.wait_ge(S["turn_copied"], u + 1)
                        if kv == 0:
                            pe.wait_ge(S["out_copied"], NU // 2 - 1)
                        o = core.ps[r, 4, 0:P]
                        nc.tensor.matmul(o, v_tok[0:TS, NB, 0, r], pT[0:TS, u % 2, 1, :], start=True, stop=False)
                        for b in range(DEC_BATCH):
                            ins = nc.tensor.matmul(o[:, b * 16:(b + 1) * 16], vc[:, b, r], pT[:, u % 2, 0, b * 16:(b + 1) * 16],
                                                   start=False, stop=(b == DEC_BATCH - 1))
                        ins.then_inc(S["out_done"], 1)

                    for u in range(NU + 2):
                        if u < NU:
                            scores(u)
                        if u >= 1 and u - 1 < NU:
                            turn(u - 1)
                        if u >= 2:
                            values(u - 2)
                    for kv in range(2):
                        sample_scores(kv)
                    for kv in range(2):
                        turn(NU + kv)
                    for kv in range(2):
                        sample_values(kv)

                @block.vector
                def _(dve):
                    qv = qs[:].rearrange("p (b i t) -> p i b t", b=DEC_BATCH, i=4)
                    for i in range(4):
                        nc.vector.tensor_copy(qv[:, i], pr[:, SQ + i, SEQ:TOK].rearrange("p (b t) -> p b t", t=DEC_SEQ)
                                              ).then_inc(S["q_ready"], 1)

                    def row(k, u):
                        return small[:, k, u:u + 1]

                    def sink(u):
                        if u < NU:
                            h = units[u][1] + 4 * units[u][2]
                            return core.vec(VEC["sinks"] + h)
                        return core.vec(VEC["sink_rows"] + u - NU)

                    def soft(u):
                        n = keys(u)
                        dve.wait_ge(S["scored"], u + 1)
                        if u >= 2:
                            dve.wait_ge(S["exped"], u - 1)
                        m = mask[:, 2 * P - n:2 * P] if u < NU else mask_s[:]
                        nc.vector.scalar_tensor_tensor(logit[:, u % 2, 0:n], core.ps[:, u % 2, 0:n], scale, m,
                                                       ALU.mult, ALU.add).then_inc(S["masked"], 1)
                        dve.wait_ge(S["masked"], u + 1)
                        nc.vector.tensor_reduce(row(0, u), logit[:, u % 2, 0:n], AX_X, ALU.max).then_inc(S["maxed"], 1)
                        dve.wait_ge(S["maxed"], u + 1)
                        nc.vector.tensor_scalar(row(2, u), row(0, u), sink(u), -1.0, ALU.max, ALU.mult).then_inc(S["negated"], 1)

                    def divide(u):
                        n = keys(u)
                        dve.wait_ge(S["sink_exped"], u + 1)
                        nc.vector.tensor_tensor(row(5, u), row(3, u), row(4, u), ALU.add).then_inc(S["totalled"], 1)
                        dve.wait_ge(S["totalled"], u + 1)
                        nc.vector.reciprocal(row(6, u), row(5, u)).then_inc(S["inverted"], 1)
                        dve.wait_ge(S["inverted"], u + 1)
                        nc.vector.tensor_scalar(prob[:, u % 2, 0:n], prob[:, u % 2, 0:n], row(6, u), None, ALU.mult
                                                ).then_inc(S["scaled"], 1)

                    for u in range(NU):
                        soft(u)
                        if u >= 1:
                            divide(u - 1)
                    divide(NU - 1)
                    for kv in range(2):
                        dve.wait_ge(S["cached"], kv + 1)
                        nc.vector.tensor_copy(sT[:, kv], core.ps[:, 6 + kv, 0:P]).then_inc(S["sT_ready"], 1)
                    for kv in range(2):
                        soft(NU + kv)
                    for kv in range(2):
                        divide(NU + kv)
                    dve.wait_ge(S["high_ready"], 4)
                    nc.vector.tensor_tensor(core.h[1][:, 4:8], o_sb[:], core.h[0][:, 4:8].bitcast(F32), ALU.subtract)

                @block.scalar
                def _(act):
                    def row(k, u):
                        return small[:, k, u:u + 1]

                    def exps(u):
                        n = keys(u)
                        act.wait_ge(S["negated"], u + 1)
                        if u >= 2:
                            act.wait_ge(S["turned"], u - 1)
                        nc.scalar.activation(prob[:, u % 2, 0:n], logit[:, u % 2, 0:n], ACT.Exp, bias=row(2, u),
                                             accum_out=row(3, u)).then_inc(S["exped"], 1)
                        h = core.vec(VEC["sinks"] + units[u][1] + 4 * units[u][2]) if u < NU else \
                            core.vec(VEC["sink_rows"] + u - NU)
                        nc.scalar.activation(row(4, u), h, ACT.Exp, bias=row(2, u)).then_inc(S["sink_exped"], 1)

                    def turned_copy(u):
                        n = keys(u)
                        act.wait_ge(S["turned"], u + 1)
                        if u >= 2:
                            act.wait_ge(S["out_done"], u - 1)
                        if n == P + TS:
                            nc.scalar.activation(pT[:, u % 2, 0], core.ps[:, 2 + u % 2, 0:P], ACT.Copy)
                            nc.scalar.activation(pT[0:TS, u % 2, 1], core.ps[0:TS, 2 + u % 2, P:2 * P], ACT.Copy
                                                 ).then_inc(S["turn_copied"], 1)
                        else:
                            nc.scalar.activation(pT[:, u % 2, 0:n // P], core.ps[:, 2 + u % 2, 0:n].rearrange(
                                "p (t c) -> p t c", c=P), ACT.Copy).then_inc(S["turn_copied"], 1)

                    def out_copy(u):
                        b, i, _ = units[u]
                        act.wait_ge(S["out_done"], u + 1)
                        nc.scalar.activation(o_sb[:, i, b * P:(b + 1) * P], core.ps[:, 4 + (u // 2) % 2, 0:P], ACT.Copy
                                             ).then_inc(S["out_copied"], 1)

                    for u in range(NU + 2):
                        if u < NU:
                            exps(u)
                        if u >= 1 and u - 1 < NU:
                            turned_copy(u - 1)
                        if u >= 2 and u % 2 == 1:
                            out_copy(u - 2)
                    for kv in range(2):
                        exps(NU + kv)
                    for kv in range(2):
                        turned_copy(NU + kv)
                    act.wait_ge(S["out_done"], NU + 2)
                    ov = core.ps[:, 4, 0:P].rearrange("p (b i t) -> p i b t", b=DEC_BATCH, i=4)
                    for i in range(4):
                        nc.scalar.activation(o_sb[:, i, SEQ:TOK].rearrange("p (b t) -> p b t", t=DEC_SEQ), ov[:, i], ACT.Copy
                                             ).then_inc(S["out_copied"], 1)
                    act.wait_ge(S["out_copied"], NU // 2 + 4)
                    for i in range(4):
                        nc.scalar.activation(core.h[0][:, 4 + i], o_sb[:, i], ACT.Copy).then_inc(S["high_ready"], 1)


def odd_mixer(nc, core, a, out, after_in, after_out):
    with ExitStack() as ctx:
        pr = ctx.enter_context(nc.sbuf_tensor("odd_proj", [P, ODD_TILES, TOK], F32))
        core.z = ctx.enter_context(nc.sbuf_tensor("odd_z", [P, 4, TOK], F32))
        glu = core.pairs_of(a["s5_w_glu"])
        projection(nc, core, "odd_in", core.pairs_of(a["odd_w_in"]), ODD_TILES // 2, KT, core.h, TOK, "copy", pr,
                   after=(glu, 4), norm=of_x(core, VEC["mix_norm"] + KT), scaled=True)
        s5(nc, core, pr, a, out)
        z_parts = [core.h[0][:, 4:8], core.h[1][:, 4:8]]
        projection(nc, core, "odd_glu", glu, 2, 4, z_parts, TOK, "copy", pr, after=after_in)
        s5_gate(nc, core, pr)
        window_attention(nc, core, pr, a, out)
    projection(nc, core, "odd_out", core.pairs_of(a["odd_w_out"]), KT // 2, KT, core.h, TOK, "add", core.x,
               after=after_out)


def build(nc, a, out):
    with ExitStack() as ctx:
        def sb(name, shape, dt=F32):
            return ctx.enter_context(nc.sbuf_tensor(name, shape, dt))

        core = Core()
        core.nc, core.section_sems = nc, []
        core.ps = ctx.enter_context(nc.psum_tensor("ps", [P, 8, 512], F32))
        core.x = sb("x", [P, KT, TOK])
        core.h = [sb("h_high", [P, KT, TOK], F32R), sb("h_low", [P, KT, TOK], F32R)]
        core.raw = [sb(f"w_raw{s}", [P, max(HT, KT) * P]) for s in range(2)]
        core.high = [sb(f"w_high{s}", [P, max(HT, KT) * P], F32R) for s in range(2)]
        core.low = [sb(f"w_low{s}", [P, max(HT, KT) * P], F32R) for s in range(2)]
        core.mats = sb("mats", [P, 6, P])
        core.vectors = sb("vectors", [P, NVEC])
        core.mask_chunk = sb("mask_chunk", [P, 2 * P], I32)
        core.mask_dec = sb("mask_dec", [TS, 4 * TS], I32)
        resets = sb("resets", [P, 2, TOK])
        core.reset, core.reset_s5 = resets[:, 0], resets[:, 1]
        core.resets = resets
        core.eps = sb("eps", [P, 1])
        core.rstd = sb("rstd", [P, TOK])
        core.landed = [ctx.enter_context(nc.semaphore(f"w_landed{s}")) for s in range(2)]
        core.loads = [0, 0]

        def vec(i):
            return core.vectors[:, i:i + 1]

        def vecs(name):
            i = VEC[name]
            n = {"sinks": 8}.get(name, S5_TILES)
            return core.vectors[:, i:i + n]

        def pairs_of(w):
            w = w.rearrange("(i s) p c -> s i p c", s=2)
            return [w[0], w[1]]

        def ffn_weights(which, layer, half):
            rows = slice(half * HT, (half + 1) * HT)
            up = [a[f"ffn{which}_w_{n}"][layer, rows] for n in ("gate", "up")]
            return up, pairs_of(a[f"ffn{which}_w_down"][layer, half])

        core.vec, core.vecs, core.pairs_of, core.ffn_weights = vec, vecs, pairs_of, ffn_weights
        core.first = (ffn_weights(1, 0, 0)[0], KT)
        load_constants(nc, core, a)
        for layer in range(2):
            even = layer == 0
            kind = "even" if even else "odd"
            ffn(nc, core, 1, layer, (pairs_of(a[f"{kind}_w_in"]), KT))
            mixer = even_mixer if even else odd_mixer
            core.end_section()
            mixer(nc, core, a, out, (pairs_of(a[f"{kind}_w_out"]), KT), (pairs_of(a["mem_w_k"][layer]), KT))
            core.end_section()
            memory_attention(nc, core, a, out, layer, (ffn_weights(2, layer, 0)[0], KT))
            core.end_section()
            ffn(nc, core, 2, layer, (ffn_weights(1, 1, 0)[0], KT) if even else None)
        with nc.semaphore("y_stored") as stored, nc.Block("store_y") as block:
            @block.sync
            def _(sp):
                sp.dma_start(out["y"], core.x[:]).then_inc(stored, 16)
                sp.wait_ge(stored, 16)


def _constants(np):
    f = np.float32
    mats = np.zeros((P, 6, P), f)
    at = np.arange(P)
    mats[:, IDENT] = np.eye(P, dtype=f)
    mats[:, ONES] = 1.0
    mats[:, ONES64] = (at[:, None] // 64 == at[None, :] // 64)
    for i in range(0, P, 2):
        mats[i + 1, SWAP2, i] = -1.0
        mats[i, SWAP2, i + 1] = 1.0
    for h in range(0, P, 64):
        for d in range(8):
            mats[h + d + 8, SWAP8, h + d] = -1.0
            mats[h + d, SWAP8, h + d + 8] = 1.0
    for b in range(DEC_BATCH):
        mats[DEC_SEQ * b:DEC_SEQ * (b + 1), 5, b] = 1.0
    pos = np.concatenate([np.arange(SEQ), np.tile(PAST_LEN + np.arange(DEC_SEQ), DEC_BATCH)]).astype(f)
    step = np.concatenate([np.arange(SEQ) % CHUNK, np.tile(np.arange(DEC_SEQ), DEC_BATCH)])
    length = np.concatenate([np.full(SEQ, CHUNK), np.full(TS, DEC_SEQ)])
    s, t = at[:, None], at[None, :]
    chunk_mask = ((s // CHUNK == t // CHUNK) & (s <= t)).astype(np.int32)
    s, t = np.arange(TS)[:, None], np.arange(TS)[None, :]
    dec_mask = ((s // DEC_SEQ == t // DEC_SEQ) & (s <= t)).astype(np.int32)
    resets = np.ones((P, 2, TOK), f)
    resets[:, 0, step == 0] = 0.0
    resets[:, 1, SEQ::DEC_SEQ] = 0.0
    dk = 64
    log_decay = np.log(1.0 - 2.0 ** (-5.0 - np.arange(4, dtype=np.float64)))
    head = np.array([[2 * j + p // dk for j in range(2)] for p in range(P)])
    ld = log_decay[head][:, :, None]
    cum, end = ld * (step + 1), ld * length
    ret_decay = np.stack([np.exp(cum), np.exp(-cum), np.exp(end - cum)], 1).astype(f)
    chunks = np.array([CHUNK] * 8 + [DEC_SEQ] * 8)
    ret_last = np.exp(ld * chunks).astype(f).reshape(P, 32)
    inv = 1.0 / (10000.0 ** np.linspace(0.0, 1.0, dk // 2, dtype=f)).astype(f)
    ang = (pos[None, :] * inv[(at % dk) // 2][:, None]).astype(f).astype(np.float64)
    ret_rot = np.stack([np.cos(ang), np.sin(ang)], 1).astype(f)
    inv = (1.0 / (np.float64(500000.0) ** (np.arange(8) * 2.0 / 16))).astype(f)
    swa_rot = np.zeros((P, 2, TOK), f)
    swa_rot[:, 0] = 1.0
    for p in range(P):
        if p % 64 < 16:
            ang = (pos * inv[p % 8]).astype(f).astype(np.float64)
            swa_rot[p, 0], swa_rot[p, 1] = np.cos(ang), np.sin(ang)
    q, k = at[:, None], np.arange(-P, P)[None, :]
    swa_mask = np.where((k <= q) & (k > q - WIN), 0.0, NEG).astype(f)
    rb, rt = at // 16, at % DEC_SEQ
    old = np.where(at[None, :] > rt[:, None], 0.0, NEG)
    kb_, kt_ = np.arange(TS) // DEC_SEQ, np.arange(TS) % DEC_SEQ
    new = np.where((kb_[None, :] == rb[:, None]) & (kt_[None, :] <= rt[:, None]), 0.0, NEG)
    return dict(mats=mats, mask_chunk=np.tile(chunk_mask, (1, 2)), mask_dec=np.tile(dec_mask, (1, 4)), resets=resets,
                ret_decay=np.ascontiguousarray(ret_decay), ret_rot=ret_rot, swa_rot=swa_rot, swa_mask=swa_mask,
                swa_mask_s=np.concatenate([old, new], 1).astype(f), ret_last=ret_last,
                s5_steps=np.tile(np.concatenate([np.arange(CHUNK), CHUNK * np.arange(8)]).astype(f), (P, 1)))


def _chunks(w):
    k, m = w.shape
    return w.reshape(k // P, P, m // P, P).transpose(2, 1, 0, 3).reshape(m // P, P, k)


def _feature_major(x):
    t, d = x.shape
    return x.T.reshape(d // P, P, t).transpose(1, 0, 2)


def _layout(i, np):
    c = _constants(np)
    a = {n: c[n] for n in ("mats", "mask_chunk", "mask_dec", "resets", "ret_decay", "ret_rot", "swa_rot", "swa_mask",
                           "swa_mask_s", "s5_steps")}
    f = np.float32
    a["x"] = _feature_major(np.concatenate([i["x_prompt"].reshape(SEQ, D_MODEL), i["x_sample"].reshape(TS, D_MODEL)]))
    a["mem"] = _feature_major(i["mem_prompt"].reshape(N_MEM, D_MODEL))
    for n in ("1", "2"):
        for m in ("gate", "up"):
            a[f"ffn{n}_w_{m}"] = np.stack([_chunks(w) for w in i[f"ffn{n}_w_{m}"]])
        a[f"ffn{n}_w_down"] = np.stack([np.stack([_chunks(w[h * HT * P:(h + 1) * HT * P]) for h in range(2)])
                                        for w in i[f"ffn{n}_w_down"]])
    e = i["even_w_in"][0]
    rest = np.concatenate([e[:, 0:1536], e[:, 1552:3088], e[:, 1536:1552]], 1)
    wide = np.zeros((D_MODEL, EVEN_TILES * P), f)
    wide[:, 0:rest.shape[1]] = rest
    a["even_w_in"] = _chunks(wide)
    a["even_w_out"] = _chunks(i["even_w_out"][0])
    pair = np.concatenate([np.concatenate([np.arange(64) + 64 * h, np.arange(64) + 64 * (h + 4)]) for h in range(4)])
    o = i["odd_w_in"][0]
    a["odd_w_in"] = _chunks(np.concatenate([o[:, 0:512], o[:, 512:1024][:, pair], o[:, 1024:]], 1))
    o = i["odd_w_out"][0]
    a["odd_w_out"] = _chunks(np.concatenate([o[0:512], o[512:1024][pair]], 0))
    for n in "qkvo":
        a[f"mem_w_{n}"] = np.stack([_chunks(w) for w in i[f"mem_w_{n}"]])
    a["s5_w_glu"] = _chunks(i["s5_w_glu"][0])
    a["gla_w_gate"] = i["gla_w_gate"][0]

    def cols(w):
        return w.reshape(-1, P).T

    def tile_states(w):
        return w.reshape(S5_TILES, P).T
    v = np.zeros((P, NVEC), f)

    def put(name, w):
        v[:, VEC[name]:VEC[name] + w.shape[1]] = w
    for n in ("ffn1_norm", "ffn2_norm", "mix_norm", "mem_x_norm", "mem_m_norm", "mem_q_norm", "mem_k_norm"):
        put(n, cols(i[n]))
    put("gla_out_norm", cols(i["gla_out_norm"]))
    put("one", np.ones((P, 1), f))
    put("gla_b_gate", cols(i["gla_b_gate"]))
    put("swa_q_norm", np.tile(i["swa_q_norm"][0], 2)[:, None])
    put("swa_k_norm", np.tile(i["swa_k_norm"][0], 2)[:, None])
    put("s5_d", cols(i["s5_d"]))
    put("s5_b_glu", cols(i["s5_b_glu"]))
    put("sinks", np.tile(i["swa_sinks"][0], (P, 1)))
    put("sink_rows", np.stack([i["swa_sinks"][0][4 * kv + (np.arange(P) % 16) // 4] for kv in range(2)], 1))
    put("s5_a_re", tile_states(i["s5_a_re"][0]))
    put("s5_a_im", tile_states(i["s5_a_im"][0]))
    put("s5_log_step", tile_states(np.repeat(i["s5_log_step"][0], 64)))
    put("ret_last", c["ret_last"])
    a["vectors"] = v
    b = np.zeros((2, 64, 2, S5_TILES, 2, 16), f)
    ct = np.zeros((2, 64, 2, S5_TILES, 4, 2, 16), f)
    for ri, part in enumerate(("re", "im")):
        bw = i[f"s5_b_{part}"][0].reshape(S5_TILES, 2, 64, 16)
        cw = i[f"s5_c_{part}"][0].reshape(S5_TILES, 2, 16, 64)
        for g in range(2):
            b[g, :, ri, :, g, :] = bw[:, g].transpose(1, 0, 2)
            for j in range(S5_TILES):
                ct[g, :, ri, j, j % 4, g, :] = cw[j, g].T
    a["s5_b"] = b.reshape(P, 2, S5_TILES, 32)
    a["s5_c"] = ct.reshape(P, 2, S5_TILES, P)
    a["state_s5"] = np.stack([i[f"state_s5_{p}"][0].reshape(DEC_BATCH, S5_TILES, P).transpose(2, 1, 0)
                              for p in ("re", "im")], 1)
    for n in ("gla", "ret"):
        s = i[f"state_{n}"][0].reshape(DEC_BATCH, 2, P, P)
        a[f"state_{n}"] = s.transpose(1, 2, 0, 3)
    a["cache_swa_k"] = i["cache_swa_k"][0].reshape(DEC_BATCH, WIN, P).transpose(2, 0, 1)
    a["cache_swa_v"] = i["cache_swa_v"][0].reshape(DEC_BATCH, WIN, P).transpose(1, 0, 2)
    a["cache_mem_k"] = i["cache_mem_k"].reshape(2, DEC_BATCH, N_MEM, KT, P).transpose(0, 1, 4, 3, 2)
    a["cache_mem_v"] = i["cache_mem_v"].reshape(2, DEC_BATCH, 2, P, KT, P).transpose(0, 1, 3, 2, 4, 5)
    return {n: np.ascontiguousarray(x) for n, x in a.items()}


_OUTS = dict(y=(P, KT, TOK), p_gla=(P, 2, P), p_ret=(P, 2, P), s_gla=(2, P, DEC_BATCH, P), s_ret=(2, P, DEC_BATCH, P),
             s5=(P, 2, S5_TILES, DEC_BATCH + 1), p_swa_k=(P, WIN), p_swa_v=(WIN, P), s_swa_k=(P, DEC_BATCH, WIN),
             s_swa_v=(WIN, DEC_BATCH, P), p_mem_k=(2, P, KT, N_MEM), p_mem_v=(2, P, 2, KT, P))


def kernel(**inputs):
    import numpy as np
    import concourse.bacc as bacc
    from concourse.bass_utils import run_bass_kernel_spmd

    arrays = _layout({n: np.asarray(x) for n, x in inputs.items()}, np)
    nc = bacc.Bacc("TRN2", target_bir_lowering=False, num_devices=1)
    a = {n: nc.dram_tensor(f"in_{n}", x.shape, mybir.dt.from_np(x.dtype), kind="ExternalInput").ap()
         for n, x in arrays.items()}
    out = {n: nc.dram_tensor(f"out_{n}", shape, F32, kind="ExternalOutput").ap() for n, shape in _OUTS.items()}
    build(nc, a, out)
    r = run_bass_kernel_spmd(nc, [{f"in_{n}": x for n, x in arrays.items()}], core_ids=[0]).results[0]
    r = {n: r[f"out_{n}"] for n in _OUTS}
    y = r["y"].transpose(2, 1, 0).reshape(TOK, D_MODEL)
    s5 = r["s5"].transpose(1, 3, 2, 0).reshape(2, DEC_BATCH + 1, 32, 64)

    def p_state(x):
        return x.reshape(2, 64, 2, P).transpose(2, 0, 1, 3).reshape(1, 1, 4, 64, P)

    def s_state(x):
        return x.reshape(2, 2, 64, DEC_BATCH, P).transpose(3, 0, 1, 2, 4).reshape(1, DEC_BATCH, 4, 64, P)
    return (y[:SEQ].reshape(1, SEQ, D_MODEL), y[SEQ:].reshape(DEC_BATCH, DEC_SEQ, D_MODEL),
            p_state(r["p_gla"]), p_state(r["p_ret"]), s5[0, 0:1][None], s5[1, 0:1][None],
            r["p_swa_k"].T.reshape(1, 1, WIN, 2, 64), r["p_swa_v"].reshape(1, 1, WIN, 2, 64),
            r["p_mem_k"].transpose(0, 3, 2, 1).reshape(2, 1, N_MEM, MEM_HEADS, MEM_HD),
            r["p_mem_v"].transpose(0, 2, 1, 3, 4).reshape(2, 1, N_MEM, MEM_HEADS, MEM_HD),
            s_state(r["s_gla"]), s_state(r["s_ret"]), s5[0, 1:][None], s5[1, 1:][None],
            r["s_swa_k"].transpose(1, 2, 0).reshape(1, DEC_BATCH, WIN, 2, 64),
            r["s_swa_v"].transpose(1, 0, 2).reshape(1, DEC_BATCH, WIN, 2, 64))
```

```python
from contextlib import ExitStack

import concourse.bass as bass
from concourse import mybir

F32 = mybir.dt.float32
F32R = mybir.dt.float32r
I32 = mybir.dt.int32
ACT = mybir.ActivationFunctionType
ALU = mybir.AluOpType
AX_X = mybir.AxisListType.X

P = 128
D_MODEL = 1024
KT = D_MODEL // P
SEQ, DEC_BATCH, DEC_SEQ = 512, 8, 4
TS = DEC_BATCH * DEC_SEQ
TOK = SEQ + TS
PAST_LEN = 1024
FFN_HIDDEN = 2816
HT = FFN_HIDDEN // P // 2
N_MEM, MEM_HEADS, MEM_HD = 256, 4, 256
EPS = 1e-6
CHUNK = 64
S5_TILES = 16
WIN = 128
NEG = -1e30
TWO_PI = 6.283185307179586
MAGIC = 12582912.0
MAGIC13 = 1536.0
PI_SAFE = 3.1415925

GQ, GK, GV, GG, RQ, RK, RV, RG, GA = 0, 2, 4, 8, 12, 14, 16, 20, 24
EVEN_TILES = 26
SU, SQ, SK, SV = 0, 4, 8, 9
ODD_TILES = 10

IDENT, ONES, ONES64, SWAP2, SWAP8 = range(5)
VEC = {}
_at = 0
for _name, _n in (("ffn1_norm", 16), ("ffn2_norm", 16), ("mix_norm", 16), ("mem_x_norm", 16), ("mem_m_norm", 16),
                  ("mem_q_norm", 4), ("mem_k_norm", 4), ("gla_out_norm", 1), ("one", 1), ("gla_b_gate", 2),
                  ("swa_q_norm", 1), ("swa_k_norm", 1), ("s5_d", 4), ("s5_b_glu", 4), ("sinks", 8),
                  ("sink_rows", 2), ("s5_a_re", 16), ("s5_a_im", 16), ("s5_log_step", 16), ("ret_last", 32),
                  ("batch_rows", DEC_BATCH)):
    VEC[_name] = _at
    _at += _n
NVEC = _at


class Core:

    def sem(self, name):
        self.section_sems.append(self.nc.alloc_semaphore(name))
        return self.section_sems[-1]

    def end_section(self):
        self.nc.clear_and_free_semaphores(self.section_sems)
        self.section_sems = []
        self.nc.all_engine_barrier(sem_only=True)


def halves(n):
    return (2, n // 2) if n > 512 else (1, n)


def in_groups(ap, n):
    g, w = halves(n)
    return ap.rearrange("p (a c) -> p a c", c=w)


def first_chunks(core, sp, weights, kt):
    for s in range(2):
        sp.dma_start(core.raw[s][:, 0:kt * P], weights[s][0]).then_inc(core.landed[s], 16)


def high_part(nc, core, s, kt):
    return nc.scalar.activation(core.high[s][:, 0:kt * P], core.raw[s][:, 0:kt * P], ACT.Copy)


def low_part(nc, core, s, kt):
    return nc.vector.tensor_tensor(core.low[s][:, 0:kt * P], core.raw[s][:, 0:kt * P],
                                   core.high[s][:, 0:kt * P].bitcast(F32), ALU.subtract)


def projection(nc, core, name, weights, pairs, kt, src, cols, finish, dst, scale=1.0, after=None, norm=None, scaled=False):
    groups, width = halves(cols)
    base = list(core.loads)
    core.loads = [b + 16 * pairs for b in base]
    last_pair = pairs - 1

    def sem(what):
        return core.sem(f"{name}_{what}")

    with ExitStack() as ctx:
        def sb(what, shape, dt=F32):
            return ctx.enter_context(nc.sbuf_tensor(f"{name}_{what}", shape, dt))

        high_ready = sem("high_ready")
        low_ready = sem("low_ready")
        tile_done = sem("tile_done")
        psum_free = [sem("psum_free0"), sem("psum_free1")]
        rstd = core.rstd[:, 0:cols]
        if finish == "gate":
            gate_scaled = sem("gate_scaled")
            up_scaled = sem("up_scaled")
            gate_ready = sem("gate_ready")
            product_ready = sem("product_ready")
            hid_high = sem("hid_high")
            hid_ready = sem("hid_ready")
            sg, up, prod = sb("sg", [P, cols]), sb("up", [P, cols]), sb("prod", [P, cols])
        if norm:
            x_tiles, gain = norm
            x_high, x_ready = sem("x_high"), sem("x_ready")
            sq_act, sq_pool = sem("sq_act"), sem("sq_pool")
            added = sem("added")
            summed, log_ready, rstd_ready = sem("summed"), sem("log_ready"), sem("rstd_ready")
            sq = [sb("sq0", [P, 2, cols]), sb("sq1", [P, 2, cols])]
            total = sb("total", [P, cols])
            half_k = kt // 2
        acc = [core.ps[:, 2 * s:2 * s + groups, 0:width] for s in range(2)]
        sums = core.ps[:, 4:4 + groups, 0:width]

        with nc.Block(name) as block:
            @block.sync
            def _(sp):
                def load(s, source, size):
                    sp.dma_start(core.raw[s][:, 0:size * P], source).then_inc(core.landed[s], 16)

                load(0, weights[0][1], kt)
                if pairs > 2:
                    with sp.Fori(0, pairs - 2) as i:
                        sp.wait_ge(low_ready, i * 2 + 1)
                        load(1, weights[1][i + 1], kt)
                        sp.wait_ge(low_ready, i * 2 + 2)
                        load(0, weights[0][i + 2], kt)
                sp.wait_ge(low_ready, 2 * last_pair - 1)
                load(1, weights[1][last_pair], kt)
                if after is not None:
                    for s in range(2):
                        sp.wait_ge(low_ready, 2 * last_pair + s)
                        load(s, after[0][s][0], after[1])

            @block.gpsimd
            def _(pool):
                if norm:
                    for k in range(4):
                        if k >= 2:
                            pool.wait_ge(added, 2 * k - 3)
                        x = x_tiles[4 + k]
                        nc.gpsimd.tensor_tensor(sq[1][:, k % 2], x, x, ALU.mult).then_inc(sq_pool, 1)

            @block.scalar
            def _(act):
                def split_high(s, landed_at, done_at, size=kt):
                    act.wait_ge(core.landed[s], landed_at)
                    if done_at is not None:
                        act.wait_ge(tile_done, done_at)
                    high_part(nc, core, s, size).then_inc(high_ready, 1)

                def gate(i):
                    act.wait_ge(gate_scaled, i + 1)
                    nc.scalar.activation(sg[:], sg[:], ACT.Silu).then_inc(gate_ready, 1)

                if norm:
                    for k in range(kt):
                        nc.scalar.activation(src[0][:, k], x_tiles[k], ACT.Copy, scale=core.vec(gain + k)).then_inc(x_high, 1)
                        if k == 3:
                            split_high(1, base[1] + 16, None)
                    for k in range(4):
                        if k >= 2:
                            act.wait_ge(added, 2 * k - 3)
                        nc.scalar.activation(sq[0][:, k % 2], x_tiles[k], ACT.Square).then_inc(sq_act, 1)
                    act.wait_ge(summed, 1)
                    nc.scalar.activation(in_groups(rstd, cols), sums, ACT.Ln, bias=core.eps[:], scale=1.0 / D_MODEL
                                         ).then_inc(log_ready, 1)
                    act.wait_ge(log_ready, 1)
                    nc.scalar.activation(rstd, rstd, ACT.Exp, scale=-0.5).then_inc(rstd_ready, 1)
                else:
                    split_high(1, base[1] + 16, None)
                with act.Fori(0, last_pair) as i:
                    split_high(0, i * 16 + (base[0] + 16), i * 2 + 1)
                    if finish == "gate":
                        gate(i)
                    split_high(1, i * 16 + (base[1] + 32), i * 2 + 2)
                if after is not None:
                    split_high(0, base[0] + 16 * pairs, 2 * last_pair + 1, after[1])
                if finish == "gate":
                    gate(last_pair)

            @block.vector
            def _(dve):
                def split_low(s, high_at, size=kt):
                    dve.wait_ge(high_ready, high_at)
                    low_part(nc, core, s, size).then_inc(low_ready, 1)

                def finish_tile(s, i):
                    dve.wait_ge(tile_done, i * 2 + (s + 1))
                    if finish == "gate":
                        to = (sg, up)[s]
                        nc.vector.tensor_tensor(in_groups(to[:], cols), acc[s], in_groups(rstd, cols), ALU.mult
                                                ).then_inc((gate_scaled, up_scaled)[s], 1)
                        if s == 0:
                            return
                        dve.wait_ge(up_scaled, i + 1)
                        dve.wait_ge(gate_ready, i + 1)
                        nc.vector.tensor_tensor(prod[:], sg[:], up[:], ALU.mult).then_inc(product_ready, 1)
                        dve.wait_ge(product_ready, i + 1)
                        high = dst[0][:, bass.ds(i, 1), :].rearrange("p o c -> p (o c)")
                        low = dst[1][:, bass.ds(i, 1), :].rearrange("p o c -> p (o c)")
                        nc.vector.tensor_scalar(high, prod[:], 1.0, None, ALU.mult).then_inc(hid_high, 1)
                        dve.wait_ge(hid_high, i + 1)
                        nc.vector.tensor_tensor(low, prod[:], high.bitcast(F32), ALU.subtract).then_inc(hid_ready, 1)
                        return
                    out = dst[:, bass.ds(i * 2 + s, 1), :].rearrange("p o (a c) -> p (o a) c", c=width)
                    if finish == "add":
                        ins = nc.vector.scalar_tensor_tensor(out, acc[s], scale, out, ALU.mult, ALU.add)
                    elif scaled:
                        ins = nc.vector.tensor_tensor(out, acc[s], in_groups(rstd, cols), ALU.mult)
                    else:
                        ins = nc.vector.tensor_scalar(out, acc[s], scale, None, ALU.mult)
                    ins.then_inc(psum_free[s], 1)

                if norm:
                    for k in range(kt):
                        dve.wait_ge(x_high, k + 1)
                        nc.vector.scalar_tensor_tensor(src[1][:, k], x_tiles[k], core.vec(gain + k),
                                                       src[0][:, k].bitcast(F32), ALU.mult, ALU.subtract).then_inc(x_ready, 1)
                        if k == 4:
                            split_low(1, 1)
                    for n in range(1, 8):
                        e, k = n % 2, n // 2
                        if n == 1:
                            dve.wait_ge(sq_act, 1)
                        dve.wait_ge((sq_act, sq_pool)[e], k + 1)
                        if n > 1:
                            dve.wait_ge(added, n - 1)
                        first = sq[0][:, 0] if n == 1 else total[:]
                        nc.vector.tensor_tensor(total[:], first, sq[e][:, k % 2], ALU.add).then_inc(added, 1)
                    dve.wait_ge(rstd_ready, 1)
                else:
                    split_low(1, 1)
                with dve.Fori(0, last_pair) as i:
                    for s in range(2):
                        split_low(s, i * 2 + (s + 2))
                        finish_tile(s, i)
                if after is not None:
                    split_low(0, 2 * pairs, after[1])
                for s in range(2):
                    finish_tile(s, last_pair)

            @block.tensor
            def _(pe):
                def tile(s, i, first=False):
                    if not (first and s == 0):
                        pe.wait_ge(low_ready, i * 2 + s)
                    if not first:
                        if finish == "gate":
                            pe.wait_ge((gate_scaled, up_scaled)[s], i)
                        else:
                            pe.wait_ge(psum_free[s], i)
                    for k in range(kt):
                        if norm and first and s == 0:
                            pe.wait_ge(x_ready, k + 1)
                        if norm and first and s == 1 and k == half_k:
                            pe.wait_ge(added, 7)
                            for a in range(groups):
                                ins = nc.tensor.matmul(sums[:, a, :], core.mats[:, ONES],
                                                       total[:, a * width:(a + 1) * width], start=True, stop=True)
                            ins.then_inc(summed, 1)
                        w_high = core.high[s][:, k * P:(k + 1) * P]
                        w_low = core.low[s][:, k * P:(k + 1) * P]
                        passes = ((w_high, src[0]), (w_high, src[1]), (w_low, src[0]))
                        for n, (w, x) in enumerate(passes):
                            for a in range(groups):
                                last = nc.tensor.matmul(acc[s][:, a, :], w, x[:, k, a * width:(a + 1) * width],
                                                        start=(k == 0 and n == 0), stop=(k == kt - 1 and n == 2))
                    last.then_inc(tile_done, 1)

                for s in range(2):
                    tile(s, 0, True)
                with pe.Fori(1, pairs) as i:
                    for s in range(2):
                        tile(s, i)


def rms_norm(nc, core, name, groups, ones, count, cols):
    g_n, width = halves(cols)
    tiles = [(g, t) for g, group in enumerate(groups) for t in range(len(group["x"]))]
    last_of = [sum(len(x["x"]) for x in groups[:g + 1]) for g in range(len(groups))]
    times = "times" in groups[0]
    split = "split" in groups[0]
    with ExitStack() as ctx:
        def sem(what):
            return core.sem(f"{name}_{what}")

        squared, summed, log_ready, rstd_ready = sem("squared"), sem("summed"), sem("log_ready"), sem("rstd_ready")
        normed, timed, high_ready, done = sem("normed"), sem("timed"), sem("high_ready"), sem("done")
        sq = ctx.enter_context(nc.sbuf_tensor(f"{name}_sq", [P, 2, cols], F32))
        val = ctx.enter_context(nc.sbuf_tensor(f"{name}_val", [P, 2, cols], F32)) if split else None

        batch = 8 // g_n
        batches = [range(g, min(g + batch, len(groups))) for g in range(0, len(groups), batch)]

        def total(g):
            b = g_n * (g % batch)
            return core.ps[:, b:b + g_n, 0:width]

        def value(n, group, t):
            return val[:, n % 2] if split else group["out"][t]

        with nc.Block(name) as block:
            @block.scalar
            def _(act):
                def squares(g):
                    for n, (gg, t) in enumerate(tiles):
                        if gg != g:
                            continue
                        if n >= 2:
                            act.wait_ge(summed, n - 1)
                        nc.scalar.activation(sq[:, n % 2], groups[g]["x"][t], ACT.Square).then_inc(squared, 1)

                def scales(gs):
                    for g in gs:
                        act.wait_ge(summed, last_of[g])
                        nc.scalar.activation(total(g), total(g), ACT.Ln, bias=core.eps[:], scale=1.0 / count
                                             ).then_inc(log_ready, 1)
                    for g in gs:
                        act.wait_ge(log_ready, g + 1)
                        nc.scalar.activation(total(g), total(g), ACT.Exp, scale=-0.5).then_inc(rstd_ready, 1)

                def highs(g):
                    for n, (gg, t) in enumerate(tiles):
                        if gg == g:
                            act.wait_ge(timed if times else normed, n + 1)
                            nc.scalar.activation(groups[g]["split"][t][0], value(n, groups[g], t),
                                                 ACT.Copy).then_inc(high_ready, 1)

                for gs in batches:
                    for g in gs:
                        if split and g >= batch:
                            highs(g - batch)
                        squares(g)
                    scales(gs)
                if split:
                    for g in range(max(0, batches[-1][-1] + 1 - batch), len(groups)):
                        highs(g)

            @block.tensor
            def _(pe):
                for n, (g, t) in enumerate(tiles):
                    pe.wait_ge(squared, n + 1)
                    if t == 0 and g >= batch:
                        pe.wait_ge(normed if split else done, last_of[g - batch])
                    for a in range(g_n):
                        last = nc.tensor.matmul(total(g)[:, a, :], ones, sq[:, n % 2, a * width:(a + 1) * width],
                                                start=(t == 0), stop=(t == len(groups[g]["x"]) - 1))
                    last.then_inc(summed, 1)

            @block.vector
            def _(dve):
                def low(n):
                    g, t = tiles[n]
                    dve.wait_ge(high_ready, n + 1)
                    high, low_out = groups[g]["split"][t]
                    nc.vector.tensor_tensor(low_out, value(n, groups[g], t), high.bitcast(F32),
                                            ALU.subtract).then_inc(done, 1)

                for n, (g, t) in enumerate(tiles):
                    group = groups[g]
                    if split and n >= 2:
                        low(n - 2)
                        dve.wait_ge(done, n - 1)
                    if t == 0:
                        dve.wait_ge(rstd_ready, g + 1)
                    ins = nc.vector.scalar_tensor_tensor(in_groups(value(n, group, t), cols), in_groups(group["x"][t], cols),
                                                         group["gain"][t], total(g), ALU.mult, ALU.mult)
                    ins.then_inc(normed if split else done, 1)
                    if times:
                        dve.wait_ge(normed, n + 1)
                        nc.vector.tensor_tensor(value(n, group, t), value(n, group, t), group["times"][t],
                                                ALU.mult).then_inc(timed, 1)
                if split:
                    for n in range(max(0, len(tiles) - 2), len(tiles)):
                        low(n)


def of_x(core, gain):
    return [core.x[:, k] for k in range(KT)], gain


def load_constants(nc, core, a):
    landed, high_ready = core.sem("constants_landed"), core.sem("first_high")
    with nc.Block("constants") as block:
        @block.sync
        def _(sp):
            loads = [(core.x[:], a["x"]), (core.mats[:], a["mats"]), (core.vectors[:], a["vectors"]),
                     (core.mask_chunk[:], a["mask_chunk"]), (core.mask_dec[:], a["mask_dec"]),
                     (core.resets[:], a["resets"])]
            for dst, src in loads:
                sp.dma_start(dst, src).then_inc(landed, 16)
            first_chunks(core, sp, *core.first)
            sp.wait_ge(landed, 16 * len(loads))

        @block.scalar
        def _(act):
            act.wait_ge(core.landed[0], 16)
            high_part(nc, core, 0, core.first[1]).then_inc(high_ready, 1)

        @block.vector
        def _(dve):
            nc.vector.memset(core.eps[:], EPS)
            dve.wait_ge(high_ready, 1)
            low_part(nc, core, 0, core.first[1])
    core.loads = [16, 0]


def ffn(nc, core, which, layer, after):
    name = f"ffn{which}_{layer}"
    with ExitStack() as ctx:
        hid = [ctx.enter_context(nc.sbuf_tensor(f"{name}_hid{s}", [P, HT, TOK], F32R)) for s in range(2)]
        for half in range(2):
            gate_up, down = core.ffn_weights(which, layer, half)
            nxt = (core.ffn_weights(which, layer, 1)[0], KT) if half == 0 else after
            norm = of_x(core, VEC[f"ffn{which}_norm"] + KT * layer) if half == 0 else None
            projection(nc, core, f"{name}_up{half}", gate_up, HT, KT, core.h, TOK, "gate", hid, after=(down, HT),
                       norm=norm, scaled=True)
            projection(nc, core, f"{name}_down{half}", down, KT // 2, HT, hid, TOK, "add", core.x, scale=0.5,
                       after=nxt)


def even_mixer(nc, core, a, out, after_in, after_out):
    qt, kt_, vt, gt = (GQ, GQ + 1, RQ, RQ + 1), (GK, GK + 1, RK, RK + 1), (GV, RV), (GG, RG)
    NB = SEQ // P
    with ExitStack() as ctx:
        pr = ctx.enter_context(nc.sbuf_tensor("even_proj", [P, EVEN_TILES, TOK], F32))
        projection(nc, core, "even_in", core.pairs_of(a["even_w_in"]), EVEN_TILES // 2, KT, core.h, TOK, "copy", pr,
                   after=after_in, norm=of_x(core, VEC["mix_norm"]), scaled=True)
        held = ctx.enter_context(ExitStack())

        def sb(what, shape, dt=F32):
            return held.enter_context(nc.sbuf_tensor(f"even_{what}", shape, dt))

        ki = sb("k_inv", [P, 4, TOK])
        last = sb("decay_last", [P, 4, 16])
        q_tiles = [pr[:, t] for t in qt]
        k_tiles = [pr[:, t] for t in kt_]

        with ExitStack() as c2:
            def sb2(what, shape, dt=F32):
                return c2.enter_context(nc.sbuf_tensor(f"even_{what}", shape, dt))

            def sem(what):
                return core.sem(f"evend_{what}")

            decay = sb2("decay", [P, 3, 4, TOK])
            rot = sb2("rot", [P, 2, TOK])
            wg = sb2("wg", [16, 256])
            za, zb, cum = sb2("za", [P, TOK]), sb2("zb", [P, TOK]), sb2("cum", [P, TOK])
            tables, gate_done, swapped = sem("tables"), sem("gate_done"), sem("swapped")
            dve_steps, act_steps, cos_done = sem("dve_steps"), sem("act_steps"), sem("cos_done")
            rotated = sem("rotated")
            with nc.Block("even_decay") as block:
                @block.sync
                def _(sp):
                    sp.dma_start(decay[:, :, 2:4], a["ret_decay"]).then_inc(tables, 16)
                    sp.dma_start(rot[:], a["ret_rot"]).then_inc(tables, 16)
                    sp.dma_start(wg[:], a["gla_w_gate"]).then_inc(tables, 16)

                @block.tensor
                def _(pe):
                    pe.wait_ge(tables, 48)
                    for j in range(2):
                        for g in range(2):
                            ins = nc.tensor.matmul(core.ps[:, 2 * j + g, 0:272], wg[:, j * P:(j + 1) * P],
                                                   pr[0:16, GA, g * 272:(g + 1) * 272], start=True, stop=True)
                        ins.then_inc(gate_done, 1)
                    for n, t in enumerate((RQ, RQ + 1, RK, RK + 1)):
                        b = 4 + 2 * (n % 2)
                        if n >= 2:
                            pe.wait_ge(rotated, n - 1)
                        for g in range(2):
                            ins = nc.tensor.matmul(core.ps[:, b + g, 0:272], core.mats[:, SWAP2],
                                                   pr[:, t, g * 272:(g + 1) * 272], start=True, stop=True)
                        ins.then_inc(swapped, 1)

                @block.scalar
                def _(act):
                    n = 0

                    def step(ins):
                        nonlocal n
                        n += 1
                        ins.then_inc(act_steps, 1)
                        act.wait_ge(act_steps, n)
                    for j in range(2):
                        act.wait_ge(dve_steps, 5 * j + 1)
                        step(nc.scalar.activation(zb[:], za[:], ACT.Abs))
                        step(nc.scalar.activation(zb[:], zb[:], ACT.Exp, scale=-1.0))
                        step(nc.scalar.activation(zb[:], zb[:], ACT.Ln, bias=1.0))
                        act.wait_ge(dve_steps, 5 * j + 5)
                        step(nc.scalar.activation(decay[:, 0, j], cum[:], ACT.Exp, scale=1.0 / 16))
                        step(nc.scalar.activation(decay[:, 1, j], cum[:], ACT.Exp, scale=-1.0 / 16))
                        step(nc.scalar.activation(decay[:, 2, j], zb[:], ACT.Exp, scale=1.0 / 16))
                        step(nc.scalar.activation(last[:, j, 0:8], cum[:, CHUNK - 1:SEQ:CHUNK], ACT.Exp, scale=1.0 / 16))
                        step(nc.scalar.activation(last[:, j, 8:16], cum[:, SEQ + 3:TOK:4], ACT.Exp, scale=1.0 / 16))

                @block.gpsimd
                def _(pool):
                    pool.wait_ge(tables, 48)
                    for n, t in enumerate((RQ, RQ + 1, RK, RK + 1)):
                        pool.wait_ge(swapped, n + 1)
                        nc.gpsimd.tensor_tensor(pr[:, t], pr[:, t], rot[:, 0], ALU.mult).then_inc(cos_done, 1)

                @block.vector
                def _(dve):
                    n = 0

                    def step(ins):
                        nonlocal n
                        n += 1
                        ins.then_inc(dve_steps, 1)
                        dve.wait_ge(dve_steps, n)
                    for j in range(2):
                        dve.wait_ge(gate_done, j + 1)
                        if j:
                            dve.wait_ge(act_steps, 8 * j)
                        step(nc.vector.tensor_scalar(in_groups(za[:], TOK), core.ps[:, 2 * j:2 * j + 2, 0:272],
                                                     core.vec(VEC["gla_b_gate"] + j), None, ALU.add))
                        dve.wait_ge(act_steps, 8 * j + 3)
                        step(nc.vector.scalar_tensor_tensor(za[:], za[:], 0.0, zb[:], ALU.min, ALU.subtract))
                        step(nc.vector.tensor_tensor_scan(cum[:], core.reset[:], za[:], 0.0, ALU.mult, ALU.add))
                        for lo, hi, w in ((0, SEQ, CHUNK), (SEQ, TOK, DEC_SEQ)):
                            c3 = cum[:, lo:hi].rearrange("p (c t) -> p c t", t=w)
                            end = c3[:, :, w - 1:w].to_broadcast([P, (hi - lo) // w, w])
                            z3 = zb[:, lo:hi].rearrange("p (c t) -> p c t", t=w)
                            step(nc.vector.tensor_tensor(z3, end, c3, ALU.subtract))
                    dve.wait_ge(tables, 48)
                    m = 0
                    for n2, t in enumerate((RQ, RQ + 1, RK, RK + 1)):
                        b = 4 + 2 * (n2 % 2)
                        dve.wait_ge(swapped, n2 + 1)
                        step(nc.vector.tensor_tensor(in_groups(za[:], TOK), core.ps[:, b:b + 2, 0:272],
                                                     in_groups(rot[:, 1], TOK), ALU.mult))
                        dve.wait_ge(cos_done, n2 + 1)
                        nc.vector.tensor_tensor(pr[:, t], pr[:, t], za[:], ALU.add).then_inc(rotated, 1)
                        dve.wait_ge(rotated, n2 + 1)
                    step(nc.vector.tensor_copy(last[:, 2:4, :].rearrange("p a b -> p (a b)"),
                                               core.vectors[:, VEC["ret_last"]:VEC["ret_last"] + 32]))
                    dve.wait_ge(act_steps, 16)
                    for j in range(4):
                        qs, ks = (0.125, 1.0) if j < 2 else (1.0, 0.125)
                        step(nc.vector.scalar_tensor_tensor(q_tiles[j], q_tiles[j], qs, decay[:, 0, j], ALU.mult, ALU.mult))
                        step(nc.vector.scalar_tensor_tensor(ki[:, j], k_tiles[j], ks, decay[:, 1, j], ALU.mult, ALU.mult))
                        step(nc.vector.scalar_tensor_tensor(k_tiles[j], k_tiles[j], ks, decay[:, 2, j], ALU.mult, ALU.mult))

        v_tok = sb("v_tok", [P, NB + 1, 8, P])
        kd_tok = sb("kd_tok", [P, NB + 1, 4, P])
        v_tiles = [pr[:, vt[h // 4] + h % 4] for h in range(8)]
        transposes(nc, core, "even_t", [(v_tiles[0:4], v_tok, 0), (v_tiles[4:8], v_tok, 4), (k_tiles, kd_tok, 0)])

        s_in = sb("s_in", [P, DEC_BATCH, 4, P])
        st = [pr[:, t:t + 2].rearrange("p a c -> p (a c)")[:, 0:3 * 2 * P].rearrange("p (s j c) -> p s j c", s=3, j=2)
              for t in (GK, RK)]
        sc = pr[:, GA, 0:4 * P].rearrange("p (u h c) -> p u h c", u=2, h=2)
        o_tiles = [pr[:, t:t + 4] for t in vt]
        units = [(tt, j) for tt in range(NB) for j in range(4)]
        with ExitStack() as c2:
            def sem(what):
                return core.sem(f"evenr_{what}")

            scored, masked, updated, stated = sem("scored"), sem("masked"), sem("updated"), sem("stated")
            out_done, out_copied, state_in = sem("out_done"), sem("out_copied"), sem("state_in")
            chained, stored, zeroed = sem("chained"), sem("stored"), sem("zeroed")
            with nc.Block("even_recur") as block:
                @block.sync
                def _(sp):
                    for j in range(2):
                        sp.dma_start(s_in[:, :, j, :], a["state_gla"][j]).then_inc(state_in, 16)
                        sp.dma_start(s_in[:, :, 2 + j, :], a["state_ret"][j]).then_inc(state_in, 16)
                    sp.wait_ge(stated, len(units))
                    sp.dma_start(out["p_gla"], st[0][:, 2]).then_inc(stored, 16)
                    sp.dma_start(out["p_ret"], st[1][:, 2]).then_inc(stored, 16)
                    sp.wait_ge(state_in, 64)
                    sp.wait_ge(stored, 32)

                @block.tensor
                def _(pe):
                    def first(u):
                        tt, j = units[u]
                        c = slice(tt * P, (tt + 1) * P)
                        if u >= 2:
                            pe.wait_ge(masked, u - 1)
                        for hh in range(2):
                            r = slice(64 * hh, 64 * hh + 64)
                            ins = nc.tensor.matmul(core.ps[:, 2 * (u % 2) + hh, 0:P], ki[r, j, c],
                                                   q_tiles[j][r, c], start=True, stop=True)
                        ins.then_inc(scored, 1)

                    def updates(u):
                        tt, j = units[u]
                        if u >= 1:
                            pe.wait_ge(stated, u)
                        for half in range(2):
                            s = slice(64 * half, 64 * half + 64)
                            for hh in range(2):
                                ins = nc.tensor.matmul(core.ps[64 * hh:64 * hh + 64, 4 + half, 0:P],
                                                       kd_tok[s, tt, j, 64 * hh:64 * hh + 64],
                                                       v_tok[s, tt, 2 * j + hh, :], start=True, stop=True)
                        ins.then_inc(updated, 1)

                    def second(u):
                        tt, j = units[u]
                        pe.wait_ge(masked, u + 1)
                        pe.wait_ge(chained, u + 1)
                        if u >= 1:
                            pe.wait_ge(out_copied, u)
                        for hh in range(2):
                            r = slice(64 * hh, 64 * hh + 64)
                            o = core.ps[:, 6 + hh, 0:P]
                            nc.tensor.matmul(o, v_tok[:, tt, 2 * j + hh, :], sc[:, u % 2, hh, :], start=True, stop=False)
                            for half in range(2):
                                ch = 2 * tt + half
                                if ch == 0:
                                    continue
                                ins = nc.tensor.matmul(o[:, 64 * half:64 * half + 64], st[j // 2][r, ch % 3, j % 2, :],
                                                       q_tiles[j][r, ch * CHUNK:(ch + 1) * CHUNK],
                                                       start=False, stop=(half == 1))
                        ins.then_inc(out_done, 1)

                    for u in range(len(units) + 1):
                        if u < len(units):
                            first(u)
                        if u >= 1:
                            second(u - 1)
                        if u < len(units):
                            updates(u)

                @block.scalar
                def _(act):
                    for u, (tt, j) in enumerate(units):
                        act.wait_ge(out_done, u + 1)
                        dst = o_tiles[j // 2][:, 2 * (j % 2):2 * (j % 2) + 2, tt * P:(tt + 1) * P]
                        nc.scalar.activation(dst, core.ps[:, 6:8, 0:P], ACT.Copy).then_inc(out_copied, 1)

                @block.vector
                def _(dve):
                    nc.vector.memset(sc, 0.0).then_inc(zeroed, 1)
                    dve.wait_ge(zeroed, 1)
                    for u, (tt, j) in enumerate(units):
                        dve.wait_ge(scored, u + 1)
                        if u >= 2:
                            dve.wait_ge(out_done, u - 1)
                        nc.vector.copy_predicated(sc[:, u % 2], core.mask_chunk[:].rearrange("p (h c) -> p h c", h=2),
                                                  core.ps[:, 2 * (u % 2):2 * (u % 2) + 2, 0:P]).then_inc(masked, 1)
                        dve.wait_ge(updated, u + 1)
                        for half in range(2):
                            ch = 2 * tt + half
                            new = st[j // 2][:, (ch + 1) % 3, j % 2, :]
                            add = core.ps[:, 4 + half, 0:P]
                            if ch >= 2:
                                dve.wait_ge(out_done, u - 4 + 1)
                            if half:
                                dve.wait_ge(chained, u + 1)
                            elif ch >= 2:
                                dve.wait_ge(stated, u - 3)
                            if ch == 0:
                                ins = nc.vector.tensor_copy(new, add)
                            else:
                                ins = nc.vector.scalar_tensor_tensor(new, st[j // 2][:, ch % 3, j % 2, :], last[:, j, ch:ch + 1], add,
                                                                     ALU.mult, ALU.add)
                            ins.then_inc(stated if half else chained, 1)

        kd_b = pr[0:TS, GK:GK + 2].rearrange("p a c -> p (a c)")[:, 0:8 * P].rearrange("p (u c) -> p u c", u=2)
        sc_s = pr[0:TS, GA + 1, 0:8 * TS].rearrange("p (h c) -> p h c", h=8)
        with ExitStack() as c2:
            def sem(what):
                return core.sem(f"evens_{what}")

            zeroed, scored, masked, out_done = sem("zeroed"), sem("scored"), sem("masked"), sem("out_done")
            picked, updated, stated, copied, stored = (sem("picked"), sem("updated"), sem("stated"), sem("copied"),
                                                       sem("stored"))
            with nc.Block("even_sample") as block:
                @block.tensor
                def _(pe):
                    for h in range(8):
                        r, j = slice(64 * (h % 2), 64 * (h % 2) + 64), h // 2
                        ins = nc.tensor.matmul(core.ps[0:TS, h % 2, j * TS:(j + 1) * TS], ki[r, j, SEQ:TOK],
                                               q_tiles[j][r, SEQ:TOK], start=True, stop=True)
                    ins.then_inc(scored, 1)
                    pe.wait_ge(masked, 2)
                    for h in range(8):
                        r, j = slice(64 * (h % 2), 64 * (h % 2) + 64), h // 2
                        o = core.ps[:, 2 + h % 2, j * TS:(j + 1) * TS]
                        nc.tensor.matmul(o, v_tok[0:TS, NB, h, :], sc_s[:, h, :], start=True, stop=False)
                        for b in range(DEC_BATCH):
                            c = slice(DEC_SEQ * b, DEC_SEQ * (b + 1))
                            ins = nc.tensor.matmul(o[:, c], s_in[r, b, j, :],
                                                   q_tiles[j][r, SEQ + DEC_SEQ * b:SEQ + DEC_SEQ * (b + 1)],
                                                   start=False, stop=(b == DEC_BATCH - 1))
                    ins.then_inc(out_done, 1)
                    for b in range(DEC_BATCH):
                        pe.wait_ge(picked, b + 1)
                        if b >= 2:
                            pe.wait_ge(stated, 4 * (b - 1))
                        for h in range(8):
                            ins = nc.tensor.matmul(core.ps[64 * (h % 2):64 * (h % 2) + 64, 4 + b % 2,
                                                           (h // 2) * P:(h // 2 + 1) * P],
                                                   kd_b[:, b % 2, h * 64:(h + 1) * 64], v_tok[0:TS, NB, h, :],
                                                   start=True, stop=True)
                        ins.then_inc(updated, 1)

                @block.scalar
                def _(act):
                    act.wait_ge(out_done, 1)
                    for g in range(2):
                        for hh in range(2):
                            nc.scalar.activation(o_tiles[g][:, hh:4:2, SEQ:TOK],
                                                 core.ps[:, 2 + hh, 2 * g * TS:2 * (g + 1) * TS].rearrange(
                                                     "p (j c) -> p j c", j=2), ACT.Copy).then_inc(copied, 1)

                @block.vector
                def _(dve):
                    nc.vector.memset(sc_s, 0.0).then_inc(zeroed, 1)
                    dve.wait_ge(zeroed, 1)
                    dve.wait_ge(scored, 1)
                    for hh in range(2):
                        nc.vector.copy_predicated(sc_s[:, hh:8:2], core.mask_dec[:].rearrange("p (j c) -> p j c", j=4),
                                                  core.ps[0:TS, hh, 0:4 * TS].rearrange("p (j c) -> p j c", j=4)
                                                  ).then_inc(masked, 1)
                    for b in range(DEC_BATCH + 1):
                        if b < DEC_BATCH:
                            if b >= 2:
                                dve.wait_ge(updated, b - 1)
                            nc.vector.tensor_scalar(kd_b[:, b % 2, :], kd_tok[0:TS, NB].rearrange("p a b -> p (a b)"),
                                                    core.vectors[0:TS, VEC["batch_rows"] + b:VEC["batch_rows"] + b + 1], None, ALU.mult).then_inc(picked, 1)
                        if b >= 1:
                            dve.wait_ge(updated, b)
                            dve.wait_ge(out_done, 1)
                            for j in range(4):
                                s = s_in[:, b - 1, j, :]
                                nc.vector.scalar_tensor_tensor(s, s, last[:, j, 8 + b - 1:8 + b],
                                                               core.ps[:, 4 + (b - 1) % 2, j * P:(j + 1) * P],
                                                               ALU.mult, ALU.add).then_inc(stated, 1)

                @block.sync
                def _(sp):
                    sp.wait_ge(stated, 4 * DEC_BATCH)
                    for j in range(2):
                        sp.dma_start(out["s_gla"][j], s_in[:, :, j, :]).then_inc(stored, 16)
                        sp.dma_start(out["s_ret"][j], s_in[:, :, 2 + j, :]).then_inc(stored, 16)
                    sp.wait_ge(stored, 64)

        held.close()
        with nc.Block("even_gates") as block:
            @block.scalar
            def _(act):
                for g in gt:
                    for t in range(4):
                        nc.scalar.activation(pr[:, g + t], pr[:, g + t], ACT.Silu)
        rms_norm(nc, core, "even_on", [dict(
            x=[o_tiles[h // 4][:, h % 4]], gain=[core.vec(VEC["gla_out_norm"] if h < 4 else VEC["one"])],
            split=[(core.h[0][:, h], core.h[1][:, h])], times=[pr[:, gt[h // 4] + h % 4]]) for h in range(8)],
            core.mats[:, ONES], P, TOK)
    projection(nc, core, "even_out", core.pairs_of(a["even_w_out"]), KT // 2, KT, core.h, TOK, "add", core.x,
               after=after_out)


def transposes(nc, core, name, jobs, blocks=None):
    blocks = blocks or [(b * P, P) for b in range(SEQ // P)] + [(SEQ, TS)]
    work = [(lo, w, n, job) for n, (lo, w) in enumerate(blocks) for job in jobs]
    with ExitStack() as ctx:
        turned = core.sem(f"{name}_turned")
        copied = [core.sem(f"{name}_copied{e}") for e in range(2)]
        with nc.Block(name) as block:
            @block.tensor
            def _(pe):
                for u, (lo, w, n, (tiles, dst, at)) in enumerate(work):
                    if u >= 4:
                        pe.wait_ge(copied[u % 2], (u - 4) // 2 + 1)
                    for t, tile in enumerate(tiles):
                        ins = nc.tensor.transpose(core.ps[0:w, u % 4, t * P:(t + 1) * P], tile[:, lo:lo + w],
                                                  core.mats[:, IDENT])
                    ins.then_inc(turned, 1)

            def copies(eng, which, copy):
                for u, (lo, w, n, (tiles, dst, at)) in enumerate(work):
                    if u % 2 == which:
                        eng.wait_ge(turned, u + 1)
                        src = core.ps[0:w, u % 4, 0:len(tiles) * P].rearrange("p (h c) -> p h c", c=P)
                        copy(dst[0:w, n, at:at + len(tiles), :], src).then_inc(copied[which], 1)

            @block.scalar
            def _(act):
                copies(act, 0, lambda o, i: nc.scalar.activation(o, i, ACT.Copy))

            @block.vector
            def _(dve):
                copies(dve, 1, lambda o, i: nc.vector.tensor_copy(o, i))


def memory_attention(nc, core, a, out, layer, after_out):
    name = f"mem{layer}"
    scale = MEM_HD ** -0.5
    w = {n: core.pairs_of(a[f"mem_w_{n}"][layer]) for n in "kvqo"}
    with ExitStack() as ctx:
        def sb(what, shape, dt=F32):
            return ctx.enter_context(nc.sbuf_tensor(f"{name}_{what}", shape, dt))

        def sem(what):
            return core.sem(f"{name}_{what}")

        k_part = [sb("k_high", [P, KT, N_MEM], F32R), sb("k_low", [P, KT, N_MEM], F32R)]
        v_part = [sb("v_high", [P, 2, KT, P], F32R), sb("v_low", [P, 2, KT, P], F32R)]
        with ExitStack() as c2:
            def sb2(what, shape, dt=F32):
                return c2.enter_context(nc.sbuf_tensor(f"{name}_{what}", shape, dt))

            kT = sb2("kT", [P, KT, N_MEM])
            v_tok = sb2("v", [P, 2, KT, P])
            mem = sb2("mem", [P, KT, N_MEM])
            mh = [sb2("mh0", [P, KT, N_MEM], F32R), sb2("mh1", [P, KT, N_MEM], F32R)]
            with nc.semaphore(f"{name}_loaded") as loaded, nc.Block(f"{name}_load") as block:
                @block.sync
                def _(sp):
                    sp.dma_start(mem[:], a["mem"]).then_inc(loaded, 16)
                    sp.wait_ge(loaded, 16)
            projection(nc, core, name + "k", w["k"], KT // 2, KT, mh, N_MEM, "copy", kT, after=(w["v"], KT),
                       norm=([mem[:, k] for k in range(KT)], VEC["mem_m_norm"] + KT * layer), scaled=True)
            projection(nc, core, name + "v", w["v"], KT // 2, KT, mh, N_MEM, "copy", mem, after=(w["q"], KT),
                       scaled=True)
            rms_norm(nc, core, name + "kn", [dict(
                x=[kT[:, 2 * h + t] for t in range(2)], gain=[core.vec(VEC["mem_k_norm"] + 2 * layer + t) for t in range(2)],
                out=[kT[:, 2 * h + t] for t in range(2)]) for h in range(MEM_HEADS)], core.mats[:, ONES], MEM_HD, N_MEM)
            transposes(nc, core, name + "vt", [([mem[:, k] for k in range(4)], v_tok, 0),
                                               ([mem[:, k] for k in range(4, 8)], v_tok, 4)], [(0, P), (P, P)])
            stored, high_ready = sem("kv_stored"), sem("kv_high")
            with nc.Block(f"{name}_split") as block:
                @block.sync
                def _(sp):
                    sp.dma_start(out["p_mem_k"][layer], kT[:]).then_inc(stored, 16)
                    sp.dma_start(out["p_mem_v"][layer], v_tok[:]).then_inc(stored, 16)
                    sp.wait_ge(stored, 32)

                @block.scalar
                def _(act):
                    nc.scalar.activation(k_part[0][:], kT[:], ACT.Copy).then_inc(high_ready, 1)
                    nc.scalar.activation(v_part[0][:], v_tok[:], ACT.Copy).then_inc(high_ready, 1)

                @block.vector
                def _(dve):
                    for n, (parts, x) in enumerate(((k_part, kT), (v_part, v_tok))):
                        dve.wait_ge(high_ready, n + 1)
                        nc.vector.tensor_tensor(parts[1][:], x[:], parts[0][:].bitcast(F32), ALU.subtract)
        RING, PARTS = 6, 3
        HALF = KT * N_MEM // 2
        HALVES = 4 * DEC_BATCH
        ring = sb("ring", [P, RING, HALF])

        ring_in = [sem(f"ring_in{r}") for r in range(RING)]

        def load(sp, j):
            i, m = j // 2, j % 2
            src = (a["cache_mem_k"][layer, i].rearrange("p k c -> p (k c)") if i < DEC_BATCH else
                   a["cache_mem_v"][layer, i - DEC_BATCH].rearrange("p t f c -> p (t f c)"))
            sp.dma_start(ring[:, j % RING], src[:, m * HALF:(m + 1) * HALF]).then_inc(ring_in[j % RING], 16)

        FRONT = DEC_SEQ * (DEC_BATCH - 1)
        own = [sb("own_high", [P, 2, FRONT + KT * P], F32R), sb("own_low", [P, 2, FRONT + KT * P], F32R)]
        zeros = core.mats[:, IDENT, 0:1].unsqueeze(2).broadcast_to([P, 2, FRONT + KT * P])
        with nc.Block(f"{name}_ring") as block:
            @block.sync
            def _(sp):
                for j in range(RING):
                    load(sp, j)

            @block.scalar
            def _(act):
                nc.scalar.activation(own[0][:], zeros, ACT.Copy, scale=0.0)

            @block.vector
            def _(dve):
                nc.vector.tensor_scalar(own[1][:], zeros, 0.0, None, ALU.mult)

        q_stack = ctx.enter_context(ExitStack())
        q = q_stack.enter_context(nc.sbuf_tensor(f"{name}_q", [P, KT, TOK], F32))
        projection(nc, core, name + "q", w["q"], KT // 2, KT, core.h, TOK, "copy", q, after=(w["o"], KT),
                   norm=of_x(core, VEC["mem_x_norm"] + KT * layer), scaled=True)
        rms_norm(nc, core, name + "qn", [dict(
            x=[q[:, 2 * h + t] for t in range(2)], gain=[core.vec(VEC["mem_q_norm"] + 2 * layer + t) for t in range(2)],
            split=[(core.h[0][:, 2 * h + t], core.h[1][:, 2 * h + t]) for t in range(2)]) for h in range(MEM_HEADS)],
            core.mats[:, ONES], MEM_HD, TOK)
        q_stack.close()
        ring_high = sb("ring_high", [P, PARTS, HALF], F32R)
        ring_low = sb("ring_low", [P, PARTS, HALF], F32R)

        stages = [0, 1, 2, 3, "sample"]
        NS = len(stages)
        blocks = SEQ // P
        prob = sb("prob", [P, 2, blocks, N_MEM])
        pT = [sb("pT_high", [P, 2, SEQ], F32R), sb("pT_low", [P, 2, SEQ], F32R)]
        small = core.rstd[:, 0:NS * 3 * blocks].rearrange("p (n k b) -> p n k b", n=NS, k=3)
        sample_pT = prob[:, 0, 1]
        sample_rows = prob[:, 0, 0]
        with ExitStack() as c2:
            scored, maxed, shifted, exped, summed, inverted, scaled = [sem(n) for n in
                ("scored", "maxed", "shifted", "exped", "summed", "inverted", "scaled")]
            turned, pT_high, pT_low, out_done, high_ready, low_ready = [sem(n) for n in
                ("turned", "pT_high_ready", "pT_low_ready", "out_done", "high_ready", "low_ready")]
            sample_turned, split_high, split_low, used, rows_copied, rows_turned = [sem(n) for n in
                ("sample_turned", "split_high", "split_low", "used", "rows_copied", "rows_turned")]

            def own_columns(which, i):
                return own[which][:, i % 2, FRONT:].rearrange("p (h t c) -> p h t c", t=2, c=P)[:, :, :, 0:DEC_SEQ]

            def sample_queries(which, i):
                return core.h[which][:, :, SEQ + i * DEC_SEQ:SEQ + (i + 1) * DEC_SEQ].rearrange("p (h t) c -> p h t c", t=2)

            def sample_probs(i):
                b = i - DEC_BATCH
                rows = sample_pT.rearrange("p (t h c) -> p h t c", t=2, h=MEM_HEADS)
                return rows[:, :, :, b * DEC_SEQ:(b + 1) * DEC_SEQ]

            PASSES = ((0, 0), (0, 1), (1, 0))
            sample_out = core.ps[:, 7, 0:2 * P].rearrange("p (d h c) -> p h d c", d=2, h=MEM_HEADS)

            def sample_part(which):
                return core.h[which][:, :, SEQ:TOK].rearrange("p (h d) c -> p h d c", d=2)

            def rows(n):
                return 1 if stages[n] == "sample" else blocks

            def scores_of(n):
                if stages[n] == "sample":
                    return core.ps[:, 6:7, 0:N_MEM]
                return core.ps[:, 0:2, :].rearrange("p k (b c) -> p (k b) c", b=blocks // 2)

            def heads_before(n):
                return len([s for s in stages[:n] if s != "sample"])

            with nc.Block(f"{name}_attend") as block:
                @block.sync
                def _(sp):
                    for j in range(RING, HALVES):
                        sp.wait_ge(split_low, j - RING + 1)
                        load(sp, j)

                @block.tensor
                def _(pe):
                    def scores(n):
                        h = stages[n]
                        if n >= 1:
                            pe.wait_ge(shifted, n)
                        for b in range(blocks):
                            c = (b % 2) * N_MEM
                            for t in range(2):
                                for n_pass, (i, j) in enumerate(PASSES):
                                    ins = nc.tensor.matmul(core.ps[:, b // 2, c:c + N_MEM],
                                                           core.h[i][:, 2 * h + t, b * P:(b + 1) * P],
                                                           k_part[j][:, 2 * h + t, :], start=(t + n_pass == 0),
                                                           stop=(t == 1 and n_pass == 2))
                        ins.then_inc(scored, 1)

                    def turn(n):
                        pe.wait_ge(scaled, n + 1)
                        if n >= 1 and stages[n] != "sample":
                            pe.wait_ge(pT_low, heads_before(n))
                        for b in range(rows(n)):
                            for t in range(2):
                                dst = (core.ps[:, 7, N_MEM + t * P:N_MEM + (t + 1) * P] if stages[n] == "sample" else
                                       core.ps[:, 2 + t, b * P:(b + 1) * P])
                                ins = nc.tensor.transpose(dst, prob[:, n % 2, b, t * P:(t + 1) * P], core.mats[:, IDENT])
                        ins.then_inc(turned, 1)

                    def values(n):
                        h = stages[n]
                        pe.wait_ge(pT_low, heads_before(n) + 1)
                        if h >= 1:
                            pe.wait_ge(low_ready, 2 * h)
                        for d in range(2):
                            for t in range(2):
                                for n_pass, (i, j) in enumerate(PASSES):
                                    ins = nc.tensor.matmul(core.ps[:, 4 + d, :], v_part[i][:, t, 2 * h + d, :],
                                                           pT[j][:, t, :], start=(t + n_pass == 0),
                                                           stop=(t == 1 and n_pass == 2))
                            ins.then_inc(out_done, 1)

                    def half_item(j):
                        i, m = j // 2, j % 2
                        b = i % DEC_BATCH
                        pe.wait_ge(split_low, j + 1)
                        if i < DEC_BATCH:
                            tiles = [(h, t, (2 * (h - 2 * m) + t) * N_MEM) for h in (2 * m, 2 * m + 1) for t in range(2)]
                        else:
                            tiles = [(h, m, 2 * h * P) for h in range(MEM_HEADS)]
                        for h, t, at in tiles:
                            first = FRONT + (2 * h + t) * P - h * TS - b * DEC_SEQ
                            for n, (mine, streamed) in enumerate(PASSES):
                                start = b + m + n == 0 and (h, t, at) == tiles[0]
                                stop = b == DEC_BATCH - 1 and m == 1 and n == 2 and (h, t, at) == tiles[-1]
                                ins = nc.tensor.matmul(core.ps[:, 6, 0:N_MEM], own[mine][:, i % 2, first:first + P],
                                                       (ring_high, ring_low)[streamed][:, j % PARTS, at:at + N_MEM],
                                                       start=start, stop=stop)
                        ins.then_inc(used, 1)

                    def items(first, count):
                        for j in range(2 * first, 2 * (first + count)):
                            half_item(j)

                    scores(0)
                    items(0, 1)
                    scores(1)
                    items(1, 1)
                    turn(0)
                    items(2, 1)
                    scores(2)
                    values(0)
                    items(3, 1)
                    turn(1)
                    scores(3)
                    values(1)
                    items(4, 1)
                    turn(2)
                    items(5, 1)
                    values(2)
                    items(6, 1)
                    turn(3)
                    items(7, 1)
                    values(3)
                    turn(4)
                    items(8, 8)
                    pe.wait_ge(rows_copied, 1)
                    for d in range(2):
                        ins = nc.tensor.transpose(core.ps[:, 7, d * P:(d + 1) * P], sample_rows[:, d * P:(d + 1) * P],
                                                  core.mats[:, IDENT])
                    ins.then_inc(rows_turned, 1)

                @block.vector
                def _(dve):
                    def spread(n, what):
                        return small[:, n, what, 0:rows(n)].unsqueeze(2).broadcast_to([P, rows(n), N_MEM])

                    def shift(n):
                        if stages[n] == "sample":
                            dve.wait_ge(used, HALVES // 2)
                        else:
                            dve.wait_ge(scored, heads_before(n) + 1)
                        nc.vector.tensor_reduce(small[:, n, 0, 0:rows(n)], scores_of(n), AX_X, ALU.max).then_inc(maxed, 1)
                        dve.wait_ge(maxed, n + 1)
                        if n >= 2:
                            dve.wait_ge(turned, n - 1)
                        p = prob[:, n % 2, 0:rows(n)]
                        nc.vector.tensor_tensor(p, scores_of(n), spread(n, 0), ALU.subtract).then_inc(shifted, 1)

                    def divide(n):
                        p = prob[:, n % 2, 0:rows(n)]
                        dve.wait_ge(exped, n + 1)
                        nc.vector.tensor_reduce(small[:, n, 1, 0:rows(n)], p, AX_X, ALU.add).then_inc(summed, 1)
                        dve.wait_ge(summed, n + 1)
                        nc.vector.reciprocal(small[:, n, 2, 0:rows(n)], small[:, n, 1, 0:rows(n)]).then_inc(inverted, 1)
                        dve.wait_ge(inverted, n + 1)
                        nc.vector.tensor_tensor(p, p, spread(n, 2), ALU.mult).then_inc(scaled, 1)

                    def turned_low(h):
                        dve.wait_ge(pT_high, h + 1)
                        nc.vector.tensor_tensor(pT[1][:], core.ps[:, 2:4, :], pT[0][:].bitcast(F32), ALU.subtract
                                                ).then_inc(pT_low, 1)

                    def low(h):
                        for d in range(2):
                            n = 2 * h + d
                            dve.wait_ge(high_ready, n + 1)
                            nc.vector.tensor_tensor(core.h[1][:, n, 0:SEQ], core.ps[:, 4 + d, :],
                                                    core.h[0][:, n, 0:SEQ].bitcast(F32), ALU.subtract
                                                    ).then_inc(low_ready, 1)

                    def low_parts(first, count):
                        for j in range(2 * first, 2 * (first + count)):
                            i = j // 2
                            dve.wait_ge(split_high, j + 1)
                            if j % 2 == 0 and i < DEC_BATCH:
                                nc.vector.tensor_copy(own_columns(1, i), sample_queries(1, i).bitcast(F32))
                            elif j % 2 == 0:
                                nc.vector.tensor_tensor(own_columns(1, i), sample_probs(i),
                                                        own_columns(0, i).bitcast(F32), ALU.subtract)
                            nc.vector.tensor_tensor(ring_low[:, j % PARTS], ring[:, j % RING],
                                                    ring_high[:, j % PARTS].bitcast(F32), ALU.subtract
                                                    ).then_inc(split_low, 1)

                    low_parts(0, 1)
                    shift(0)
                    low_parts(1, 1)
                    divide(0)
                    shift(1)
                    low_parts(2, 1)
                    divide(1)
                    turned_low(0)
                    shift(2)
                    low_parts(3, 1)
                    divide(2)
                    low(0)
                    turned_low(1)
                    shift(3)
                    low_parts(4, 1)
                    divide(3)
                    low(1)
                    low_parts(5, 1)
                    turned_low(2)
                    low_parts(6, 1)
                    low_parts(7, 1)
                    low(2)
                    turned_low(3)
                    shift(4)
                    divide(4)
                    low(3)
                    low_parts(8, 8)
                    dve.wait_ge(used, HALVES)
                    nc.vector.tensor_copy(sample_rows, core.ps[:, 6, 0:N_MEM]).then_inc(rows_copied, 1)
                    dve.wait_ge(high_ready, 2 * MEM_HEADS + 1)
                    nc.vector.tensor_tensor(sample_part(1), sample_out, sample_part(0).bitcast(F32), ALU.subtract
                                            ).then_inc(low_ready, 1)

                @block.scalar
                def _(act):
                    def exps(n):
                        act.wait_ge(shifted, n + 1)
                        p = prob[:, n % 2, 0:rows(n)]
                        nc.scalar.activation(p, p, ACT.Exp, scale=scale).then_inc(exped, 1)

                    def turned_copy(n):
                        act.wait_ge(turned, n + 1)
                        if n >= 1:
                            act.wait_ge(out_done, 2 * heads_before(n))
                        nc.scalar.activation(pT[0][:], core.ps[:, 2:4, :], ACT.Copy).then_inc(pT_high, 1)

                    def high(h):
                        for d in range(2):
                            n = 2 * h + d
                            act.wait_ge(out_done, n + 1)
                            nc.scalar.activation(core.h[0][:, n, 0:SEQ], core.ps[:, 4 + d, :], ACT.Copy
                                                 ).then_inc(high_ready, 1)

                    def high_parts(first, count):
                        for j in range(2 * first, 2 * (first + count)):
                            i = j // 2
                            act.wait_ge(ring_in[j % RING], 16 * (j // RING + 1))
                            if j >= PARTS:
                                act.wait_ge(used, j - PARTS + 1)
                            if j == 2 * DEC_BATCH:
                                act.wait_ge(turned, NS)
                                nc.scalar.activation(sample_pT, core.ps[:, 7, N_MEM:2 * N_MEM], ACT.Copy
                                                     ).then_inc(sample_turned, 1)
                                act.wait_ge(sample_turned, 1)
                            if j % 2 == 0:
                                source = sample_queries(0, i).bitcast(F32) if i < DEC_BATCH else sample_probs(i)
                                nc.scalar.activation(own_columns(0, i), source, ACT.Copy)
                            nc.scalar.activation(ring_high[:, j % PARTS], ring[:, j % RING], ACT.Copy
                                                 ).then_inc(split_high, 1)

                    high_parts(0, 1)
                    high_parts(1, 1)
                    exps(0)
                    exps(1)
                    high_parts(2, 1)
                    turned_copy(0)
                    high_parts(3, 1)
                    exps(2)
                    high(0)
                    high_parts(4, 1)
                    turned_copy(1)
                    exps(3)
                    high_parts(5, 1)
                    high(1)
                    high_parts(6, 1)
                    turned_copy(2)
                    high_parts(7, 1)
                    high(2)
                    turned_copy(3)
                    exps(4)
                    high(3)
                    high_parts(8, 8)
                    act.wait_ge(rows_turned, 1)
                    nc.scalar.activation(sample_part(0), sample_out, ACT.Copy).then_inc(high_ready, 1)
    projection(nc, core, name + "o", w["o"], KT // 2, KT, core.h, TOK, "add", core.x, after=after_out)


def s5(nc, core, pr, a, out):
    T, NB = S5_TILES, 8
    with ExitStack() as ctx:
        def sb(what, shape, dt=F32):
            return ctx.enter_context(nc.sbuf_tensor(f"s5_{what}", shape, dt))

        def sem(what):
            return core.sem(f"s5_{what}")

        prm = sb("prm", [P, 12, T])
        STEP, MAG, TH, PHI, PHIC, RND, SIN, COS, ABR, ABI, CR, CI = range(12)
        tmp = sb("tmp", [P, 4, T])
        fine = sb("fine", [P, 4, T, CHUNK])
        coarse = sb("coarse", [P, 4, T, NB])
        phi2 = sb("phi2", [P, 2, T])
        steps = sb("steps", [P, CHUNK + NB])
        b_in = sb("b_in", [P, 2, T, 32])
        bb = sb("bb", [P, 2, T, 32])
        bt = sb("bt", [P, 2, 4, P])
        cT = sb("cT", [P, 2, T, P])
        s0 = sb("s0", [P, 2, T, DEC_BATCH])
        inj = sb("inj", [P, 2, T, DEC_BATCH])
        fin = sb("fin", [P, 2, T, DEC_BATCH + 1])
        rot = sb("rot", [P, 2, 2, TOK])
        mags = sb("mags", [P, TOK])
        t0, t1, t2, t3 = sb("t0", [P, TOK]), sb("t1", [P, TOK]), sb("t2", [P, TOK]), sb("t3", [P, TOK])
        g = sb("g", [P, 2, TOK])
        hs = sb("hs", [P, 2, 2, TOK])
        z = core.z
        loaded, act_steps, dve_steps, b_turned, bt_ready = [sem(n) for n in
            ("loaded", "act_steps", "dve_steps", "b_turned", "bt_ready")]
        driven, drive_read, rot_ready, state_ready, tile_used = [sem(n) for n in
            ("driven", "drive_read", "rot_ready", "state_ready", "tile_used")]
        y_ready, high_ready, z_ready, stored, fin_ready, pool_steps = [sem(n) for n in
            ("y_ready", "high_ready", "z_ready", "stored", "fin_ready", "pool_steps")]
        mags_ready, chain = sem("mags_ready"), sem("chain")
        v = nc.vector
        ANGLES = 8 + 5 + 3 + 2 * (7 + 5)

        with nc.Block("s5_prepare") as block:
            @block.sync
            def _(sp):
                for dst, src in ((steps[:], a["s5_steps"]), (b_in[:], a["s5_b"]), (cT[:], a["s5_c"]), (s0[:], a["state_s5"])):
                    sp.dma_start(dst, src).then_inc(loaded, 16)

            @block.scalar
            def _(act):
                n = 0

                def step(ins):
                    nonlocal n
                    n += 1
                    ins.then_inc(act_steps, 1)
                    act.wait_ge(act_steps, n)
                step(nc.scalar.activation(prm[:, STEP], core.vecs("s5_log_step"), ACT.Exp))
                act.wait_ge(dve_steps, 1)
                step(nc.scalar.activation(prm[:, MAG], prm[:, MAG], ACT.Exp))
                act.wait_ge(dve_steps, ANGLES)
                step(nc.scalar.activation(prm[:, SIN:COS + 1], prm[:, SIN:COS + 1], ACT.Sin))
                step(nc.scalar.activation(fine[:, 0:2], fine[:, 0:2], ACT.Sin))
                step(nc.scalar.activation(coarse[:, 0:2], coarse[:, 0:2], ACT.Sin))

            @block.tensor
            def _(pe):
                pe.wait_ge(bt_ready, 1)
                for ri in range(2):
                    for j4 in range(4):
                        ins = nc.tensor.transpose(core.ps[:, ri, j4 * P:(j4 + 1) * P],
                                                  bb[:, ri, 4 * j4:4 * j4 + 4, :].rearrange("p a b -> p (a b)"),
                                                  core.mats[:, IDENT])
                ins.then_inc(b_turned, 1)

            def to_angle(step, x, ring):
                step(v.tensor_scalar(ring, x, MAGIC, None, ALU.add))
                step(v.tensor_scalar(ring, ring, MAGIC, None, ALU.subtract))
                step(v.tensor_tensor(x, x, ring, ALU.subtract))
                step(v.tensor_scalar(x, x, TWO_PI, PI_SAFE, ALU.mult, ALU.min))
                step(v.tensor_scalar(x, x, -PI_SAFE, None, ALU.max))

            def prepare(step, dve, waits=True):
                if waits:
                    dve.wait_ge(act_steps, 1)
                step(v.tensor_tensor(prm[:, MAG], core.vecs("s5_a_re"), prm[:, STEP], ALU.mult))
                step(v.tensor_tensor(prm[:, TH], core.vecs("s5_a_im"), prm[:, STEP], ALU.mult))
                step(v.tensor_scalar(prm[:, PHI], prm[:, TH], 1.0 / TWO_PI, None, ALU.mult))
                step(v.tensor_scalar(prm[:, RND], prm[:, PHI], MAGIC, None, ALU.add))
                step(v.tensor_scalar(prm[:, RND], prm[:, RND], MAGIC, None, ALU.subtract))
                step(v.tensor_tensor(prm[:, PHI], prm[:, PHI], prm[:, RND], ALU.subtract))
                step(v.tensor_copy(prm[:, SIN], prm[:, PHI]))
                step(v.tensor_scalar(prm[:, COS], prm[:, PHI], 0.25, None, ALU.add))
                to_angle(step, prm[:, SIN:COS + 1], tmp[:, 0:2])
                step(v.tensor_scalar(tmp[:, 0], prm[:, PHI], MAGIC13, None, ALU.add))
                step(v.tensor_scalar(phi2[:, 0], tmp[:, 0], MAGIC13, None, ALU.subtract))
                step(v.tensor_tensor(phi2[:, 1], prm[:, PHI], phi2[:, 0], ALU.subtract))
                if waits:
                    dve.wait_ge(loaded, 64)
                for tab, lo, w in ((fine, 0, CHUNK), (coarse, CHUNK, NB)):
                    num = steps[:, lo:lo + w].rearrange("p (o c) -> p o c", o=1).to_broadcast([P, T, w])
                    hi = phi2[:, 0].rearrange("p (t o) -> p t o", o=1).to_broadcast([P, T, w])
                    lo_ = phi2[:, 1].rearrange("p (t o) -> p t o", o=1).to_broadcast([P, T, w])
                    step(v.tensor_tensor(tab[:, 0], num, hi, ALU.mult))
                    step(v.tensor_scalar(tab[:, 2], tab[:, 0], MAGIC, None, ALU.add))
                    step(v.tensor_scalar(tab[:, 2], tab[:, 2], MAGIC, None, ALU.subtract))
                    step(v.tensor_tensor(tab[:, 0], tab[:, 0], tab[:, 2], ALU.subtract))
                    step(v.tensor_tensor(tab[:, 2], num, lo_, ALU.mult))
                    step(v.tensor_tensor(tab[:, 1], tab[:, 0], tab[:, 2], ALU.add))
                    step(v.tensor_scalar(tab[:, 0], tab[:, 1], 0.25, None, ALU.add))
                    to_angle(step, tab[:, 0:2], tab[:, 2:4])

            @block.vector
            def _(dve):
                n = 0

                def step(ins):
                    nonlocal n
                    n += 1
                    ins.then_inc(dve_steps, 1)
                    dve.wait_ge(dve_steps, n)

                prepare(step, dve)
                assert n == ANGLES
                dve.wait_ge(act_steps, 5)
                are, aim = core.vecs("s5_a_re"), core.vecs("s5_a_im")
                m = tmp
                step(v.tensor_tensor(prm[:, ABR], prm[:, MAG], prm[:, COS], ALU.mult))
                step(v.tensor_tensor(prm[:, ABI], prm[:, MAG], prm[:, SIN], ALU.mult))
                step(v.tensor_tensor(m[:, 0], are, are, ALU.mult))
                step(v.tensor_tensor(m[:, 1], aim, aim, ALU.mult))
                step(v.tensor_tensor(m[:, 0], m[:, 0], m[:, 1], ALU.add))
                step(v.reciprocal(m[:, 0], m[:, 0]))
                step(v.tensor_scalar(m[:, 1], prm[:, ABR], 1.0, None, ALU.subtract))
                step(v.tensor_tensor(m[:, 2], m[:, 1], are, ALU.mult))
                step(v.tensor_tensor(m[:, 3], prm[:, ABI], aim, ALU.mult))
                step(v.tensor_tensor(m[:, 2], m[:, 2], m[:, 3], ALU.add))
                step(v.tensor_tensor(prm[:, CR], m[:, 2], m[:, 0], ALU.mult))
                step(v.tensor_tensor(m[:, 2], prm[:, ABI], are, ALU.mult))
                step(v.tensor_tensor(m[:, 3], m[:, 1], aim, ALU.mult))
                step(v.tensor_tensor(m[:, 2], m[:, 2], m[:, 3], ALU.subtract))
                step(v.tensor_tensor(prm[:, CI], m[:, 2], m[:, 0], ALU.mult))

                def cmul(o_re, o_im, x_re, x_im, y_re, y_im, s):
                    step(v.tensor_tensor(o_re, x_re, y_re, ALU.mult))
                    step(v.tensor_tensor(s, x_im, y_im, ALU.mult))
                    step(v.tensor_tensor(o_re, o_re, s, ALU.subtract))
                    step(v.tensor_tensor(o_im, x_re, y_im, ALU.mult))
                    step(v.tensor_tensor(s, x_im, y_re, ALU.mult))
                    step(v.tensor_tensor(o_im, o_im, s, ALU.add))

                def over(i, w):
                    return prm[:, i].rearrange("p (t o) -> p t o", o=1).to_broadcast([P, T, w])

                cmul(bb[:, 0], bb[:, 1], over(CR, 32), over(CI, 32), b_in[:, 0], b_in[:, 1],
                     t0[:, 0:T * 32].rearrange("p (t c) -> p t c", t=T))
                step(v.tensor_scalar(cT[:, 1], cT[:, 1], -1.0, None, ALU.mult))
                cmul(inj[:, 0], inj[:, 1], over(ABR, DEC_BATCH), over(ABI, DEC_BATCH), s0[:, 0], s0[:, 1],
                     t0[:, 0:T * DEC_BATCH].rearrange("p (t c) -> p t c", t=T))
                dve.sem_inc(bt_ready, 1)
                dve.wait_ge(b_turned, 1)
                v.tensor_copy(bt[:].rearrange("p r j c -> p r (j c)"), core.ps[:, 0:2, :]).then_inc(bt_ready, 1)

        with nc.Block("s5_scan") as block:
            @block.tensor
            def _(pe):
                def drive(j):
                    r = slice(32 * (j % 4), 32 * (j % 4) + 32)
                    if j >= 1:
                        pe.wait_ge(drive_read, j)
                    for ri in range(2):
                        for gr in range(2):
                            ins = nc.tensor.matmul(core.ps[:, 2 * ri + gr, 0:272], bt[r, ri, j // 4, :],
                                                   pr[r, SU + j // 4, gr * 272:(gr + 1) * 272], start=True, stop=True)
                    ins.then_inc(driven, 1)

                def outputs(j):
                    pe.wait_ge(state_ready, 2 * (j + 1))
                    if j % 4 == 0 and j >= 8:
                        pe.wait_ge(y_ready, j // 4 - 1)
                    b = 4 + 2 * ((j // 4) % 2)
                    for ri in range(2):
                        for gr in range(2):
                            ins = nc.tensor.matmul(core.ps[:, b + gr, 0:272], cT[:, ri, j, :],
                                                   hs[:, j % 2, ri, gr * 272:(gr + 1) * 272],
                                                   start=(j % 4 == 0 and ri == 0), stop=(j % 4 == 3 and ri == 1))
                    ins.then_inc(tile_used, 1)

                for j in range(T + 1):
                    if j < T:
                        drive(j)
                    if j >= 1:
                        outputs(j - 1)

            def finish_y(dve, t):
                b = 4 + 2 * (t % 2)
                dve.wait_ge(tile_used, 4 * (t + 1))
                v.scalar_tensor_tensor(in_groups(z[:, t], TOK), in_groups(pr[:, SU + t], TOK), core.vec(VEC["s5_d"] + t),
                                       core.ps[:, b:b + 2, 0:272], ALU.mult, ALU.add).then_inc(y_ready, 1)

            @block.gpsimd
            def _(pool):
                n = 0

                def step(ins):
                    nonlocal n
                    n += 1
                    ins.then_inc(pool_steps, 1)
                    pool.wait_ge(pool_steps, n)
                for j in range(T):
                    if j >= 2:
                        pool.wait_ge(state_ready, 2 * (j - 1))
                    dst = [rot[:, j % 2, ri, 0:SEQ].rearrange("p (c t) -> p c t", t=CHUNK) for ri in range(2)]
                    co = [coarse[:, ri, j].rearrange("p (c o) -> p c o", o=1).to_broadcast([P, NB, CHUNK]) for ri in range(2)]
                    fi = [fine[:, ri, j].rearrange("p (o t) -> p o t", o=1).to_broadcast([P, NB, CHUNK]) for ri in range(2)]
                    sc = t3[:, 0:SEQ].rearrange("p (c t) -> p c t", t=CHUNK)
                    step(nc.gpsimd.tensor_tensor(dst[0], co[0], fi[0], ALU.mult))
                    step(nc.gpsimd.tensor_tensor(sc, co[1], fi[1], ALU.mult))
                    step(nc.gpsimd.tensor_tensor(dst[0], dst[0], sc, ALU.subtract))
                    step(nc.gpsimd.tensor_tensor(dst[1], co[1], fi[0], ALU.mult))
                    step(nc.gpsimd.tensor_tensor(sc, co[0], fi[1], ALU.mult))
                    step(nc.gpsimd.tensor_tensor(dst[1], dst[1], sc, ALU.add))
                    for ri in range(2):
                        src = fine[:, ri, j, 0:DEC_SEQ].rearrange("p (o t) -> p o t", o=1).to_broadcast([P, DEC_BATCH, DEC_SEQ])
                        ins = nc.gpsimd.tensor_copy(rot[:, j % 2, ri, SEQ:TOK].rearrange("p (b t) -> p b t", t=DEC_SEQ), src)
                        if ri == 0:
                            step(ins)
                    ins.then_inc(rot_ready, 1)

            @block.vector
            def _(dve):
                n = 0

                def step(ins):
                    nonlocal n
                    n += 1
                    ins.then_inc(chain, 1)
                    dve.wait_ge(chain, n)

                def wide(ap):
                    return in_groups(ap, TOK)
                for j in range(T):
                    dve.wait_ge(driven, j + 1)
                    dve.wait_ge(rot_ready, j + 1)
                    if j >= 1:
                        dve.wait_ge(state_ready, 2 * j)
                    co, si = rot[:, j % 2, 0], rot[:, j % 2, 1]
                    re, im = core.ps[:, 0:2, 0:272], core.ps[:, 2:4, 0:272]
                    v.tensor_tensor(wide(t0[:]), re, wide(co), ALU.mult)
                    v.tensor_tensor(wide(t1[:]), im, wide(si), ALU.mult)
                    v.tensor_tensor(wide(t2[:]), im, wide(co), ALU.mult)
                    v.tensor_tensor(wide(g[:, 1]), re, wide(si), ALU.mult).then_inc(drive_read, 1)
                    dve.wait_ge(drive_read, j + 1)
                    v.tensor_tensor(t0[:], t0[:], t1[:], ALU.add)
                    step(v.tensor_tensor(t2[:], t2[:], g[:, 1], ALU.subtract))
                    first = slice(SEQ, TOK, DEC_SEQ)
                    v.tensor_tensor(t0[:, first], t0[:, first], inj[:, 0, j], ALU.add)
                    ins = v.tensor_tensor(t2[:, first], t2[:, first], inj[:, 1, j], ALU.add)
                    step(ins)
                    dve.wait_ge(mags_ready, j + 1)
                    v.tensor_tensor_scan(g[:, 0], mags[:], t0[:], 0.0, ALU.mult, ALU.add)
                    step(v.tensor_tensor_scan(g[:, 1], mags[:], t2[:], 0.0, ALU.mult, ALU.add))
                    if j >= 2:
                        dve.wait_ge(tile_used, j - 1)
                        dve.wait_ge(fin_ready, j - 1)
                    hr, hi = hs[:, j % 2, 0], hs[:, j % 2, 1]
                    v.tensor_tensor(hr, g[:, 0], co, ALU.mult)
                    v.tensor_tensor(t0[:], g[:, 1], si, ALU.mult)
                    v.tensor_tensor(hi, g[:, 0], si, ALU.mult)
                    step(v.tensor_tensor(t1[:], g[:, 1], co, ALU.mult))
                    v.tensor_tensor(hr, hr, t0[:], ALU.subtract).then_inc(state_ready, 1)
                    v.tensor_tensor(hi, hi, t1[:], ALU.add).then_inc(state_ready, 1)
                    if j % 4 == 3 and j > 4:
                        finish_y(dve, j // 4 - 1)
                finish_y(dve, 3)

            @block.scalar
            def _(act):
                for j in range(T + 1):
                    if j < T:
                        if j >= 1:
                            act.wait_ge(state_ready, 2 * j)
                        nc.scalar.activation(mags[:], core.reset_s5[:], ACT.Copy, scale=prm[:, MAG, j:j + 1]
                                             ).then_inc(mags_ready, 1)
                    if j >= 1:
                        act.wait_ge(state_ready, 2 * j)
                        nc.scalar.activation(fin[:, :, j - 1, 0:1], hs[:, (j - 1) % 2, :, SEQ - 1:SEQ], ACT.Copy)
                        nc.scalar.activation(fin[:, :, j - 1, 1:9], hs[:, (j - 1) % 2, :, SEQ + 3:TOK:DEC_SEQ], ACT.Copy
                                             ).then_inc(fin_ready, 1)
                for t in range(4):
                    act.wait_ge(y_ready, t + 1)
                    nc.scalar.activation(z[:, t], z[:, t], ACT.Gelu_apprx_tanh).then_inc(z_ready, 1)
                    act.wait_ge(z_ready, t + 1)
                    nc.scalar.activation(core.h[0][:, 4 + t], z[:, t], ACT.Copy).then_inc(high_ready, 1)

            @block.sync
            def _(sp):
                sp.wait_ge(fin_ready, T)
                sp.dma_start(out["s5"], fin[:]).then_inc(stored, 16)
                sp.wait_ge(stored, 16)

        with nc.Block("s5_low") as block:
            @block.vector
            def _(dve):
                nc.vector.tensor_tensor(core.h[1][:, 4:8], z[:], core.h[0][:, 4:8].bitcast(F32), ALU.subtract)


def s5_gate(nc, core, glu):
    with ExitStack() as ctx:
        def sem(what):
            return core.sem(f"glu_{what}")

        sig_ready, prod_ready, high_ready = sem("sig_ready"), sem("prod_ready"), sem("high_ready")
        with nc.Block("s5_gate") as block:
            @block.scalar
            def _(act):
                for t in range(4):
                    nc.scalar.activation(glu[:, t], glu[:, t], ACT.Sigmoid, bias=core.vec(VEC["s5_b_glu"] + t)
                                         ).then_inc(sig_ready, 1)
                for t in range(4):
                    act.wait_ge(prod_ready, t + 1)
                    nc.scalar.activation(core.h[0][:, t], core.z[:, t], ACT.Copy).then_inc(high_ready, 1)

            @block.vector
            def _(dve):
                for t in range(4):
                    dve.wait_ge(sig_ready, t + 1)
                    nc.vector.tensor_tensor(core.z[:, t], core.z[:, t], glu[:, t], ALU.mult).then_inc(prod_ready, 1)
                for t in range(4):
                    dve.wait_ge(high_ready, t + 1)
                    nc.vector.tensor_tensor(core.h[1][:, t], core.z[:, t], core.h[0][:, t].bitcast(F32), ALU.subtract)


def window_attention(nc, core, pr, a, out):
    scale = 64 ** -0.5
    NB = SEQ // P
    with ExitStack() as ctx:
        def sb(what, shape, dt=F32):
            return ctx.enter_context(nc.sbuf_tensor(f"swa_{what}", shape, dt))

        heads = [pr[:, SQ + i] for i in range(4)] + [pr[:, SK]]
        rms_norm(nc, core, "swa_qk", [dict(x=[x], out=[x], gain=[core.vec(VEC["swa_q_norm" if i < 4 else "swa_k_norm"])])
                                      for i, x in enumerate(heads)], core.mats[:, ONES64], 64, TOK)
        rot = sb("rot", [P, 2, TOK])
        tmp = sb("tmp", [P, TOK])
        kc = sb("kc", [P, DEC_BATCH, P])
        vc = sb("vc", [P, DEC_BATCH, P])
        v_tok = sb("v_tok", [P, NB + 1, 1, P])
        mask = sb("mask", [P, 2 * P])
        mask_s = sb("mask_s", [P, P + TS])
        transposes(nc, core, "swa_vt", [([pr[:, SV]], v_tok, 0)])
        with ExitStack() as c2:
            def sem(what):
                return core.sem(f"swar_{what}")
            loaded, swapped, cosed, sined, rotated = [sem(n) for n in ("loaded", "swapped", "cosed", "sined", "rotated")]
            with nc.Block("swa_rotate") as block:
                @block.sync
                def _(sp):
                    loads = ((rot[:], a["swa_rot"]), (kc[:], a["cache_swa_k"]), (vc[:], a["cache_swa_v"]),
                             (mask[:], a["swa_mask"]), (mask_s[:], a["swa_mask_s"]))
                    for dst, src in loads:
                        sp.dma_start(dst, src).then_inc(loaded, 16)
                    sp.wait_ge(loaded, 16 * len(loads))

                @block.tensor
                def _(pe):
                    for n, x in enumerate(heads):
                        b = 2 * (n % 2)
                        if n >= 2:
                            pe.wait_ge(sined, n - 1)
                        for g in range(2):
                            ins = nc.tensor.matmul(core.ps[:, b + g, 0:272], core.mats[:, SWAP8],
                                                   x[:, g * 272:(g + 1) * 272], start=True, stop=True)
                        ins.then_inc(swapped, 1)

                @block.vector
                def _(dve):
                    dve.wait_ge(loaded, 80)
                    for n, x in enumerate(heads):
                        b = 2 * (n % 2)
                        dve.wait_ge(swapped, n + 1)
                        if n:
                            dve.wait_ge(rotated, n)
                        nc.vector.tensor_tensor(in_groups(tmp[:], TOK), core.ps[:, b:b + 2, 0:272],
                                                in_groups(rot[:, 1], TOK), ALU.mult).then_inc(sined, 1)
                        nc.vector.tensor_tensor(x, x, rot[:, 0], ALU.mult).then_inc(cosed, 1)
                        dve.wait_ge(sined, n + 1)
                        dve.wait_ge(cosed, n + 1)
                        nc.vector.tensor_tensor(x, x, tmp[:], ALU.add).then_inc(rotated, 1)

        units = [(b, i, kv) for b in range(NB) for i in range(4) for kv in range(2)]
        NU = len(units)
        logit = sb("logit", [P, 2, 2 * P])
        prob = sb("prob", [P, 3, 2 * P])
        pT = sb("pT", [P, 2, 2, P])
        small = sb("small", [P, 7, NU + 2])
        qs = sb("qs", [P, 4 * TS])
        sT = sb("sT", [P, 2, P])
        o_sb = sb("o_sb", [P, 4, TOK])
        sinks = core.vecs("sinks")
        kT = pr[:, SK]
        with ExitStack() as c2:
            def sem(what):
                return core.sem(f"swa_{what}")

            names = ("scored", "masked", "maxed", "sunk", "negated", "exped", "sink_exped", "totalled", "inverted", "scaled",
                     "turned", "turn_copied", "out_done", "out_copied", "q_ready", "cached", "sT_ready", "stored", "high_ready")
            S = {n: sem(n) for n in names}

            def keys(u):
                b = units[u][0] if u < NU else None
                return 2 * P if u < NU and b else (P if u < NU else P + TS)

            def scores_at(u):
                return core.ps[:, (0, 1, 6)[u % 3]]

            def cached_at(kv):
                return core.ps[:, (7, 4)[kv], 0:P]

            with nc.Block("swa_attend") as block:
                @block.sync
                def _(sp):
                    with nc.allow_non_contiguous_dma(reason="four new rows a batch"):
                        sp.dma_start(out["s_swa_k"][:, :, 0:WIN - DEC_SEQ], kc[:, :, DEC_SEQ:WIN]).then_inc(S["stored"], 16)
                        sp.dma_start(out["s_swa_k"][:, :, WIN - DEC_SEQ:WIN],
                                     kT[:, SEQ:TOK].rearrange("p (b t) -> p b t", t=DEC_SEQ)).then_inc(S["stored"], 16)
                        sp.dma_start(out["s_swa_v"][0:WIN - DEC_SEQ], vc[DEC_SEQ:WIN]).then_inc(S["stored"], 16)
                        for b in range(DEC_BATCH):
                            sp.dma_start(out["s_swa_v"][WIN - DEC_SEQ:WIN, b],
                                         v_tok[DEC_SEQ * b:DEC_SEQ * (b + 1), NB, 0, :]).then_inc(S["stored"], 16)
                        sp.dma_start(out["p_swa_k"], kT[:, SEQ - WIN:SEQ]).then_inc(S["stored"], 16)
                        sp.dma_start(out["p_swa_v"], v_tok[:, NB - 1, 0, :]).then_inc(S["stored"], 16)
                    sp.wait_ge(S["stored"], 16 * (5 + DEC_BATCH))

                @block.tensor
                def _(pe):
                    def scores(u):
                        b, i, kv = units[u]
                        r = slice(64 * kv, 64 * kv + 64)
                        lo = max(0, b - 1) * P
                        if u >= 3:
                            pe.wait_ge(S["masked"], u - 2)
                        nc.tensor.matmul(scores_at(u)[:, 0:keys(u)], pr[r, SQ + i, b * P:(b + 1) * P],
                                         kT[r, lo:(b + 1) * P], start=True, stop=True).then_inc(S["scored"], 1)

                    def turn(u):
                        pe.wait_ge(S["scaled"], u + 1)
                        if u >= 2:
                            pe.wait_ge(S["turn_copied"], u - 1)
                        n = keys(u)
                        for t in range((n + P - 1) // P):
                            w = min(P, n - t * P)
                            ins = nc.tensor.transpose(core.ps[0:w, 2 + u % 2, t * P:(t + 1) * P],
                                                      prob[:, u % 3, t * P:t * P + w], core.mats[:, IDENT])
                        ins.then_inc(S["turned"], 1)

                    def values(u):
                        b, i, kv = units[u]
                        r = slice(64 * kv, 64 * kv + 64)
                        pe.wait_ge(S["turn_copied"], u + 1)
                        if u == 0:
                            pe.wait_ge(S["sT_ready"], 2)
                        if u >= 4:
                            pe.wait_ge(S["out_copied"], u // 2 - 1)
                        nt = keys(u) // P
                        for t in range(nt):
                            ins = nc.tensor.matmul(core.ps[r, 4 + (u // 2) % 2, 0:P],
                                                   v_tok[:, b - nt + 1 + t, 0, r], pT[:, u % 2, t, :],
                                                   start=(t == 0), stop=(t == nt - 1))
                        ins.then_inc(S["out_done"], 1)

                    def cached_scores(kv):
                        r = slice(64 * kv, 64 * kv + 64)
                        pe.wait_ge(S["q_ready"], 4)
                        for b in range(DEC_BATCH):
                            ins = nc.tensor.matmul(cached_at(kv)[:, b * 16:(b + 1) * 16], kc[r, b, :],
                                                   qs[r, b * 16:(b + 1) * 16], start=True, stop=True)
                        ins.then_inc(S["cached"], 1)

                    def sample_scores(kv):
                        r = slice(64 * kv, 64 * kv + 64)
                        u = NU + kv
                        pe.wait_ge(S["sT_ready"], kv + 1)
                        pe.wait_ge(S["masked"], u - 2)
                        nc.tensor.transpose(scores_at(u)[:, 0:P], sT[:, kv, :], core.mats[:, IDENT])
                        nc.tensor.matmul(scores_at(u)[:, P:P + TS], qs[r, :], kT[r, SEQ:TOK],
                                         start=True, stop=True).then_inc(S["scored"], 1)

                    def sample_values(kv):
                        r = slice(64 * kv, 64 * kv + 64)
                        u = NU + kv
                        pe.wait_ge(S["turn_copied"], u + 1)
                        if kv == 0:
                            pe.wait_ge(S["out_copied"], NU // 2 - 1)
                        o = core.ps[r, 4, 0:P]
                        nc.tensor.matmul(o, v_tok[0:TS, NB, 0, r], pT[0:TS, u % 2, 1, :], start=True, stop=False)
                        for b in range(DEC_BATCH):
                            ins = nc.tensor.matmul(o[:, b * 16:(b + 1) * 16], vc[:, b, r], pT[:, u % 2, 0, b * 16:(b + 1) * 16],
                                                   start=False, stop=(b == DEC_BATCH - 1))
                        ins.then_inc(S["out_done"], 1)

                    for kv in range(2):
                        cached_scores(kv)
                    for u in range(NU + 2 + 3):
                        if u < NU:
                            scores(u)
                        elif u < NU + 2:
                            sample_scores(u - NU)
                        if 0 <= u - 2 < NU + 2:
                            turn(u - 2)
                        if 0 <= u - 3 < NU:
                            values(u - 3)
                        elif u - 3 >= NU:
                            sample_values(u - 3 - NU)

                @block.vector
                def _(dve):
                    qv = qs[:].rearrange("p (b i t) -> p i b t", b=DEC_BATCH, i=4)
                    for i in range(4):
                        nc.vector.tensor_copy(qv[:, i], pr[:, SQ + i, SEQ:TOK].rearrange("p (b t) -> p b t", t=DEC_SEQ)
                                              ).then_inc(S["q_ready"], 1)

                    def row(k, u):
                        return small[:, k, u:u + 1]

                    def sink(u):
                        if u < NU:
                            h = units[u][1] + 4 * units[u][2]
                            return core.vec(VEC["sinks"] + h)
                        return core.vec(VEC["sink_rows"] + u - NU)

                    def soft(u):
                        n = keys(u)
                        dve.wait_ge(S["scored"], u + 1)
                        if u >= 2:
                            dve.wait_ge(S["exped"], u - 1)
                        m = mask[:, 2 * P - n:2 * P] if u < NU else mask_s[:]
                        nc.vector.scalar_tensor_tensor(logit[:, u % 2, 0:n], scores_at(u)[:, 0:n], scale, m,
                                                       ALU.mult, ALU.add).then_inc(S["masked"], 1)
                        dve.wait_ge(S["masked"], u + 1)
                        nc.vector.tensor_reduce(row(0, u), logit[:, u % 2, 0:n], AX_X, ALU.max).then_inc(S["maxed"], 1)
                        dve.wait_ge(S["maxed"], u + 1)
                        nc.vector.tensor_scalar(row(2, u), row(0, u), sink(u), -1.0, ALU.max, ALU.mult).then_inc(S["negated"], 1)

                    def divide(u):
                        n = keys(u)
                        dve.wait_ge(S["sink_exped"], u + 1)
                        nc.vector.tensor_tensor(row(5, u), row(3, u), row(4, u), ALU.add).then_inc(S["totalled"], 1)
                        dve.wait_ge(S["totalled"], u + 1)
                        nc.vector.reciprocal(row(6, u), row(5, u)).then_inc(S["inverted"], 1)
                        dve.wait_ge(S["inverted"], u + 1)
                        nc.vector.tensor_scalar(prob[:, u % 3, 0:n], prob[:, u % 3, 0:n], row(6, u), None, ALU.mult
                                                ).then_inc(S["scaled"], 1)

                    for kv in range(2):
                        dve.wait_ge(S["cached"], kv + 1)
                        nc.vector.tensor_copy(sT[:, kv], cached_at(kv)).then_inc(S["sT_ready"], 1)
                    for u in range(NU + 2):
                        soft(u)
                        if u >= 1:
                            divide(u - 1)
                    divide(NU + 1)
                    dve.wait_ge(S["high_ready"], 4)
                    nc.vector.tensor_tensor(core.h[1][:, 4:8], o_sb[:], core.h[0][:, 4:8].bitcast(F32), ALU.subtract)

                @block.scalar
                def _(act):
                    def row(k, u):
                        return small[:, k, u:u + 1]

                    def exps(u):
                        n = keys(u)
                        act.wait_ge(S["negated"], u + 1)
                        if u >= 3:
                            act.wait_ge(S["turned"], u - 2)
                        nc.scalar.activation(prob[:, u % 3, 0:n], logit[:, u % 2, 0:n], ACT.Exp, bias=row(2, u),
                                             accum_out=row(3, u)).then_inc(S["exped"], 1)
                        h = core.vec(VEC["sinks"] + units[u][1] + 4 * units[u][2]) if u < NU else \
                            core.vec(VEC["sink_rows"] + u - NU)
                        nc.scalar.activation(row(4, u), h, ACT.Exp, bias=row(2, u)).then_inc(S["sink_exped"], 1)

                    def turned_copy(u):
                        n = keys(u)
                        act.wait_ge(S["turned"], u + 1)
                        if u >= 2:
                            act.wait_ge(S["out_done"], u - 1)
                        if n == P + TS:
                            nc.scalar.activation(pT[:, u % 2, 0], core.ps[:, 2 + u % 2, 0:P], ACT.Copy)
                            nc.scalar.activation(pT[0:TS, u % 2, 1], core.ps[0:TS, 2 + u % 2, P:2 * P], ACT.Copy
                                                 ).then_inc(S["turn_copied"], 1)
                        else:
                            nc.scalar.activation(pT[:, u % 2, 0:n // P], core.ps[:, 2 + u % 2, 0:n].rearrange(
                                "p (t c) -> p t c", c=P), ACT.Copy).then_inc(S["turn_copied"], 1)

                    def out_copy(u):
                        b, i, _ = units[u]
                        act.wait_ge(S["out_done"], u + 1)
                        nc.scalar.activation(o_sb[:, i, b * P:(b + 1) * P], core.ps[:, 4 + (u // 2) % 2, 0:P], ACT.Copy
                                             ).then_inc(S["out_copied"], 1)

                    for u in range(NU + 2 + 2):
                        if u < NU + 2:
                            exps(u)
                        if u >= 2:
                            turned_copy(u - 2)
                        if u >= 4 and u % 2 == 1:
                            out_copy(u - 4)
                    act.wait_ge(S["out_done"], NU + 2)
                    ov = core.ps[:, 4, 0:P].rearrange("p (b i t) -> p i b t", b=DEC_BATCH, i=4)
                    for i in range(4):
                        nc.scalar.activation(o_sb[:, i, SEQ:TOK].rearrange("p (b t) -> p b t", t=DEC_SEQ), ov[:, i], ACT.Copy
                                             ).then_inc(S["out_copied"], 1)
                    act.wait_ge(S["out_copied"], NU // 2 + 4)
                    for i in range(4):
                        nc.scalar.activation(core.h[0][:, 4 + i], o_sb[:, i], ACT.Copy).then_inc(S["high_ready"], 1)


def odd_mixer(nc, core, a, out, after_in, after_out):
    with ExitStack() as ctx:
        pr = ctx.enter_context(nc.sbuf_tensor("odd_proj", [P, ODD_TILES, TOK], F32))
        core.z = ctx.enter_context(nc.sbuf_tensor("odd_z", [P, 4, TOK], F32))
        glu = core.pairs_of(a["s5_w_glu"])
        projection(nc, core, "odd_in", core.pairs_of(a["odd_w_in"]), ODD_TILES // 2, KT, core.h, TOK, "copy", pr,
                   after=(glu, 4), norm=of_x(core, VEC["mix_norm"] + KT), scaled=True)
        s5(nc, core, pr, a, out)
        z_parts = [core.h[0][:, 4:8], core.h[1][:, 4:8]]
        projection(nc, core, "odd_glu", glu, 2, 4, z_parts, TOK, "copy", pr, after=after_in)
        s5_gate(nc, core, pr)
        window_attention(nc, core, pr, a, out)
    projection(nc, core, "odd_out", core.pairs_of(a["odd_w_out"]), KT // 2, KT, core.h, TOK, "add", core.x,
               after=after_out)


def build(nc, a, out):
    with ExitStack() as ctx:
        def sb(name, shape, dt=F32):
            return ctx.enter_context(nc.sbuf_tensor(name, shape, dt))

        core = Core()
        core.nc, core.section_sems = nc, []
        core.ps = ctx.enter_context(nc.psum_tensor("ps", [P, 8, 512], F32))
        core.x = sb("x", [P, KT, TOK])
        core.h = [sb("h_high", [P, KT, TOK], F32R), sb("h_low", [P, KT, TOK], F32R)]
        core.raw = [sb(f"w_raw{s}", [P, max(HT, KT) * P]) for s in range(2)]
        core.high = [sb(f"w_high{s}", [P, max(HT, KT) * P], F32R) for s in range(2)]
        core.low = [sb(f"w_low{s}", [P, max(HT, KT) * P], F32R) for s in range(2)]
        core.mats = sb("mats", [P, 5, P])
        core.vectors = sb("vectors", [P, NVEC])
        core.mask_chunk = sb("mask_chunk", [P, 2 * P], I32)
        core.mask_dec = sb("mask_dec", [TS, 4 * TS], I32)
        resets = sb("resets", [P, 2, TOK])
        core.reset, core.reset_s5 = resets[:, 0], resets[:, 1]
        core.resets = resets
        core.eps = sb("eps", [P, 1])
        core.rstd = sb("rstd", [P, TOK])
        core.landed = [ctx.enter_context(nc.semaphore(f"w_landed{s}")) for s in range(2)]
        core.loads = [0, 0]

        def vec(i):
            return core.vectors[:, i:i + 1]

        def vecs(name):
            i = VEC[name]
            n = {"sinks": 8}.get(name, S5_TILES)
            return core.vectors[:, i:i + n]

        def pairs_of(w):
            w = w.rearrange("(i s) p c -> s i p c", s=2)
            return [w[0], w[1]]

        def ffn_weights(which, layer, half):
            rows = slice(half * HT, (half + 1) * HT)
            up = [a[f"ffn{which}_w_{n}"][layer, rows] for n in ("gate", "up")]
            return up, pairs_of(a[f"ffn{which}_w_down"][layer, half])

        core.vec, core.vecs, core.pairs_of, core.ffn_weights = vec, vecs, pairs_of, ffn_weights
        core.first = (ffn_weights(1, 0, 0)[0], KT)
        load_constants(nc, core, a)
        for layer in range(2):
            even = layer == 0
            kind = "even" if even else "odd"
            ffn(nc, core, 1, layer, (pairs_of(a[f"{kind}_w_in"]), KT))
            mixer = even_mixer if even else odd_mixer
            core.end_section()
            mixer(nc, core, a, out, (pairs_of(a[f"{kind}_w_out"]), KT), (pairs_of(a["mem_w_k"][layer]), KT))
            core.end_section()
            memory_attention(nc, core, a, out, layer, (ffn_weights(2, layer, 0)[0], KT))
            core.end_section()
            ffn(nc, core, 2, layer, (ffn_weights(1, 1, 0)[0], KT) if even else None)
        with nc.semaphore("y_stored") as stored, nc.Block("store_y") as block:
            @block.sync
            def _(sp):
                sp.dma_start(out["y"], core.x[:]).then_inc(stored, 16)
                sp.wait_ge(stored, 16)


def _constants(np):
    f = np.float32
    mats = np.zeros((P, 5, P), f)
    at = np.arange(P)
    mats[:, IDENT] = np.eye(P, dtype=f)
    mats[:, ONES] = 1.0
    mats[:, ONES64] = (at[:, None] // 64 == at[None, :] // 64)
    for i in range(0, P, 2):
        mats[i + 1, SWAP2, i] = -1.0
        mats[i, SWAP2, i + 1] = 1.0
    for h in range(0, P, 64):
        for d in range(8):
            mats[h + d + 8, SWAP8, h + d] = -1.0
            mats[h + d, SWAP8, h + d + 8] = 1.0
    batch_rows = (at[:, None] // DEC_SEQ == np.arange(DEC_BATCH)[None, :]).astype(f)
    pos = np.concatenate([np.arange(SEQ), np.tile(PAST_LEN + np.arange(DEC_SEQ), DEC_BATCH)]).astype(f)
    step = np.concatenate([np.arange(SEQ) % CHUNK, np.tile(np.arange(DEC_SEQ), DEC_BATCH)])
    length = np.concatenate([np.full(SEQ, CHUNK), np.full(TS, DEC_SEQ)])
    s, t = at[:, None], at[None, :]
    chunk_mask = ((s // CHUNK == t // CHUNK) & (s <= t)).astype(np.int32)
    s, t = np.arange(TS)[:, None], np.arange(TS)[None, :]
    dec_mask = ((s // DEC_SEQ == t // DEC_SEQ) & (s <= t)).astype(np.int32)
    resets = np.ones((P, 2, TOK), f)
    resets[:, 0, step == 0] = 0.0
    resets[:, 1, SEQ::DEC_SEQ] = 0.0
    dk = 64
    log_decay = np.log(1.0 - 2.0 ** (-5.0 - np.arange(4, dtype=np.float64)))
    head = np.array([[2 * j + p // dk for j in range(2)] for p in range(P)])
    ld = log_decay[head][:, :, None]
    cum, end = ld * (step + 1), ld * length
    ret_decay = np.stack([np.exp(cum), np.exp(-cum), np.exp(end - cum)], 1).astype(f)
    chunks = np.array([CHUNK] * 8 + [DEC_SEQ] * 8)
    ret_last = np.exp(ld * chunks).astype(f).reshape(P, 32)
    inv = 1.0 / (10000.0 ** np.linspace(0.0, 1.0, dk // 2, dtype=f)).astype(f)
    ang = (pos[None, :] * inv[(at % dk) // 2][:, None]).astype(f).astype(np.float64)
    ret_rot = np.stack([np.cos(ang), np.sin(ang)], 1).astype(f)
    inv = (1.0 / (np.float64(500000.0) ** (np.arange(8) * 2.0 / 16))).astype(f)
    swa_rot = np.zeros((P, 2, TOK), f)
    swa_rot[:, 0] = 1.0
    for p in range(P):
        if p % 64 < 16:
            ang = (pos * inv[p % 8]).astype(f).astype(np.float64)
            swa_rot[p, 0], swa_rot[p, 1] = np.cos(ang), np.sin(ang)
    q, k = at[:, None], np.arange(-P, P)[None, :]
    swa_mask = np.where((k <= q) & (k > q - WIN), 0.0, NEG).astype(f)
    rb, rt = at // 16, at % DEC_SEQ
    old = np.where(at[None, :] > rt[:, None], 0.0, NEG)
    kb_, kt_ = np.arange(TS) // DEC_SEQ, np.arange(TS) % DEC_SEQ
    new = np.where((kb_[None, :] == rb[:, None]) & (kt_[None, :] <= rt[:, None]), 0.0, NEG)
    return dict(mats=mats, mask_chunk=np.tile(chunk_mask, (1, 2)), mask_dec=np.tile(dec_mask, (1, 4)), resets=resets,
                ret_decay=np.ascontiguousarray(ret_decay), ret_rot=ret_rot, swa_rot=swa_rot, swa_mask=swa_mask,
                swa_mask_s=np.concatenate([old, new], 1).astype(f), ret_last=ret_last, batch_rows=batch_rows,
                s5_steps=np.tile(np.concatenate([np.arange(CHUNK), CHUNK * np.arange(8)]).astype(f), (P, 1)))


def _chunks(w):
    k, m = w.shape
    return w.reshape(k // P, P, m // P, P).transpose(2, 1, 0, 3).reshape(m // P, P, k)


def _feature_major(x):
    t, d = x.shape
    return x.T.reshape(d // P, P, t).transpose(1, 0, 2)


def _layout(i, np):
    c = _constants(np)
    a = {n: c[n] for n in ("mats", "mask_chunk", "mask_dec", "resets", "ret_decay", "ret_rot", "swa_rot", "swa_mask",
                           "swa_mask_s", "s5_steps")}
    f = np.float32
    a["x"] = _feature_major(np.concatenate([i["x_prompt"].reshape(SEQ, D_MODEL), i["x_sample"].reshape(TS, D_MODEL)]))
    a["mem"] = _feature_major(i["mem_prompt"].reshape(N_MEM, D_MODEL))
    for n in ("1", "2"):
        for m in ("gate", "up"):
            a[f"ffn{n}_w_{m}"] = np.stack([_chunks(w) for w in i[f"ffn{n}_w_{m}"]])
        a[f"ffn{n}_w_down"] = np.stack([np.stack([_chunks(w[h * HT * P:(h + 1) * HT * P]) for h in range(2)])
                                        for w in i[f"ffn{n}_w_down"]])
    e = i["even_w_in"][0]
    rest = np.concatenate([e[:, 0:1536], e[:, 1552:3088], e[:, 1536:1552]], 1)
    wide = np.zeros((D_MODEL, EVEN_TILES * P), f)
    wide[:, 0:rest.shape[1]] = rest
    a["even_w_in"] = _chunks(wide)
    a["even_w_out"] = _chunks(i["even_w_out"][0])
    pair = np.concatenate([np.concatenate([np.arange(64) + 64 * h, np.arange(64) + 64 * (h + 4)]) for h in range(4)])
    o = i["odd_w_in"][0]
    a["odd_w_in"] = _chunks(np.concatenate([o[:, 0:512], o[:, 512:1024][:, pair], o[:, 1024:]], 1))
    o = i["odd_w_out"][0]
    a["odd_w_out"] = _chunks(np.concatenate([o[0:512], o[512:1024][pair]], 0))
    for n in "qkvo":
        a[f"mem_w_{n}"] = np.stack([_chunks(w) for w in i[f"mem_w_{n}"]])
    a["s5_w_glu"] = _chunks(i["s5_w_glu"][0])
    a["gla_w_gate"] = i["gla_w_gate"][0]

    def cols(w):
        return w.reshape(-1, P).T

    def tile_states(w):
        return w.reshape(S5_TILES, P).T
    v = np.zeros((P, NVEC), f)

    def put(name, w):
        v[:, VEC[name]:VEC[name] + w.shape[1]] = w
    for n in ("ffn1_norm", "ffn2_norm", "mix_norm", "mem_x_norm", "mem_m_norm", "mem_q_norm", "mem_k_norm"):
        put(n, cols(i[n]))
    put("gla_out_norm", cols(i["gla_out_norm"]))
    put("one", np.ones((P, 1), f))
    put("gla_b_gate", cols(i["gla_b_gate"]))
    put("swa_q_norm", np.tile(i["swa_q_norm"][0], 2)[:, None])
    put("swa_k_norm", np.tile(i["swa_k_norm"][0], 2)[:, None])
    put("s5_d", cols(i["s5_d"]))
    put("s5_b_glu", cols(i["s5_b_glu"]))
    put("sinks", np.tile(i["swa_sinks"][0], (P, 1)))
    put("sink_rows", np.stack([i["swa_sinks"][0][4 * kv + (np.arange(P) % 16) // 4] for kv in range(2)], 1))
    put("s5_a_re", tile_states(i["s5_a_re"][0]))
    put("s5_a_im", tile_states(i["s5_a_im"][0]))
    put("s5_log_step", tile_states(np.repeat(i["s5_log_step"][0], 64)))
    put("ret_last", c["ret_last"])
    put("batch_rows", c["batch_rows"])
    a["vectors"] = v
    b = np.zeros((2, 64, 2, S5_TILES, 2, 16), f)
    ct = np.zeros((2, 64, 2, S5_TILES, 4, 2, 16), f)
    for ri, part in enumerate(("re", "im")):
        bw = i[f"s5_b_{part}"][0].reshape(S5_TILES, 2, 64, 16)
        cw = i[f"s5_c_{part}"][0].reshape(S5_TILES, 2, 16, 64)
        for g in range(2):
            b[g, :, ri, :, g, :] = bw[:, g].transpose(1, 0, 2)
            for j in range(S5_TILES):
                ct[g, :, ri, j, j % 4, g, :] = cw[j, g].T
    a["s5_b"] = b.reshape(P, 2, S5_TILES, 32)
    a["s5_c"] = ct.reshape(P, 2, S5_TILES, P)
    a["state_s5"] = np.stack([i[f"state_s5_{p}"][0].reshape(DEC_BATCH, S5_TILES, P).transpose(2, 1, 0)
                              for p in ("re", "im")], 1)
    for n in ("gla", "ret"):
        s = i[f"state_{n}"][0].reshape(DEC_BATCH, 2, P, P)
        a[f"state_{n}"] = s.transpose(1, 2, 0, 3)
    a["cache_swa_k"] = i["cache_swa_k"][0].reshape(DEC_BATCH, WIN, P).transpose(2, 0, 1)
    a["cache_swa_v"] = i["cache_swa_v"][0].reshape(DEC_BATCH, WIN, P).transpose(1, 0, 2)
    a["cache_mem_k"] = i["cache_mem_k"].reshape(2, DEC_BATCH, N_MEM, KT, P).transpose(0, 1, 4, 3, 2)
    a["cache_mem_v"] = i["cache_mem_v"].reshape(2, DEC_BATCH, 2, P, KT, P).transpose(0, 1, 3, 2, 4, 5)
    return {n: np.ascontiguousarray(x) for n, x in a.items()}


_OUTS = dict(y=(P, KT, TOK), p_gla=(P, 2, P), p_ret=(P, 2, P), s_gla=(2, P, DEC_BATCH, P), s_ret=(2, P, DEC_BATCH, P),
             s5=(P, 2, S5_TILES, DEC_BATCH + 1), p_swa_k=(P, WIN), p_swa_v=(WIN, P), s_swa_k=(P, DEC_BATCH, WIN),
             s_swa_v=(WIN, DEC_BATCH, P), p_mem_k=(2, P, KT, N_MEM), p_mem_v=(2, P, 2, KT, P))


def kernel(**inputs):
    import numpy as np
    import concourse.bacc as bacc
    from concourse.bass_utils import run_bass_kernel_spmd

    arrays = _layout({n: np.asarray(x) for n, x in inputs.items()}, np)
    nc = bacc.Bacc("TRN2", target_bir_lowering=False, num_devices=1)
    a = {n: nc.dram_tensor(f"in_{n}", x.shape, mybir.dt.from_np(x.dtype), kind="ExternalInput").ap()
         for n, x in arrays.items()}
    out = {n: nc.dram_tensor(f"out_{n}", shape, F32, kind="ExternalOutput").ap() for n, shape in _OUTS.items()}
    build(nc, a, out)
    r = run_bass_kernel_spmd(nc, [{f"in_{n}": x for n, x in arrays.items()}], core_ids=[0]).results[0]
    r = {n: r[f"out_{n}"] for n in _OUTS}
    y = r["y"].transpose(2, 1, 0).reshape(TOK, D_MODEL)
    s5 = r["s5"].transpose(1, 3, 2, 0).reshape(2, DEC_BATCH + 1, 32, 64)

    def p_state(x):
        return x.reshape(2, 64, 2, P).transpose(2, 0, 1, 3).reshape(1, 1, 4, 64, P)

    def s_state(x):
        return x.reshape(2, 2, 64, DEC_BATCH, P).transpose(3, 0, 1, 2, 4).reshape(1, DEC_BATCH, 4, 64, P)
    return (y[:SEQ].reshape(1, SEQ, D_MODEL), y[SEQ:].reshape(DEC_BATCH, DEC_SEQ, D_MODEL),
            p_state(r["p_gla"]), p_state(r["p_ret"]), s5[0, 0:1][None], s5[1, 0:1][None],
            r["p_swa_k"].T.reshape(1, 1, WIN, 2, 64), r["p_swa_v"].reshape(1, 1, WIN, 2, 64),
            r["p_mem_k"].transpose(0, 3, 2, 1).reshape(2, 1, N_MEM, MEM_HEADS, MEM_HD),
            r["p_mem_v"].transpose(0, 2, 1, 3, 4).reshape(2, 1, N_MEM, MEM_HEADS, MEM_HD),
            s_state(r["s_gla"]), s_state(r["s_ret"]), s5[0, 1:][None], s5[1, 1:][None],
            r["s_swa_k"].transpose(1, 2, 0).reshape(1, DEC_BATCH, WIN, 2, 64),
            r["s_swa_v"].transpose(1, 0, 2).reshape(1, DEC_BATCH, WIN, 2, 64))
```
